# Optimizing a Trainium2 kernel written in Bass

```python
import math
import jax, jax.numpy as jnp
from jax import lax
import numpy as np

D_MODEL = 1024
BATCH = 1
SEQ = 256
DEPTH = 2

N_A = DEPTH // 2
N_B = DEPTH - N_A
CONV_W = 3
N_HEADS = 8
HEAD_DIM = D_MODEL // N_HEADS
BLOCK = 256
TOPK = 3
Q_CHUNK = 32
ROT_DIM = HEAD_DIM // 4
ROPE_THETA = 500000.0
MEM_LEN = 256
MEM_HEADS = 4
MEM_HEAD_DIM = D_MODEL // MEM_HEADS
D_FF = ((8 * D_MODEL + 3 * 256 - 1) // (3 * 256)) * 256
EPS = 1e-6


def rms_norm(x, g):
    x32 = x.astype(jnp.float32)
    y = x32 * lax.rsqrt(jnp.mean(x32 * x32, axis=-1, keepdims=True) + EPS)
    return (y * g.astype(jnp.float32)).astype(x.dtype)

def rope_cos_sin(positions):
    inv_freq = ROPE_THETA ** (-jnp.arange(0, ROT_DIM, 2, dtype=jnp.float32) / ROT_DIM)
    ang = positions.astype(jnp.float32)[..., None] * inv_freq
    return jnp.cos(ang)[:, :, None, :], jnp.sin(ang)[:, :, None, :]

def apply_partial_rope(x, cos, sin):
    xr = x[..., :ROT_DIM].astype(jnp.float32)
    x1, x2 = xr[..., : ROT_DIM // 2], xr[..., ROT_DIM // 2:]
    rot = jnp.concatenate([x1 * cos - x2 * sin, x2 * cos + x1 * sin], axis=-1)
    return jnp.concatenate([rot.astype(x.dtype), x[..., ROT_DIM:]], axis=-1)

def short_conv_mixer(h, w_in, w_conv, w_out):
    b_gate, c_gate, u = jnp.split(h @ w_in, 3, axis=-1)
    z = c_gate * u
    conv = lax.conv_general_dilated(
        z, w_conv[:, None, :].astype(z.dtype), window_strides=(1,),
        padding=[(CONV_W - 1, 0)], dimension_numbers=("NWC", "WIO", "NWC"),
        feature_group_count=D_MODEL)
    return (b_gate * conv) @ w_out

def mem_cross_attention(h, mem_n, w_q, w_kv, w_o):
    bsz, seq, _ = h.shape
    q = (h @ w_q).reshape(bsz, seq, MEM_HEADS, MEM_HEAD_DIM)
    k, v = jnp.split(mem_n @ w_kv, 2, axis=-1)
    k = k.reshape(bsz, -1, MEM_HEADS, MEM_HEAD_DIM)
    v = v.reshape(bsz, -1, MEM_HEADS, MEM_HEAD_DIM)
    s = jnp.einsum("bshd,bmhd->bhsm", q, k).astype(jnp.float32) * (MEM_HEAD_DIM ** -0.5)
    p = jax.nn.softmax(s, axis=-1).astype(v.dtype)
    o = jnp.einsum("bhsm,bmhd->bshd", p, v).reshape(bsz, seq, D_MODEL)
    return o @ w_o

def swiglu(h, w_gu, w_down):
    g, u = jnp.split(h @ w_gu, 2, axis=-1)
    return (jax.nn.silu(g) * u) @ w_down

def shared_kv(x, kv_norm, w_kv, cos, sin):
    bsz, seq, _ = x.shape
    n_blocks = -(-seq // BLOCK)
    pad = n_blocks * BLOCK - seq
    k, v = jnp.split(rms_norm(x, kv_norm) @ w_kv, 2, axis=-1)
    k = apply_partial_rope(k.reshape(bsz, seq, N_HEADS, HEAD_DIM), cos, sin)
    v = v.reshape(bsz, seq, N_HEADS, HEAD_DIM)
    k = jnp.pad(k, ((0, 0), (0, pad), (0, 0), (0, 0)))
    v = jnp.pad(v, ((0, 0), (0, pad), (0, 0), (0, 0)))
    k_blk = k.transpose(0, 2, 1, 3).reshape(bsz, N_HEADS, n_blocks, BLOCK, HEAD_DIM)
    v_blk = v.transpose(0, 2, 1, 3).reshape(bsz, N_HEADS, n_blocks, BLOCK, HEAD_DIM)
    k_mean = jnp.mean(k_blk.astype(jnp.float32), axis=3)
    return k_blk, v_blk, k_mean

def moba_attention(h, w_q, w_o, cos, sin, k_blk, v_blk, k_mean):
    bsz, seq, _ = h.shape
    n_blocks = k_blk.shape[2]
    k_sel = min(TOPK, n_blocks)
    n_chunks = seq // Q_CHUNK
    scale = HEAD_DIM ** -0.5
    q = apply_partial_rope((h @ w_q).reshape(bsz, seq, N_HEADS, HEAD_DIM), cos, sin)
    q_chunks = q.transpose(0, 2, 1, 3).reshape(bsz, N_HEADS, n_chunks, Q_CHUNK, HEAD_DIM)
    q_chunks = q_chunks.transpose(2, 0, 1, 3, 4)
    bi = jnp.arange(bsz)[:, None, None, None]
    hi = jnp.arange(N_HEADS)[None, :, None, None]

    def chunk_fn(args):
        c, q_c = args
        qpos = c * Q_CHUNK + jnp.arange(Q_CHUNK)
        qb = (c * Q_CHUNK) // BLOCK
        gate = jnp.einsum("bhqd,bhnd->bhqn", q_c.astype(jnp.float32), k_mean)
        past = jnp.arange(n_blocks) < qb
        gate = jnp.where(past[None, None, None, :], gate, -jnp.inf)
        _, idx = lax.top_k(gate, k_sel)
        valid = idx < qb
        kg = k_blk[bi, hi, idx]
        vg = v_blk[bi, hi, idx]
        s_sel = jnp.einsum("bhqd,bhqrkd->bhqrk", q_c, kg).astype(jnp.float32) * scale
        s_sel = jnp.where(valid[..., None], s_sel, -jnp.inf)
        s_sel = s_sel.reshape(bsz, N_HEADS, Q_CHUNK, k_sel * BLOCK)
        k_own = lax.dynamic_index_in_dim(k_blk, qb, axis=2, keepdims=False)
        v_own = lax.dynamic_index_in_dim(v_blk, qb, axis=2, keepdims=False)
        s_own = jnp.einsum("bhqd,bhkd->bhqk", q_c, k_own).astype(jnp.float32) * scale
        kpos = qb * BLOCK + jnp.arange(BLOCK)
        s_own = jnp.where((kpos[None, :] <= qpos[:, None])[None, None], s_own, -jnp.inf)
        p = jax.nn.softmax(jnp.concatenate([s_sel, s_own], axis=-1), axis=-1)
        p_sel = p[..., : k_sel * BLOCK].reshape(bsz, N_HEADS, Q_CHUNK, k_sel, BLOCK)
        p_own = p[..., k_sel * BLOCK:]
        o = jnp.einsum("bhqrk,bhqrkd->bhqd", p_sel.astype(vg.dtype), vg)
        o = o + jnp.einsum("bhqk,bhkd->bhqd", p_own.astype(v_own.dtype), v_own)
        return o

    out = lax.map(chunk_fn, (jnp.arange(n_chunks, dtype=jnp.int32), q_chunks))
    out = out.transpose(1, 0, 3, 2, 4).reshape(bsz, seq, D_MODEL)
    return out @ w_o

def first_inputs(seed: int = 0) -> dict:
    key = jax.random.key(seed)
    ks = jax.random.split(key, 24)
    f32 = jnp.float32

    def w(k, shape, fan_in):
        return jax.random.normal(k, shape, f32) * (fan_in ** -0.5)

    def gain(k, shape):
        return 1.0 + 0.02 * jax.random.normal(k, shape, f32)

    x = jax.random.normal(ks[0], (BATCH, SEQ, D_MODEL), f32)
    mem = jax.random.normal(ks[1], (BATCH, MEM_LEN, D_MODEL), f32)
    offset = jax.random.randint(ks[2], (BATCH, 1), 0, 8192, dtype=jnp.int32)
    positions = offset + jnp.arange(SEQ, dtype=jnp.int32)[None, :]
    return {
        "x": x,
        "mem": mem,
        "positions": positions,
        "norm_mix": gain(ks[3], (DEPTH, D_MODEL)),
        "norm_mem": gain(ks[4], (DEPTH, D_MODEL)),
        "norm_memkv": gain(ks[5], (DEPTH, D_MODEL)),
        "norm_ffn": gain(ks[6], (DEPTH, D_MODEL)),
        "norm_final": gain(ks[7], (D_MODEL,)),
        "conv_w_in": w(ks[8], (N_A, D_MODEL, 3 * D_MODEL), D_MODEL),
        "conv_w": w(ks[9], (N_A, CONV_W, D_MODEL), CONV_W),
        "conv_w_out": w(ks[10], (N_A, D_MODEL, D_MODEL), D_MODEL),
        "kv_norm": gain(ks[11], (D_MODEL,)),
        "w_kv": w(ks[12], (D_MODEL, 2 * D_MODEL), D_MODEL),
        "moba_w_q": w(ks[13], (N_B, D_MODEL, D_MODEL), D_MODEL),
        "moba_w_o": w(ks[14], (N_B, D_MODEL, D_MODEL), D_MODEL),
        "mem_w_q": w(ks[15], (DEPTH, D_MODEL, D_MODEL), D_MODEL),
        "mem_w_kv": w(ks[16], (DEPTH, D_MODEL, 2 * D_MODEL), D_MODEL),
        "mem_w_o": w(ks[17], (DEPTH, D_MODEL, D_MODEL), D_MODEL),
        "ffn_w_gu": w(ks[18], (DEPTH, D_MODEL, 2 * D_FF), D_MODEL),
        "ffn_w_down": w(ks[19], (DEPTH, D_FF, D_MODEL), D_FF),
    }

def first_block(x, mem, positions, norm_mix, norm_mem, norm_memkv, norm_ffn, norm_final,
              conv_w_in, conv_w, conv_w_out, kv_norm, w_kv, moba_w_q, moba_w_o,
              mem_w_q, mem_w_kv, mem_w_o, ffn_w_gu, ffn_w_down):
    cos, sin = rope_cos_sin(positions)
    k_blk = v_blk = k_mean = None
    for l in range(DEPTH):
        h = rms_norm(x, norm_mix[l])
        if l < N_A:
            x = x + short_conv_mixer(h, conv_w_in[l], conv_w[l], conv_w_out[l])
        else:
            j = l - N_A
            x = x + moba_attention(h, moba_w_q[j], moba_w_o[j], cos, sin, k_blk, v_blk, k_mean)
        x = x + mem_cross_attention(rms_norm(x, norm_mem[l]), rms_norm(mem, norm_memkv[l]),
                                    mem_w_q[l], mem_w_kv[l], mem_w_o[l])
        x = x + swiglu(rms_norm(x, norm_ffn[l]), ffn_w_gu[l], ffn_w_down[l])
        if l == N_A - 1:
            k_blk, v_blk, k_mean = shared_kv(x, kv_norm, w_kv, cos, sin)
    return rms_norm(x, norm_final)


DEPTH_2 = 1

DN_HEADS = 8
DN_HEAD_DIM = 128
DN_WIDTH = DN_HEADS * DN_HEAD_DIM
CONV_K = 5
CHUNK = 64
MLA_HEADS = 8
Q_LORA = 512
KV_LORA = 256
NOPE_DIM = 128
ROPE_DIM = 64
V_DIM = 128
QK_DIM = NOPE_DIM + ROPE_DIM
MLA_WIDTH = MLA_HEADS * V_DIM
ROPE_THETA_2 = 10000.0
Q_BLOCK = 128
N_EXPERTS = 16
CAPACITY_FACTOR = 2
D_EXPERT = 1024
N_BRANCHES = 2
N_MOD = 6

IN_SPLITS = (3 * DN_WIDTH,
             DN_WIDTH,
             2 * DN_HEADS,
             2 * DN_HEADS,
             Q_LORA,
             KV_LORA,
             ROPE_DIM,
             N_BRANCHES * D_MODEL)
N_IN = sum(IN_SPLITS)


def rms_norm_2(x, g):
    xf = x.astype(jnp.float32)
    y = xf * lax.rsqrt(jnp.mean(xf * xf, axis=-1, keepdims=True) + EPS)
    return (y * g.astype(jnp.float32)).astype(x.dtype)

def l2_norm(x):
    return x * lax.rsqrt(jnp.sum(x * x, axis=-1, keepdims=True) + EPS)

def apply_rope(x, cos, sin):
    x1, x2 = jnp.split(x.astype(jnp.float32), 2, axis=-1)
    return jnp.concatenate([x1 * cos - x2 * sin, x2 * cos + x1 * sin], axis=-1).astype(x.dtype)

def centred_depthwise_conv(x, w):
    ch = x.shape[-1]
    pad = (CONV_K - 1) // 2
    return lax.conv_general_dilated(x, w[:, None, :].astype(x.dtype), window_strides=(1,),
                                    padding=[(pad, pad)], dimension_numbers=('NWC', 'WIO', 'NWC'),
                                    feature_group_count=ch)

def chunk_gated_delta_rule(q, k, v, g, beta):
    b, h, s, dk = k.shape
    dv = v.shape[-1]
    nc = s // CHUNK
    q = q * (dk ** -0.5)
    qc = q.reshape(b, h, nc, CHUNK, dk)
    kc = k.reshape(b, h, nc, CHUNK, dk)
    vc = v.reshape(b, h, nc, CHUNK, dv)
    bc = beta.reshape(b, h, nc, CHUNK)
    gc = jnp.cumsum(g.reshape(b, h, nc, CHUNK), axis=-1)
    tril = jnp.tril(jnp.ones((CHUNK, CHUNK), dtype=bool))
    strict = jnp.tril(jnp.ones((CHUNK, CHUNK), dtype=bool), -1)
    diff = gc[..., :, None] - gc[..., None, :]
    decay = jnp.where(tril, jnp.exp(jnp.where(tril, diff, 0.0)), 0.0)
    k_beta = kc * bc[..., None]
    v_beta = vc * bc[..., None]
    lower = jnp.where(strict, jnp.einsum('bhnik,bhnjk->bhnij', k_beta, kc) * decay, 0.0)
    eye = jnp.eye(CHUNK, dtype=jnp.float32)
    t_inv = lax.linalg.triangular_solve(eye + lower, jnp.broadcast_to(eye, lower.shape),
                                        left_side=True, lower=True, unit_diagonal=True)
    u = t_inv @ v_beta
    w = t_inv @ (k_beta * jnp.exp(gc)[..., None])
    intra = jnp.where(tril, jnp.einsum('bhnik,bhnjk->bhnij', qc, kc) * decay, 0.0)
    q_dec = qc * jnp.exp(gc)[..., None]
    g_last = gc[..., -1]
    k_state = kc * jnp.exp(g_last[..., None] - gc)[..., None]

    def step(state, xs):
        w_i, u_i, intra_i, qd_i, ks_i, gl_i = xs
        v_new = u_i - w_i @ state
        o_i = qd_i @ state + intra_i @ v_new
        state = state * jnp.exp(gl_i)[..., None, None] + jnp.swapaxes(ks_i, -1, -2) @ v_new
        return state, o_i

    xs = tuple(jnp.moveaxis(t, 2, 0) for t in (w, u, intra, q_dec, k_state, g_last))
    state0 = jnp.zeros((b, h, dk, dv), jnp.float32)
    _, o = lax.scan(step, state0, xs)
    return jnp.moveaxis(o, 0, 2).reshape(b, h, s, dv)

def gated_deltanet_branch(qkv, z, b_in, a_in, conv_w, a_log, dt_bias, o_gain):
    bsz, s, _ = qkv.shape
    qkv = jax.nn.silu(centred_depthwise_conv(qkv, conv_w))
    q, k, v = jnp.split(qkv, 3, axis=-1)

    def heads(t):
        return t.reshape(bsz, s, DN_HEADS, DN_HEAD_DIM).transpose(0, 2, 1, 3).astype(jnp.float32)

    q, k, v = l2_norm(heads(q)), l2_norm(heads(k)), heads(v)
    beta = jax.nn.sigmoid(b_in.astype(jnp.float32)).reshape(bsz, s, 2, DN_HEADS).transpose(2, 0, 3, 1)
    a = a_in.astype(jnp.float32).reshape(bsz, s, 2, DN_HEADS)
    g = -jnp.exp(a_log.astype(jnp.float32)) * jax.nn.softplus(a + dt_bias.astype(jnp.float32))
    g = g.transpose(2, 0, 3, 1)
    o_fwd = chunk_gated_delta_rule(q, k, v, g[0], beta[0])
    flip = lambda t: jnp.flip(t, axis=2)
    o_bwd = flip(chunk_gated_delta_rule(flip(q), flip(k), flip(v), flip(g[1]), flip(beta[1])))
    o = (o_fwd + o_bwd).transpose(0, 2, 1, 3)
    zf = z.astype(jnp.float32).reshape(bsz, s, DN_HEADS, DN_HEAD_DIM)
    o = rms_norm_2(o, o_gain) * jax.nn.silu(zf)
    return o.reshape(bsz, s, DN_WIDTH).astype(qkv.dtype)

def mla_branch(c_q, c_kv, k_r, q_gain, w_uq, kv_gain, w_ukv, cos, sin):
    bsz, s, _ = c_q.shape
    q = (rms_norm_2(c_q, q_gain) @ w_uq).reshape(bsz, s, MLA_HEADS, QK_DIM)
    q = jnp.concatenate([q[..., :NOPE_DIM],
                         apply_rope(q[..., NOPE_DIM:], cos[:, :, None], sin[:, :, None])], axis=-1)
    kv = (rms_norm_2(c_kv, kv_gain) @ w_ukv).reshape(bsz, s, MLA_HEADS, NOPE_DIM + V_DIM)
    k_nope, v = kv[..., :NOPE_DIM], kv[..., NOPE_DIM:]
    k_rope = apply_rope(k_r, cos, sin)
    k = jnp.concatenate([k_nope, jnp.broadcast_to(k_rope[:, :, None], (bsz, s, MLA_HEADS, ROPE_DIM))], axis=-1)
    qb = (q * (QK_DIM ** -0.5)).reshape(bsz, s // Q_BLOCK, Q_BLOCK, MLA_HEADS, QK_DIM).transpose(1, 0, 2, 3, 4)

    def attend(q_blk):
        scores = jnp.einsum('bqhd,bkhd->bhqk', q_blk, k, preferred_element_type=jnp.float32)
        p = jax.nn.softmax(scores, axis=-1)
        return jnp.einsum('bhqk,bkhd->bqhd', p.astype(v.dtype), v)

    o = lax.map(attend, qb)
    return o.transpose(1, 0, 2, 3, 4).reshape(bsz, s, MLA_WIDTH)

def expert_choice_ffn(h, w_router, w_gate, w_up, w_down):
    bsz, s, d = h.shape
    cap = CAPACITY_FACTOR * s // N_EXPERTS
    aff = jax.nn.softmax((h @ w_router).astype(jnp.float32), axis=-1)
    gate, idx = lax.top_k(aff.transpose(0, 2, 1), cap)
    idx_flat = idx.reshape(bsz, N_EXPERTS * cap)
    xe = jnp.take_along_axis(h, idx_flat[..., None], axis=1).reshape(bsz, N_EXPERTS, cap, d)
    hid = jax.nn.silu(jnp.einsum('becd,edf->becf', xe, w_gate)) * jnp.einsum('becd,edf->becf', xe, w_up)
    ye = jnp.einsum('becf,efd->becd', hid, w_down) * gate[..., None].astype(h.dtype)
    out = jnp.zeros_like(h).at[jnp.arange(bsz)[:, None], idx_flat].add(ye.reshape(bsz, N_EXPERTS * cap, d))
    return out

def second_inputs(seed: int = 0) -> dict:
    key = jax.random.key(seed)
    ks = jax.random.split(key, 24)
    f32 = jnp.float32

    def nrm(k, shape, fan_in):
        return jax.random.normal(k, shape, f32) * (fan_in ** -0.5)

    def gain(k, shape):
        return 1.0 + 0.05 * jax.random.normal(k, shape, f32)

    x = jax.random.normal(ks[0], (BATCH, SEQ, D_MODEL), f32)
    c = jax.random.normal(ks[1], (BATCH, D_MODEL), f32)
    positions = (jnp.cumsum(jax.random.randint(ks[2], (BATCH, SEQ), 1, 3), axis=1) - 1).astype(jnp.int32)
    w_mod = 0.5 * nrm(ks[3], (DEPTH_2, D_MODEL, N_MOD * D_MODEL), D_MODEL)
    b_mod = 0.02 * jax.random.normal(ks[4], (DEPTH_2, N_MOD * D_MODEL), f32)
    g_mix = gain(ks[5], (DEPTH_2, D_MODEL))
    w_in = nrm(ks[6], (DEPTH_2, D_MODEL, N_IN), D_MODEL)
    conv_w = nrm(ks[7], (DEPTH_2, CONV_K, 3 * DN_WIDTH), CONV_K)
    a_log = jnp.log(jax.random.uniform(ks[8], (DEPTH_2, 2, DN_HEADS), f32, 1.0, 16.0))
    dt = jnp.exp(jax.random.uniform(ks[9], (DEPTH_2, 2, DN_HEADS), f32, math.log(1e-3), math.log(1e-1)))
    dt_bias = dt + jnp.log(-jnp.expm1(-dt))
    dn_o_gain = gain(ks[10], (DEPTH_2, DN_HEAD_DIM))
    q_gain = gain(ks[11], (DEPTH_2, Q_LORA))
    w_uq = nrm(ks[12], (DEPTH_2, Q_LORA, MLA_HEADS * QK_DIM), Q_LORA)
    kv_gain = gain(ks[13], (DEPTH_2, KV_LORA))
    w_ukv = nrm(ks[14], (DEPTH_2, KV_LORA, MLA_HEADS * (NOPE_DIM + V_DIM)), KV_LORA)
    w_o_dn = nrm(ks[15], (DEPTH_2, DN_WIDTH, D_MODEL), DN_WIDTH)
    w_o_mla = nrm(ks[16], (DEPTH_2, MLA_WIDTH, D_MODEL), MLA_WIDTH)
    w_out = nrm(ks[17], (DEPTH_2, D_MODEL, D_MODEL), D_MODEL)
    g_ffn = gain(ks[18], (DEPTH_2, D_MODEL))
    w_router = nrm(ks[19], (DEPTH_2, D_MODEL, N_EXPERTS), D_MODEL)
    w_gate = nrm(ks[20], (DEPTH_2, N_EXPERTS, D_MODEL, D_EXPERT), D_MODEL)
    w_up = nrm(ks[21], (DEPTH_2, N_EXPERTS, D_MODEL, D_EXPERT), D_MODEL)
    w_down = nrm(ks[22], (DEPTH_2, N_EXPERTS, D_EXPERT, D_MODEL), D_EXPERT)
    g_final = gain(ks[23], (D_MODEL,))
    return {'x': x, 'c': c, 'positions': positions, 'w_mod': w_mod, 'b_mod': b_mod, 'g_mix': g_mix,
            'w_in': w_in, 'conv_w': conv_w, 'a_log': a_log, 'dt_bias': dt_bias, 'dn_o_gain': dn_o_gain,
            'q_gain': q_gain, 'w_uq': w_uq, 'kv_gain': kv_gain, 'w_ukv': w_ukv, 'w_o_dn': w_o_dn,
            'w_o_mla': w_o_mla, 'w_out': w_out, 'g_ffn': g_ffn, 'w_router': w_router, 'w_gate': w_gate,
            'w_up': w_up, 'w_down': w_down, 'g_final': g_final}

def second_block(x, c, positions, w_mod, b_mod, g_mix, w_in, conv_w, a_log, dt_bias, dn_o_gain,
              q_gain, w_uq, kv_gain, w_ukv, w_o_dn, w_o_mla, w_out, g_ffn, w_router, w_gate,
              w_up, w_down, g_final):
    half = ROPE_DIM // 2
    inv_freq = ROPE_THETA_2 ** (-jnp.arange(half, dtype=jnp.float32) / half)
    ang = positions.astype(jnp.float32)[..., None] * inv_freq
    cos, sin = jnp.cos(ang), jnp.sin(ang)
    split_at = np.cumsum(IN_SPLITS)[:-1].tolist()
    for l in range(DEPTH_2):
        mod = jax.nn.silu(c) @ w_mod[l] + b_mod[l]
        sh1, sc1, gt1, sh2, sc2, gt2 = jnp.split(mod[:, None, :], N_MOD, axis=-1)
        h = rms_norm_2(x, g_mix[l]) * (1.0 + sc1) + sh1
        proj = h @ w_in[l]
        dn_qkv, dn_z, dn_b, dn_a, c_q, c_kv, k_r, gates = jnp.split(proj, split_at, axis=-1)
        y_dn = gated_deltanet_branch(dn_qkv, dn_z, dn_b, dn_a, conv_w[l], a_log[l], dt_bias[l],
                                     dn_o_gain[l]) @ w_o_dn[l]
        y_mla = mla_branch(c_q, c_kv, k_r, q_gain[l], w_uq[l], kv_gain[l], w_ukv[l], cos, sin) @ w_o_mla[l]
        g_dn, g_mla = jnp.split(jax.nn.sigmoid(gates), N_BRANCHES, axis=-1)
        merged = g_dn * y_dn + g_mla * y_mla
        x = x + gt1 * (merged @ w_out[l])
        h = rms_norm_2(x, g_ffn[l]) * (1.0 + sc2) + sh2
        x = x + gt2 * expert_choice_ffn(h, w_router[l], w_gate[l], w_up[l], w_down[l])
    return rms_norm_2(x, g_final)


def setup_inputs(seed=0):
    out = dict(first_inputs(seed))
    for name, value in second_inputs(seed + 1).items():
        if name != "x":
            out[name + "_2"] = value
    return out


def reference(
    x, mem, positions, norm_mix, norm_mem, norm_memkv, norm_ffn, norm_final, conv_w_in, conv_w,
    conv_w_out, kv_norm, w_kv, moba_w_q, moba_w_o, mem_w_q, mem_w_kv, mem_w_o, ffn_w_gu,
    ffn_w_down, c_2, positions_2, w_mod_2, b_mod_2, g_mix_2, w_in_2, conv_w_2, a_log_2,
    dt_bias_2, dn_o_gain_2, q_gain_2, w_uq_2, kv_gain_2, w_ukv_2, w_o_dn_2, w_o_mla_2, w_out_2,
    g_ffn_2, w_router_2, w_gate_2, w_up_2, w_down_2, g_final_2,
):
    x = first_block(
        x, mem, positions, norm_mix, norm_mem, norm_memkv, norm_ffn, norm_final, conv_w_in,
        conv_w, conv_w_out, kv_norm, w_kv, moba_w_q, moba_w_o, mem_w_q, mem_w_kv, mem_w_o,
        ffn_w_gu, ffn_w_down,
    )
    return second_block(
        x, c_2, positions_2, w_mod_2, b_mod_2, g_mix_2, w_in_2, conv_w_2, a_log_2, dt_bias_2,
        dn_o_gain_2, q_gain_2, w_uq_2, kv_gain_2, w_ukv_2, w_o_dn_2, w_o_mla_2, w_out_2,
        g_ffn_2, w_router_2, w_gate_2, w_up_2, w_down_2, g_final_2,
    )


_drawn_inputs = setup_inputs


def setup_inputs(seed=0):
    import zlib

    import numpy as np

    out = dict(_drawn_inputs(seed))
    spreads = {}
    factors = {'norm_mem': 8.0,
     'norm_memkv': 8.0,
     'norm_ffn': 3.278,
     'norm_final': 2.714,
     'kv_norm': 8.0,
     'b_mod_2': 4.165,
     'g_mix_2': 5.612,
     'a_log_2': 2.745,
     'dn_o_gain_2': 8.0,
     'q_gain_2': 8.0,
     'w_uq_2': 3.131,
     'kv_gain_2': 8.0,
     'g_ffn_2': 5.005}
    for name, (base, spread) in spreads.items():
        noise = np.random.default_rng([zlib.crc32(name.encode()), seed]).standard_normal(out[name].shape)
        drawn = base * np.exp(spread * noise) if base else spread * noise
        out[name] = __import__('jax').numpy.asarray(drawn.astype(out[name].dtype))
    for name, factor in factors.items():
        out[name] = (out[name] * factor).astype(out[name].dtype)
    return out
```

```python
import math

import concourse.bass as bass
import numpy as np
from concourse import mybir

ALU = mybir.AluOpType
ACT = mybir.ActivationFunctionType
F32 = mybir.dt.float32
F32R = mybir.dt.float32r
I32 = mybir.dt.int32
AX_X = mybir.AxisListType.X

P = 128
EPS = 1e-6
RING = 4
LANDED = 2 * 16
AHEAD = 2
CHUNK_W = 2048
BANK = 512

SEQ = 256
D = 1024
KT = D // P
TT = SEQ // P
D_FF = 2816
FT = D_FF // P
ROT = 32
THETA_1 = 500000.0
CONV1 = 3
CONV2 = 5
DN_H = 8
CH = 64
ROPE_2 = 64
THETA_2 = 10000.0
N_EXP = 16
CAP = 2 * SEQ // N_EXP

TWO_PI = 2.0 * math.pi
TP1 = 6.28125
TP2 = float(np.float32(TWO_PI - TP1))
TP3 = float(np.float32(TWO_PI - TP1 - TP2))
ROUND = 1.5 * 2.0**23


class Queue:

    def __init__(self, sem, chain):
        self.sem, self.n, self.ops = sem, 0, []
        self.chain, self.links = chain, 0

    def do(self, fn, *after):
        self.n += 1

        def run(e):
            for sem, value in after:
                e.wait_ge(sem, value)
            fn(e).then_inc(self.sem, 1)

        self.ops.append(run)
        return (self.sem, self.n)

    def raw(self, fn):
        self.ops.append(fn)


class Chain:

    def __init__(self, e, sem, base):
        self.e, self.sem, self.base, self.k = e, sem, base, 0

    def link(self, ins):
        self.k += 1
        ins.then_inc(self.sem, 1)
        self.e.wait_ge(self.sem, self.base + self.k)


def build(nc, A, out):
    sbuf_at = {}
    top = [0]

    def place(name, shape, dt, offset=None):
        size = 4 * int(np.prod(shape[1:]))
        if offset is None:
            offset = top[0]
            top[0] += (size + 31) // 32 * 32
        sbuf_at[name] = offset
        return nc.alloc_sbuf_tensor_at(name, list(shape), dt, offset=BASE + offset)

    BASE = (nc.sbuf_base + 63) // 64 * 64

    S = {n: nc.alloc_semaphore(n) for n in (
        "pe_done", "act_done", "dve_done", "pool_done", "sp_done",
        "pe_chain", "act_chain", "dve_chain", "pool_chain",
        "hi_ready", "lo_ready", "chunk_used", "act_evac", "dve_evac")}
    raw_in = [nc.alloc_semaphore(f"raw_in{s}") for s in range(RING)]
    n_load = [0]

    pe = Queue(S["pe_done"], S["pe_chain"])
    act = Queue(S["act_done"], S["act_chain"])
    dve = Queue(S["dve_done"], S["dve_chain"])
    pool = Queue(S["pool_done"], S["pool_chain"])
    sp = Queue(S["sp_done"], None)
    loads = Queue(None, None)

    bank = [nc.alloc_psum_tensor(f"bank{b}", [P, BANK], F32) for b in range(8)]
    G = bank[:4]
    X = bank[4:]

    raw = [place(f"w_raw{s}", [P, CHUNK_W], F32) for s in range(RING)]
    whi = [place(f"w_hi{s}", [P, CHUNK_W], F32R) for s in range(RING)]
    wlo = [place(f"w_lo{s}", [P, CHUNK_W], F32R) for s in range(RING)]
    x = place("x", [P, TT, D], F32)
    h_hi = place("h_hi", [P, KT, SEQ], F32R)
    h_lo = place("h_lo", [P, KT, SEQ], F32R)
    xn = place("xn", [P, TT, D], F32)
    ident = place("ident", [P, P], F32)
    ones = place("ones", [P, P], F32)
    vcol = place("vcol", [P, 256], F32)
    small = place("small", [P, 192], F32)
    neg_half = place("neg_half", [P, 8], F32)
    swap1 = place("swap1", [ROT, ROT], F32)
    swap2 = place("swap2", [ROPE_2, ROPE_2], F32)
    rope1 = place("rope1", [ROT, 2, SEQ], F32)
    rope2 = place("rope2", [ROPE_2, 2, SEQ], F32)
    a_hi = place("a_hi", [P, FT, SEQ], F32R)
    a_lo = place("a_lo", [P, FT, SEQ], F32R)
    invf = place("invf", [ROPE_2, 2], F32)
    F0 = top[0]

    class Stream:
        n = 0
        evac_a = 4
        evac_v = 4
        split = 0
    st = Stream()
    TOTAL = [None]

    def all_used():
        return (S["chunk_used"], RING + st.n)

    def act_evacs():
        return (S["act_evac"], st.evac_a)

    def dve_evacs():
        return (S["dve_evac"], st.evac_v)

    def finish():
        stored = nc.alloc_semaphore("stored")
        waits = [all_used(), dve_evacs(), act_evacs(), (S["dve_done"], dve.n), (S["pool_done"], pool.n)]

        def store(e):
            for w in waits:
                e.wait_ge(*w)
            e.dma_start(out[0].rearrange("(t p) d -> p t d", p=P), x[:, :, :]).then_inc(stored, 16)
            e.wait_ge(stored, 16)
        sp.raw(store)
        with nc.Block() as block:
            for engine, queue in ((block.tensor, pe), (block.scalar, act), (block.vector, dve),
                                  (block.gpsimd, pool), (block.sync, sp)):
                def run(e, queue=queue):
                    for op in queue.ops:
                        op(e)
                engine(run)

    def loop(e, n, body):
        full = n // RING
        if full >= 2:
            with e.Fori(0, full) as i:
                for u in range(RING):
                    body(i * RING + u, u)
        else:
            full = 0
        for c in range(full * RING, n):
            body(c, c % RING)

    def halves(parts):
        if len(parts) == 2:
            return parts
        (dst, src), = parts
        h = dst.shape[1] // 2
        return [(dst[:, 0:h, :], src[:, 0:h, :]), (dst[:, h:2 * h, :], src[:, h:2 * h, :])]

    def load_chunks(n, source, base):
        def run(e):
            def one(c, u):
                slot = (base + u) % RING
                m = base + c
                e.wait_ge(S["lo_ready"], m + 1)
                for dst, src in halves(source(c, raw[slot])):
                    e.dma_start(dst, src).then_inc(raw_in[slot], 16)
            loop(e, n, one)
        sp.raw(run)

    slot_incs = [[] for _ in range(RING)]

    def hi_split(e, m, slot):
        e.wait_ge(raw_in[slot], (m - slot) * (LANDED // RING) + LANDED)
        e.wait_ge(S["chunk_used"], m + 1)
        e.activation(whi[slot][:, :], raw[slot][:, :], ACT.Copy).then_inc(S["hi_ready"], 1)

    def lo_split(e, m, slot):
        e.wait_ge(S["hi_ready"], m + 1)
        e.wait_ge(S["chunk_used"], m + 1)
        e.tensor_tensor(wlo[slot][:, :], raw[slot][:, :], whi[slot][:, :].bitcast(F32),
                        ALU.subtract).then_inc(S["lo_ready"], 1)

    def first_splits():
        for m in range(AHEAD):
            act.raw(lambda e, m=m: hi_split(e, m, m % RING))
            dve.raw(lambda e, m=m: lo_split(e, m, m % RING))

    def gemm(n, source, pe_chunk, act_chunk=None, dve_chunk=None, ready=(), act_ready=(),
             dve_ready=(), last=False, act_links=0, dve_links=0, pe_free=None, evac_every=True):
        base = st.n
        ea, ev = st.evac_a, st.evac_v
        load_chunks(n, source, base)

        def run_pe(e):
            for sem, value in ready:
                e.wait_ge(sem, value)
            e.wait_ge(S["act_evac"], ea)
            e.wait_ge(S["dve_evac"], ev)

            def one(c, u):
                slot = (base + u) % RING
                e.wait_ge(S["hi_ready"], base + c + 1)
                e.wait_ge(S["lo_ready"], RING + base + c + 1)
                if evac_every:
                    if dve_chunk is not None:
                        e.wait_ge(S["dve_evac"], ev + c - 3)
                    else:
                        e.wait_ge(S["act_evac"], ea + c - 3)
                pe_chunk(e, c, u, slot).then_inc(S["chunk_used"], 1)
            loop(e, n, one)
        pe.raw(run_pe)

        def splits(e, c, u, split, mul):
            m = base + c + AHEAD
            assert not (last and n // RING >= 2)
            if last and isinstance(c, int) and c + AHEAD >= n:
                return
            split(e, m, (base + u + AHEAD) % RING)

        def runner(split, chunk, waits, sem, evbase, links, chain):
            def run(e):
                def one(c, u):
                    splits(e, c, u, split, 0)
                    if chunk is not None:
                        if isinstance(c, int) and c == 0:
                            for s_, v_ in waits:
                                e.wait_ge(s_, v_)
                        e.wait_ge(S["chunk_used"], RING + base + c + 1)
                        ch = Chain(e, chain[0], chain[1] + c * links)
                        chunk(e, c, u, ch).then_inc(sem, 1)
                        assert ch.k == links, (ch.k, links)
                if chunk is not None:
                    for s_, v_ in waits:
                        e.wait_ge(s_, v_)
                loop(e, n, one)
            return run
        act.raw(runner(hi_split, act_chunk, act_ready, S["act_evac"], ea, act_links,
                       (S["act_chain"], act.links)))
        dve.raw(runner(lo_split, dve_chunk, dve_ready, S["dve_evac"], ev, dve_links,
                       (S["dve_chain"], dve.links)))
        act.links += act_links * n
        dve.links += dve_links * n
        if act_chunk is not None:
            st.evac_a += n
        if dve_chunk is not None:
            st.evac_v += n
        st.n += n

    def cols(W, width=256, first=0):
        K = W.shape[0]
        v = W.rearrange("(k p) n -> p k n", p=P)
        k = K // P

        def source(c, slot):
            return [(slot[:, 0:k * width].rearrange("p (k n) -> p k n", k=k),
                     v[:, :, bass.ds(c * width + first, width)])]
        return source

    def chain_sources(*pairs):
        def source(c, slot):
            for n_, s_ in pairs:
                if c < n_:
                    return s_(c, slot)
                c -= n_
        return source

    def fm_chunk(bh, bl, width=256, kts=KT):
        def chunk(e, c, u, slot):
            for f in range(width // P):
                dst = G[u][:, f * SEQ:(f + 1) * SEQ]
                for k in range(kts):
                    lo, hi_ = k * width + f * P, k * width + (f + 1) * P
                    e.matmul(dst, whi[slot][:, lo:hi_], bh[:, k, :], start=(k == 0), stop=False)
                    e.matmul(dst, whi[slot][:, lo:hi_], bl[:, k, :], start=False, stop=False)
                    ins = e.matmul(dst, wlo[slot][:, lo:hi_], bh[:, k, :], start=False,
                                   stop=(k == kts - 1))
            return ins
        return chunk

    def tm_chunk(bh, bl, width=256, kts=KT):
        def chunk(e, c, u, slot):
            for t in range(TT):
                dst = G[u][:, t * width:(t + 1) * width]
                for k in range(kts):
                    xs = slice(t * P, (t + 1) * P)
                    w0, w1 = whi[slot][:, k * width:(k + 1) * width], wlo[slot][:, k * width:(k + 1) * width]
                    e.matmul(dst, bh[:, k, xs], w0, start=(k == 0), stop=False)
                    e.matmul(dst, bh[:, k, xs], w1, start=False, stop=False)
                    ins = e.matmul(dst, bl[:, k, xs], w0, start=False, stop=(k == kts - 1))
            return ins
        return chunk

    def copy_fm(dst):
        flat = dst.rearrange("p k t -> p (k t)")
        return lambda e, c, u, ch: e.activation(flat[:, bass.ds(c * BANK, BANK)], G[u][:, :], ACT.Copy)

    def copy_tm(dst, width=256):
        return lambda e, c, u, ch: e.activation(
            dst[:, :, bass.ds(c * width, width)],
            G[u][:, 0:TT * width].rearrange("p (t n) -> p t n", t=TT), ACT.Copy)

    def add_tm(dst, width=256):
        def chunk(e, c, u, ch):
            d = dst[:, :, bass.ds(c * width, width)]
            return e.tensor_tensor(d, d, G[u][:, :].rearrange("p (t n) -> p t n", t=TT), ALU.add)
        return chunk

    VROWS = [("norm_mix", 16), ("norm_mem", 16), ("norm_memkv", 16), ("norm_ffn", 16),
             ("kv_norm", 8), ("conv_w", 24), ("g_mix_2", 8), ("g_ffn_2", 8), ("q_gain_2", 4),
             ("kv_gain_2", 2), ("dn_o_gain_2", 1), ("c_2", 8)]
    vat, r = {}, 0
    for n_, k_ in VROWS:
        vat[n_] = r
        r += k_
    V1 = r
    vrow = place("vrow", [P, 2, P], F32, offset=sbuf_at["xn"])
    n_misc = 0

    def col(name, k=0):
        return vcol[:, vat[name] + k:vat[name] + k + 1]

    misc = nc.alloc_semaphore("vectors_in")
    x_in = nc.alloc_semaphore("x_in")
    pos_in = nc.alloc_semaphore("positions_in")

    pos_i = place("pos_i", [ROPE_2, 2, SEQ], I32, offset=F0)
    pos_f = place("pos_f", [ROPE_2, 2, SEQ], F32, offset=F0 + 2048)
    ang = place("ang", [ROPE_2, 4, SEQ], F32, offset=F0 + 4096)

    def load_x(e):
        e.dma_start(x[:, :, :], A["x"][0].rearrange("(t p) d -> p t d", p=P)).then_inc(x_in, 16)
    act.raw(load_x)

    def load_vectors(e):
        for n_, k_ in VROWS:
            src = A[n_]
            flat = src.rearrange(" ".join("abc"[:len(src.shape)]) + " -> (" + " ".join("abc"[:len(src.shape)]) + ")")
            e.dma_start(vrow[vat[n_]:vat[n_] + k_, 0, :], flat.rearrange("(k p) -> k p", p=P)).then_inc(misc, 16)
        w5 = A["conv_w_2"][0].rearrange("w (k p) -> (w k) p", p=P)
        e.dma_start(vrow[0:CONV2 * 24, 1, :], w5).then_inc(misc, 16)
        e.dma_start(invf[:, :], A["inv_freq"]).then_inc(pos_in, 16)
        for j, nm in enumerate(("positions", "positions_2")):
            e.dma_start(pos_i[:, j, :], A[nm].broadcast_to((ROPE_2, SEQ))).then_inc(pos_in, 16)
    act.raw(load_vectors)
    MISC = (misc, 16 * (len(VROWS) + 1))

    t_ones = pool.do(lambda e: e.memset(ones[:, :], 1.0))
    t_nh = pool.do(lambda e: e.memset(neg_half[:, :], -0.5))
    pool.do(lambda e: e.memset(ident[:, :], 0.0))
    pool.do(lambda e: e.memset(swap1[:, :], 0.0))
    t = pool.do(lambda e: e.memset(swap2[:, :], 0.0))
    t_id = pool.do(lambda e: e.affine_select(out=ident[:, :], in_=ident[:, :], compare_op=ALU.not_equal,
                                             fill=1.0, base=0, pattern=[[-1, P]], channel_multiplier=1), t)
    for sw, n_ in ((swap1, ROT), (swap2, ROPE_2)):
        t = pool.do(lambda e, sw=sw, n_=n_: e.affine_select(
            out=sw[:, :], in_=sw[:, :], compare_op=ALU.not_equal, fill=-1.0, base=-(n_ // 2),
            pattern=[[-1, n_]], channel_multiplier=1), t)
        t = pool.do(lambda e, sw=sw, n_=n_: e.affine_select(
            out=sw[:, :], in_=sw[:, :], compare_op=ALU.not_equal, fill=1.0, base=n_ // 2,
            pattern=[[-1, n_]], channel_multiplier=1), t)
    t_swap = t

    act.raw(lambda e: e.wait_ge(*t_nh))
    for n_ in range(4):
        act.raw(lambda e, n_=n_: e.activation(small[:, 160 + n_:161 + n_], neg_half[:, 0:1], ACT.Copy).then_inc(S["act_evac"], 1))
        act.raw(lambda e, n_=n_: e.activation(small[:, 164 + n_:165 + n_], neg_half[:, 0:1], ACT.Copy).then_inc(S["chunk_used"], 1))
        dve.raw(lambda e, n_=n_: e.memset(small[:, 168 + n_:169 + n_], 0.0).then_inc(S["dve_evac"], 1))
        dve.raw(lambda e, n_=n_: e.memset(small[:, 172 + n_:173 + n_], 0.0).then_inc(S["lo_ready"], 1))
    first_splits()

    pe.do(lambda e: e.transpose(X[0][:, 0:V1], vrow[0:V1, 0, :], ident[0:V1, 0:V1]), MISC, t_id)
    t = pe.do(lambda e: e.transpose(X[0][:, 128:128 + 120], vrow[0:120, 1, :], ident[0:120, 0:120]))
    dve.do(lambda e: e.tensor_copy(vcol[:, 0:V1], X[0][:, 0:V1]), t)
    t_vcol = dve.do(lambda e: e.tensor_copy(vcol[:, 128:248], X[0][:, 128:248]))
    xfree = {0: t_vcol, 1: None, 2: None, 3: None}

    def w5col(w, k):
        return vcol[:, 128 + w * 24 + k:129 + w * 24 + k]

    for j, (tab, n_) in enumerate(((rope1, ROT), (rope2, ROPE_2))):
        tp_ = dve.do(lambda e, j=j: e.tensor_copy(pos_f[:, j, :], pos_i[:, j, :]), (pos_in, 48))
        t = dve.do(lambda e, j=j: e.tensor_scalar(ang[:, 0, :], pos_f[:, j, :], invf[:, j:j + 1], None, ALU.mult), tp_, t)
        for q, shift in ((0, 0.25), (1, 0.0)):
            t = dve.do(lambda e, q=q, s_=shift: e.tensor_scalar(ang[:, 1, :], ang[:, 0, :], 1.0 / TWO_PI, s_, ALU.mult, ALU.add), t)
            t = dve.do(lambda e: e.tensor_scalar(ang[:, 2, :], ang[:, 1, :], ROUND, None, ALU.add), t)
            t = dve.do(lambda e: e.tensor_scalar(ang[:, 1, :], ang[:, 2, :], -ROUND, None, ALU.add), t)
            src = 0
            for part, (a_, b_) in zip((TP1, TP2, TP3), ((0, 2), (2, 3), (3, 2))):
                t = dve.do(lambda e, p_=part, a_=a_, b_=b_: e.scalar_tensor_tensor(
                    out=ang[:, b_, :], in0=ang[:, 1, :], scalar=-p_, in1=ang[:, a_, :],
                    op0=ALU.mult, op1=ALU.add), t)
            t = dve.do(lambda e, s_=shift: e.tensor_scalar(ang[:, 3, :], ang[:, 2, :], s_ * TWO_PI, 3.1415925, ALU.add, ALU.min), t)
            t = dve.do(lambda e: e.tensor_scalar(ang[:, 2, :], ang[:, 3, :], -3.1415925, None, ALU.max), t)
            t = act.do(lambda e, q=q, tab=tab, n_=n_: e.activation(tab[:, q, :], ang[0:n_, 2, :], ACT.Sin), t)
    t_rope = t

    slot_of = {"n": 0}

    def rstd_rows(src, ready, width, tag):
        s0 = (slot_of["n"] % 8) * 8
        slot_of["n"] += 1
        ss, rs = small[:, s0:s0 + 2], small[:, s0 + 2:s0 + 4]
        a_ = dve.do(lambda e: e.tensor_tensor_reduce(
            out=xn[:, 0, 0:width], in0=src[:, 0, :], in1=src[:, 0, :], scale=1.0, scalar=0.0,
            op0=ALU.mult, op1=ALU.add, accum_out=ss[:, 0:1]), *ready)
        b_ = act.do(lambda e: e.activation(xn[:, 1, 0:width], src[:, 1, :], ACT.Square,
                                           accum_out=ss[:, 1:2]), *ready)
        t = dve.do(lambda e: e.tensor_scalar(rs, ss, 1.0 / width, EPS, ALU.mult, ALU.add), a_, b_)
        t = pool.do(lambda e: e.tensor_tensor(ss, rs, neg_half[:, 0:2], ALU.pow), t, t_nh)
        return ss, t

    def norm_to_features(src, ready, gain, bias, free, dst=(h_hi, h_lo), xt=None):
        rs, t = rstd_rows(src, ready, D, "")
        t0 = dve.do(lambda e: e.tensor_scalar(xn[:, 0, :], src[:, 0, :], rs[:, 0:1], None, ALU.mult), t)
        t1 = act.do(lambda e: e.activation(xn[:, 1, :], src[:, 1, :], ACT.Copy, scale=rs[:, 1:2]), t)
        tls = {}
        for j in range(KT // 2):
            xt = ht_f[:, j % 2, :, :]
            war = [tls[j - 2]] if j >= 2 else []
            for kk in range(2):
                for t_ in range(TT):
                    k = 2 * j + kk
                    w = [t0, t1, t_id] + ([xfree[j]] if xfree[j] else [])
                    tp = pe.do(lambda e, j=j, kk=kk, k=k, t_=t_: e.transpose(
                        X[j][:, kk * SEQ + t_ * P:kk * SEQ + (t_ + 1) * P],
                        xn[:, t_, k * P:(k + 1) * P], ident[:, :]), *w)
            for kk in range(2):
                k = 2 * j + kk
                g_, b_ = gain(k), (bias(k) if bias else None)
                te = dve.do(lambda e, j=j, kk=kk, k=k, g_=g_, b_=b_, xt=xt: e.tensor_scalar(
                    xt[:, kk, :], X[j][:, kk * SEQ:(kk + 1) * SEQ], g_, b_, ALU.mult,
                    *((ALU.add,) if bias else ())), tp, t_vcol, *war)
            xfree[j] = te
            th = act.do(lambda e, j=j, xt=xt: e.activation(dst[0][:, 2 * j:2 * j + 2, :], xt, ACT.Copy),
                        te, *free)
            tl = dve.do(lambda e, j=j, xt=xt: e.tensor_tensor(
                dst[1][:, 2 * j:2 * j + 2, :], xt,
                dst[0][:, 2 * j:2 * j + 2, :].bitcast(F32), ALU.subtract), th)
            tls[j] = tl
        return tl

    def attention(heads, kts, scale, score, v, pbuf, ptbuf, ready, causal=None, free=(), dh=None):
        t_soft, t_pt, t_pv, t_fin = {}, {}, {}, {}
        sc0 = 64

        def scores(h):
            b = h % 2
            w = list(ready) + ([xfree[b]] if xfree[b] else []) + ([t_soft[h - 2]] if h >= 2 else [])
            tok = None
            for t_ in range(TT):
                tok = pe.do(lambda e, h=h, t_=t_, b=b: score(e, h, t_, X[b][:, t_ * SEQ:(t_ + 1) * SEQ]), *w)
                w = []
            return tok

        def softmax(h, ts):
            b = h % 2
            o = sc0 + b * 16
            mx, nb, den, rd = (small[:, o + 2 * q:o + 2 * q + 2] for q in range(4))
            s3 = X[b][:, :].rearrange("p (t m) -> p t m", t=TT)
            p3 = pbuf[b]
            wfree = [t_pt[h - 2]] if h >= 2 else []
            if causal is not None:
                tm = dve.do(lambda e: e.tensor_tensor(p3[:, :, :], s3, causal[:, :, :], ALU.add), ts, *wfree, *ready)
                src = p3[:, :, :]
                soft_free = tm
            else:
                tm = ts
                src = s3
            t = dve.do(lambda e: e.tensor_reduce(mx, src, AX_X, ALU.max), tm)
            t = dve.do(lambda e: e.tensor_scalar(nb, mx, -scale, None, ALU.mult), t)
            for t_ in range(TT):
                te = act.do(lambda e, t_=t_: e.activation(
                    p3[:, t_, :], src[:, t_, :], ACT.Exp, bias=nb[:, t_:t_ + 1], scale=scale,
                    accum_out=den[:, t_:t_ + 1]), t, *wfree)
            t_soft[h] = te
            t = dve.do(lambda e: e.reciprocal(rd, den), te)
            for t_ in range(TT):
                t2 = dve.do(lambda e, t_=t_: e.tensor_scalar(p3[:, t_, :], p3[:, t_, :], rd[:, t_:t_ + 1],
                                                             None, ALU.mult), t)
            return t2

        def turn(h, tp):
            b = h % 2
            w = [tp] + ([xfree[2]] if xfree[2] else []) + [t_id]
            for m in range(2):
                for t_ in range(TT):
                    tok = pe.do(lambda e, m=m, t_=t_, b=b: e.transpose(
                        X[2][:, m * SEQ + t_ * P:m * SEQ + (t_ + 1) * P],
                        pbuf[b][:, t_, m * P:(m + 1) * P], ident[:, :]), *w)
                    w = []
            t_pt[h] = tok
            w = [t_pv[h - 1]] if h >= 1 else []
            tc = act.do(lambda e: e.activation(ptbuf[:, :, :], X[2][:, :].rearrange("p (m q) -> p m q", m=2),
                                               ACT.Copy), tok, *w)
            xfree[2] = tc
            return tc

        def values(h, tc):
            w = [tc] + ([xfree[3]] if xfree[3] else [])
            for d in range(kts):
                for m in range(2):
                    f0 = (h * kts + d) * P
                    tok = pe.do(lambda e, d=d, m=m, f0=f0: e.matmul(
                        X[3][:, d * SEQ:(d + 1) * SEQ], v[:, m, f0:f0 + P], ptbuf[:, m, :],
                        start=(m == 0), stop=(m == 1)), *w)
                    w = []
            t_pv[h] = tok
            o3 = X[3][:, 0:kts * SEQ].rearrange("p (d q) -> p d q", d=kts)
            th = act.do(lambda e: e.activation(a_hi[:, h * kts:(h + 1) * kts, :], o3, ACT.Copy), tok, *free)
            tl = dve.do(lambda e: e.tensor_tensor(a_lo[:, h * kts:(h + 1) * kts, :], o3,
                                                  a_hi[:, h * kts:(h + 1) * kts, :].bitcast(F32),
                                                  ALU.subtract), th, *free)
            xfree[3] = tl
            return tl

        ts = scores(0)
        tp = softmax(0, ts)
        xfree_s = {}
        for h in range(heads):
            if h + 1 < heads:
                ts = scores(h + 1)
            tc = turn(h, tp)
            if h + 1 < heads:
                tp = softmax(h + 1, ts)
            tl = values(h, tc)
        xfree[0] = xfree[1] = t_soft[heads - 1]
        return tl

    xn_rope = place("xn_rope", [P, KT, SEQ], F32, offset=sbuf_at["xn"])
    qT = place("qT", [P, KT, SEQ], F32, offset=F0)
    kT = place("kT", [P, KT, SEQ], F32, offset=F0 + 8192)
    vv = place("vv", [P, TT, D], F32, offset=F0 + 16384)
    mem = place("mem", [P, TT, D], F32, offset=F0 + 24640)
    pb0 = place("pb0", [P, TT, SEQ], F32, offset=F0 + 32832)
    pb1 = place("pb1", [P, TT, SEQ], F32, offset=F0 + 34880)
    ptb = place("ptb", [P, 2, SEQ], F32, offset=F0 + 38976)
    ht_f = place("ht_f", [P, 2, 2, SEQ], F32, offset=F0 + 38976)
    bc_flat = place("bc_flat", [P, 2 * KT * SEQ], F32, offset=F0)
    bT = bc_flat[:, 0:KT * SEQ].rearrange("p (k t) -> p k t", k=KT)
    cT = bc_flat[:, KT * SEQ:2 * KT * SEQ].rearrange("p (k t) -> p k t", k=KT)
    PADZ = SEQ + CONV1 - 1
    zT = place("zT", [P, KT, PADZ], F32, offset=F0 + 16384)
    causal = place("causal", [P, TT, SEQ], F32, offset=F0 + 36928)
    silu_g = place("silu_g", [P, 2, SEQ], F32, offset=F0)
    prod_g = place("prod_g", [P, 2, SEQ], F32, offset=F0 + 2048)

    mem_in = nc.alloc_semaphore("mem_in")

    def load_mem(e):
        e.dma_start(mem[:, :, :], A["mem"][0].rearrange("(t p) d -> p t d", p=P)).then_inc(mem_in, 16)
    act.raw(load_mem)

    t = pool.do(lambda e: e.memset(causal[:, :, :], 0.0))
    for t_ in range(TT):
        t = pool.do(lambda e, t_=t_: e.affine_select(
            out=causal[:, t_, :], in_=causal[:, t_, :], compare_op=ALU.is_ge, fill=-1e30,
            base=t_ * P, pattern=[[-1, SEQ]], channel_multiplier=1), t)
    t_causal = t

    def flat(v):
        return v

    th = norm_to_features(x, [(x_in, 16)], lambda k: col("norm_mix", k), None, [])
    t_z0 = pool.do(lambda e: e.memset(zT[:, :, 0:CONV1 - 1], 0.0))

    W = A["conv_w_in"][0]
    gemm(8, cols(W), fm_chunk(h_hi, h_lo), act_chunk=lambda e, c, u, ch: e.activation(
        bc_flat[:, bass.ds(c * BANK, BANK)], G[u][:, :], ACT.Copy), ready=[th], act_ready=[t_rope])
    t_bc = act_evacs()

    def conv_chunk(e, c, u, ch):
        k0 = 2 * c
        z2 = zT[:, k0:k0 + 2, CONV1 - 1:PADZ]
        ch.link(e.tensor_tensor(z2, G[u][:, :].rearrange("p (k t) -> p k t", k=2), cT[:, k0:k0 + 2, :], ALU.mult))
        for k in (k0, k0 + 1):
            y = cT[:, k, :]
            for w in range(CONV1):
                wc = vcol[:, vat["conv_w"] + w * KT + k:vat["conv_w"] + w * KT + k + 1]
                if w == 0:
                    ch.link(e.tensor_scalar(y, zT[:, k, 0:SEQ], wc, None, ALU.mult))
                else:
                    ch.link(e.scalar_tensor_tensor(out=y, in0=zT[:, k, w:w + SEQ], scalar=wc, in1=y,
                                                   op0=ALU.mult, op1=ALU.add))
        y2 = cT[:, k0:k0 + 2, :]
        ch.link(e.tensor_tensor(y2, y2, bT[:, k0:k0 + 2, :], ALU.mult))
        ch.link(e.tensor_copy(a_hi[:, k0:k0 + 2, :], y2))
        return e.tensor_tensor(a_lo[:, k0:k0 + 2, :], y2, a_hi[:, k0:k0 + 2, :].bitcast(F32), ALU.subtract)

    gemm(4, cols(W, first=2 * D), fm_chunk(h_hi, h_lo), dve_chunk=conv_chunk, dve_links=9,
         dve_ready=[t_bc, t_z0])
    gemm(4, cols(A["conv_w_out"][0]), tm_chunk(a_hi, a_lo), dve_chunk=add_tm(x), ready=[dve_evacs()])

    def mem_attention(l, x_ready, last=False):
        tm_ = norm_to_features(mem, [(mem_in, 16), act_evacs(), dve_evacs()], lambda k: col("norm_memkv", 8 * l + k), None, [all_used()])
        W = A["mem_w_kv"][l]
        gemm(4, cols(W), fm_chunk(h_hi, h_lo), act_chunk=copy_fm(kT), ready=[tm_],
             act_ready=[x_ready])
        gemm(4, cols(W, first=D), tm_chunk(h_hi, h_lo), act_chunk=copy_tm(vv))
        tx = norm_to_features(x, [x_ready], lambda k: col("norm_mem", 8 * l + k), None, [all_used()])
        gemm(4, cols(A["mem_w_q"][l]), fm_chunk(h_hi, h_lo), act_chunk=copy_fm(qT), ready=[tx])

        def score(e, h, t_, dst):
            for k in (2 * h, 2 * h + 1):
                ins = e.matmul(dst, qT[:, k, t_ * P:(t_ + 1) * P], kT[:, k, :], start=(k == 2 * h), stop=(k == 2 * h + 1))
            return ins
        to = attention(4, 2, 256 ** -0.5, score, vv, (pb0, pb1), ptb, [act_evacs(), dve_evacs()], free=[all_used()])
        gemm(4, cols(A["mem_w_o"][l]), tm_chunk(a_hi, a_lo), dve_chunk=add_tm(x), ready=[to], last=last)

    def ffn(l, last=False):
        tx = norm_to_features(x, [dve_evacs()], lambda k: col("norm_ffn", 8 * l + k), None, [all_used()])
        W = A["ffn_w_gu"][l].rearrange("(k p) (h n) -> p k h n", p=P, h=2)

        def source(c, slot):
            dst = slot[:, :].rearrange("p (k h n) -> p k h n", k=KT, h=2)
            return [(dst[:, :, h, :], W[:, :, h, bass.ds(c * P, P)]) for h in range(2)]
        ta = act_evacs()

        def act_silu(e, c, u, ch):
            e.wait_ge(S["dve_evac"], ev0 + c - 1)
            return e.activation(silu_g[:, u % 2, :], G[u][:, 0:SEQ], ACT.Silu)
        ea0, ev0 = st.evac_a, st.evac_v

        def dve_gate(e, c, u, ch):
            e.wait_ge(S["act_evac"], ea0 + c + 1)
            pr = prod_g[:, u % 2, :]
            ch.link(e.tensor_tensor(pr, silu_g[:, u % 2, :], G[u][:, SEQ:2 * SEQ], ALU.mult))
            ch.link(e.tensor_copy(a_hi[:, bass.ds(c, 1), :], pr.rearrange("p (a t) -> p a t", a=1)))
            return e.tensor_tensor(a_lo[:, bass.ds(c, 1), :], pr.rearrange("p (a t) -> p a t", a=1),
                                   a_hi[:, bass.ds(c, 1), :].bitcast(F32), ALU.subtract)
        gemm(FT, source, fm_chunk(h_hi, h_lo), act_chunk=act_silu, dve_chunk=dve_gate, dve_links=2,
             ready=[tx], act_ready=[tx], dve_ready=[tx])
        Wd = A["ffn_w_down"][l].rearrange("(c k p) n -> p c k n", p=P, k=2)

        def down_source(c, slot):
            return [(slot[:, :].rearrange("p (k n) -> p k n", k=2), Wd[:, bass.ds(c, 1), :, :].rearrange("p a k n -> p (a k) n"))]

        n = FT // 2
        td = dve_evacs()
        down(n, down_source, last)
        for t_ in range(TT):
            for hf in range(2):
                b = 2 * t_ + hf
                xs = x[:, t_, hf * BANK:(hf + 1) * BANK]
                tok = dve.do(lambda e, b=b, xs=xs: e.tensor_tensor(xs, xs, G[b][:, :], ALU.add), all_used())
        return tok

    def down(n, source, last):
        def chunk(e, c, u, slot):
            for kk in range(2):
                k = 2 * c + kk
                for t_ in range(TT):
                    for hf in range(2):
                        dst = G[2 * t_ + hf][:, :]
                        w0 = whi[slot][:, kk * D + hf * BANK:kk * D + (hf + 1) * BANK]
                        w1 = wlo[slot][:, kk * D + hf * BANK:kk * D + (hf + 1) * BANK]
                        xh, xl = a_hi[:, k, t_ * P:(t_ + 1) * P], a_lo[:, k, t_ * P:(t_ + 1) * P]
                        e.matmul(dst, xh, w0, start=(k == 0), stop=False)
                        e.matmul(dst, xh, w1, start=False, stop=False)
                        ins = e.matmul(dst, xl, w0, start=False, stop=(k == 2 * n - 1))
            return ins
        base = st.n
        gemm_straight(n, source, chunk, last=last)

    def gemm_straight(n, source, chunk, ready=(), last=False):
        base = st.n
        ea, ev = st.evac_a, st.evac_v
        load_chunks(n, source, base)

        def run_pe(e):
            for sem, value in ready:
                e.wait_ge(sem, value)
            e.wait_ge(S["act_evac"], ea)
            e.wait_ge(S["dve_evac"], ev)
            for c in range(n):
                e.wait_ge(S["hi_ready"], base + c + 1)
                e.wait_ge(S["lo_ready"], RING + base + c + 1)
                chunk(e, c, c % RING, (base + c) % RING).then_inc(S["chunk_used"], 1)
        pe.raw(run_pe)

        def ahead(split):
            def run(e):
                loop(e, n - AHEAD * last, lambda c, u: split(e, base + c + AHEAD, (base + u + AHEAD) % RING))
            return run
        act.raw(ahead(hi_split))
        dve.raw(ahead(lo_split))
        st.n += n

    def rope_fm(buf, tiles, tab, swap, rows, ready, tmp):
        n = (tiles + 1) // 2
        f = buf[0:rows, :, :].rearrange("p k t -> p (k t)")
        tf = tmp[0:rows, :, :].rearrange("p k t -> p (k t)")
        for j in range(n):
            kk = min(2, tiles - 2 * j)
            w = list(ready) + ([xfree[j % 4]] if xfree[j % 4] else [])
            cs = slice(j * BANK, j * BANK + kk * SEQ)
            tp = pe.do(lambda e, j=j, cs=cs, kk=kk: e.matmul(X[j % 4][0:rows, 0:kk * SEQ], swap[:, :], f[:, cs],
                                                             start=True, stop=True), *w, t_swap)
            td = dve.do(lambda e, j=j, cs=cs, kk=kk: e.tensor_tensor(
                tf[:, cs].rearrange("p (k t) -> p k t", k=kk),
                X[j % 4][0:rows, 0:kk * SEQ].rearrange("p (k t) -> p k t", k=kk),
                tab[:, 1:2, :].broadcast_to((rows, kk, SEQ)), ALU.mult), tp, t_rope, *ready)
            xfree[j % 4] = td
        b3 = buf[0:rows, 0:tiles, :]
        t = dve.do(lambda e: e.tensor_tensor(b3, b3, tab[:, 0:1, :].broadcast_to((rows, tiles, SEQ)), ALU.mult), td, tp)
        return dve.do(lambda e: e.tensor_tensor(b3, b3, tmp[0:rows, 0:tiles, :], ALU.add), t)

    mem_attention(0, dve_evacs())
    tx = ffn(0)
    th = norm_to_features(x, [tx], lambda k: col("kv_norm", k), None, [all_used()])
    gemm(4, cols(A["w_kv"]), fm_chunk(h_hi, h_lo), act_chunk=copy_fm(kT), ready=[th])
    gemm(4, cols(A["w_kv"], first=D), tm_chunk(h_hi, h_lo), act_chunk=copy_tm(vv))
    th = norm_to_features(x, [tx], lambda k: col("norm_mix", 8 + k), None, [all_used()])
    gemm(4, cols(A["moba_w_q"][0]), fm_chunk(h_hi, h_lo), act_chunk=copy_fm(qT), ready=[th])
    t1 = rope_fm(kT, KT, rope1, swap1, ROT, [act_evacs()], xn_rope)
    t1 = rope_fm(qT, KT, rope1, swap1, ROT, [act_evacs(), t1], xn_rope)

    def score1(e, h, t_, dst):
        return e.matmul(dst, qT[:, h, t_ * P:(t_ + 1) * P], kT[:, h, :], start=True, stop=True)
    to = attention(8, 1, 128 ** -0.5, score1, vv, (pb0, pb1), ptb, [act_evacs(), t1, t_causal],
                   causal=causal, free=[all_used()])
    gemm(4, cols(A["moba_w_o"][0]), tm_chunk(a_hi, a_lo), dve_chunk=add_tm(x), ready=[to])
    mem_attention(1, dve_evacs())
    tx = ffn(1)

    A0 = sbuf_at["a_hi"]
    XN = sbuf_at["xn"]
    H_IN, DN_W = 4, DN_H * P
    C_Z, C_B, C_CQ, C_CKV, C_KR, C_G = 3072, 4096, 4128, 4640, 4896, 4960

    gt = place("gt", [P, 2, D], F32, offset=F0)
    mod = place("mod", [P, 6, D], F32, offset=F0 + 8192)
    gfin = place("gfin", [P, D], F32, offset=F0 + 36928)
    KEEP = F0 + 43072
    mcol = place("mcol", [P, 4, KT], F32, offset=KEEP)
    dtb = place("dtb", [P, 2, 16], F32, offset=KEEP + 128)

    mod_in, gfin_in = nc.alloc_semaphore("mod_in"), nc.alloc_semaphore("gfin_in")

    def load_late(e):
        for w in (tx, all_used_ffn1):
            e.wait_ge(*w)
        e.dma_start(mod[:, :, :].rearrange("p v d -> p (v d)"),
                    A["b_mod_2"].broadcast_to((P, 6 * D))).then_inc(mod_in, 16)
        e.dma_start(gfin[:, :], A["norm_final"].rearrange("(a d) -> a d", a=1).broadcast_to((P, D))).then_inc(gfin_in, 16)
        for j, nm in enumerate(("a_log_2", "dt_bias_2")):
            e.dma_start(dtb[:, j, :], A[nm].rearrange("a b c -> a (b c)").broadcast_to((P, 16))).then_inc(gfin_in, 16)
    all_used_ffn1 = all_used()
    act.raw(load_late)

    csil = place("csil", [P, KT], F32, offset=KEEP + 256)
    cb = place("cb", [P, KT, P], F32, offset=XN)
    t = act.do(lambda e: e.activation(csil[:, :], vcol[:, vat["c_2"]:vat["c_2"] + KT], ACT.Silu), t_vcol, tx)
    for k in range(KT):
        t2 = dve.do(lambda e, k=k: e.tensor_scalar(cb[:, k, :], ones[:, :], csil[:, k:k + 1], None, ALU.mult), t, t_ones, tx)
    t3 = act.do(lambda e: e.activation(h_hi[:, :, 0:P], cb[:, :, :], ACT.Copy), t2, all_used())
    t4 = dve.do(lambda e: e.tensor_tensor(h_lo[:, :, 0:P], cb[:, :, :], h_hi[:, :, 0:P].bitcast(F32), ALU.subtract), t3)

    def mod_chunk(e, c, u, slot):
        for k in range(KT):
            w0, w1 = whi[slot][:, k * 256:(k + 1) * 256], wlo[slot][:, k * 256:(k + 1) * 256]
            e.matmul(G[u][:, 0:256], h_hi[:, k, 0:P], w0, start=(k == 0), stop=False)
            e.matmul(G[u][:, 0:256], h_hi[:, k, 0:P], w1, start=False, stop=False)
            ins = e.matmul(G[u][:, 0:256], h_lo[:, k, 0:P], w0, start=False, stop=(k == KT - 1))
        return ins
    mflat = mod[:, :, :].rearrange("p v d -> p (v d)")

    rs, t = rstd_rows(x, [tx, t4], D, "")
    nfin = []
    for t_ in range(TT):
        nfin.append(dve.do(lambda e, t_=t_, rs=rs: e.scalar_tensor_tensor(
            out=x[:, t_, :], in0=x[:, t_, :], scalar=rs[:, t_:t_ + 1], in1=gfin[:, :],
            op0=ALU.mult, op1=ALU.mult), t, (gfin_in, 48)))
    t_x0 = nfin[-1]
    gemm(24, cols(A["w_mod_2"][0]), mod_chunk, ready=[t4], dve_ready=[(mod_in, 16)],
         dve_chunk=lambda e, c, u, ch: e.tensor_tensor(
             mflat[:, bass.ds(c * 256, 256)], mflat[:, bass.ds(c * 256, 256)], G[u][:, 0:256], ALU.add))
    t_mod = dve_evacs()
    dg = place("dg", [P, KT, P], F32, offset=XN + 4096)
    tcol = None
    for j, v_ in enumerate((0, 1, 3, 4)):
        t = dve.do(lambda e, v_=v_: e.tensor_tensor(
            dg[:, :, :], mod[:, v_, :].rearrange("p (k q) -> p k q", k=KT),
            ident[:, :].rearrange("p (a q) -> p a q", a=1).broadcast_to((P, KT, P)), ALU.mult),
            t_mod, t_id, *([tcol] if tcol else [t_x0]))
        tcol = dve.do(lambda e, j=j: e.tensor_reduce(mcol[:, j, :], dg[:, :, :], AX_X, ALU.add), t)
    for j, nm in ((1, "g_mix_2"), (3, "g_ffn_2")):
        tcol = dve.do(lambda e, j=j, nm=nm: e.scalar_tensor_tensor(
            out=mcol[:, j, :], in0=mcol[:, j, :], scalar=1.0, in1=vcol[:, vat[nm]:vat[nm] + KT],
            op0=ALU.add, op1=ALU.mult), tcol)
    tg = dve.do(lambda e: e.tensor_copy(gt[:, 0, :], mod[:, 2, :]), t_mod)
    tg = dve.do(lambda e: e.tensor_copy(gt[:, 1, :], mod[:, 5, :]), t_mod)

    th = norm_to_features(x, [t_x0, tcol, tg], lambda k: mcol[:, 1, k:k + 1], lambda k: mcol[:, 0, k:k + 1],
                          [all_used()])

    Win = A["w_in_2"][0]
    qn = place("qn", [P, 8, SEQ], F32, offset=F0 + 8192)
    kn = place("kn", [P, 8, SEQ], F32, offset=F0 + 16384)
    vm = place("vm", [P, TT, D], F32, offset=F0 + 24576)
    AU = 14 * SEQ * 4
    lat = place("lat", [P, 6, SEQ], F32, offset=A0 + AU)
    krr = place("krr", [ROPE_2, 1, SEQ], F32, offset=A0 + AU + 6144)
    qr = place("qr", [ROPE_2, 8, SEQ], F32, offset=sbuf_at["a_lo"] + AU)
    ab = place("ab", [P, TT, 32], F32, offset=KEEP + 288)

    gemm(3, cols(Win, first=C_CQ), fm_chunk(h_hi, h_lo), act_chunk=copy_fm(lat[:, :, :]), ready=[th], act_ready=[th])

    def kr_source(c, slot):
        v = Win.rearrange("(k p) n -> p k n", p=P)
        dst = slot[:, 0:KT * 96].rearrange("p (k n) -> p k n", k=KT)
        return [(dst[:, :, 0:64], v[:, :, C_KR:C_KR + 64]), (dst[:, :, 64:96], v[:, :, C_B:C_B + 32])]

    def kr_chunk(e, c, u, slot):
        for k in range(KT):
            w0, w1 = whi[slot][:, k * 96:k * 96 + 64], wlo[slot][:, k * 96:k * 96 + 64]
            e.matmul(G[u][0:64, 0:SEQ], w0, h_hi[:, k, :], start=(k == 0), stop=False)
            e.matmul(G[u][0:64, 0:SEQ], w0, h_lo[:, k, :], start=False, stop=False)
            e.matmul(G[u][0:64, 0:SEQ], w1, h_hi[:, k, :], start=False, stop=(k == KT - 1))
        for t_ in range(TT):
            for k in range(KT):
                w0, w1 = whi[slot][:, k * 96 + 64:k * 96 + 96], wlo[slot][:, k * 96 + 64:k * 96 + 96]
                xs = slice(t_ * P, (t_ + 1) * P)
                d_ = G[u][:, SEQ + t_ * 32:SEQ + t_ * 32 + 32]
                e.matmul(d_, h_hi[:, k, xs], w0, start=(k == 0), stop=False)
                e.matmul(d_, h_hi[:, k, xs], w1, start=False, stop=False)
                ins = e.matmul(d_, h_lo[:, k, xs], w0, start=False, stop=(k == KT - 1))
        return ins

    def kr_evac(e, c, u, ch):
        e.activation(krr[:, 0, :], G[u][0:64, 0:SEQ], ACT.Copy)
        return e.activation(ab[:, :, :], G[u][:, SEQ:SEQ + 64].rearrange("p (t n) -> p t n", t=TT), ACT.Copy)
    gemm(1, kr_source, kr_chunk, act_chunk=kr_evac)
    t_lat = act_evacs()

    sq = place("sq", [P, 6, SEQ], F32, offset=XN)
    rl = place("rl", [P, 2, SEQ], F32, offset=XN + 6144)
    t = act.do(lambda e: e.activation(sq[:, :, :], lat[:, :, :], ACT.Square), t_lat, th)
    for j, (k0, k1) in enumerate(((0, 4), (4, 6))):
        for k in range(k0, k1):
            tp = pe.do(lambda e, j=j, k=k, k0=k0, k1=k1: e.matmul(X[j][:, 0:SEQ], ones[:, :], sq[:, k, :],
                                                                  start=(k == k0), stop=(k == k1 - 1)), t, xfree[j])
        t2 = dve.do(lambda e, j=j, n_=(k1 - k0) * P: e.tensor_scalar(rl[:, j, :], X[j][:, 0:SEQ], 1.0 / n_, EPS, ALU.mult, ALU.add), tp, th)
        xfree[j] = t2
        t3 = act.do(lambda e, j=j: e.activation(rl[:, j, :], rl[:, j, :], ACT.Sqrt), t2)
        t3 = dve.do(lambda e, j=j: e.reciprocal(rl[:, j, :], rl[:, j, :]), t3)
        for k in range(k0, k1):
            g_ = col("q_gain_2", k) if j == 0 else col("kv_gain_2", k - 4)
            t4 = dve.do(lambda e, j=j, k=k, g_=g_: e.scalar_tensor_tensor(
                out=lat[:, k, :], in0=lat[:, k, :], scalar=g_, in1=rl[:, j, :], op0=ALU.mult, op1=ALU.mult), t3)
    t5 = act.do(lambda e: e.activation(a_hi[:, 8:14, :], lat[:, :, :], ACT.Copy), t4)
    t_l = dve.do(lambda e: e.tensor_tensor(a_lo[:, 8:14, :], lat[:, :, :], a_hi[:, 8:14, :].bitcast(F32), ALU.subtract), t5)

    def uq_chunk(e, c, u, slot):
        if c == 0:
            for b in range(4):
                e.wait_ge(*xfree_at[b])
        if c >= 2:
            e.wait_ge(S["act_evac"], ea_uq + c - 1)
        for hh in range(2):
            for (m, o, dst) in ((P, 0, G[u][:, hh * SEQ:(hh + 1) * SEQ]),
                                (64, P, X[c % 2][0:64, hh * SEQ:(hh + 1) * SEQ])):
                for k in range(4):
                    a_ = k * 384 + hh * 192 + o
                    w0, w1 = whi[slot][:, a_:a_ + m], wlo[slot][:, a_:a_ + m]
                    e.matmul(dst, w0, a_hi[:, 8 + k, :], start=(k == 0), stop=False)
                    e.matmul(dst, w0, a_lo[:, 8 + k, :], start=False, stop=False)
                    ins = e.matmul(dst, w1, a_hi[:, 8 + k, :], start=False, stop=(k == 3))
        return ins

    def uq_evac(e, c, u, ch):
        e.activation(qn[:, 2 * c:2 * c + 2, :], G[u][:, :].rearrange("p (h t) -> p h t", h=2), ACT.Copy)
        return e.activation(qr[:, 2 * c:2 * c + 2, :], X[c % 2][0:64, :].rearrange("p (h t) -> p h t", h=2), ACT.Copy)
    xfree_at = dict(xfree)
    ea_uq = st.evac_a
    gemm(4, cols(A["w_uq_2"][0], width=384), uq_chunk, act_chunk=uq_evac, ready=[t_l], act_ready=[t_l])

    def ukv_chunk(e, c, u, slot):
        e.wait_ge(S["act_evac"], ea_kv + max(0, c - 3))
        for hh in range(2):
            dst = G[u][:, hh * SEQ:(hh + 1) * SEQ]
            for k in range(2):
                a_ = k * BANK + hh * 256
                w0, w1 = whi[slot][:, a_:a_ + P], wlo[slot][:, a_:a_ + P]
                e.matmul(dst, w0, a_hi[:, 12 + k, :], start=(k == 0), stop=False)
                e.matmul(dst, w0, a_lo[:, 12 + k, :], start=False, stop=False)
                e.matmul(dst, w1, a_hi[:, 12 + k, :], start=False, stop=(k == 1))
        for t_ in range(TT):
            for hh in range(2):
                dst = X[u][:, t_ * 256 + hh * P:t_ * 256 + (hh + 1) * P]
                for k in range(2):
                    a_ = k * BANK + hh * 256 + P
                    w0, w1 = whi[slot][:, a_:a_ + P], wlo[slot][:, a_:a_ + P]
                    xs = slice(t_ * P, (t_ + 1) * P)
                    e.matmul(dst, a_hi[:, 12 + k, xs], w0, start=(k == 0), stop=False)
                    e.matmul(dst, a_hi[:, 12 + k, xs], w1, start=False, stop=False)
                    ins = e.matmul(dst, a_lo[:, 12 + k, xs], w0, start=False, stop=(k == 1))
        return ins

    def ukv_evac(e, c, u, ch):
        e.activation(kn[:, 2 * c:2 * c + 2, :], G[u][:, :].rearrange("p (h t) -> p h t", h=2), ACT.Copy)
        return e.activation(vm[:, :, c * 256:(c + 1) * 256], X[u][:, :].rearrange("p (t n) -> p t n", t=TT), ACT.Copy)
    ea_kv = st.evac_a
    gemm(4, cols(A["w_ukv_2"][0], width=512), ukv_chunk, act_chunk=ukv_evac)
    for b in range(4):
        xfree[b] = act_evacs()
    t1 = rope_fm(qr, 8, rope2, swap2, ROPE_2, [act_evacs()], xn_rope)
    t1 = rope_fm(krr, 1, rope2, swap2, ROPE_2, [act_evacs(), t1], xn_rope)

    def score2(e, h, t_, dst):
        e.matmul(dst, qn[:, h, t_ * P:(t_ + 1) * P], kn[:, h, :], start=True, stop=False)
        return e.matmul(dst, qr[:, h, t_ * P:(t_ + 1) * P], krr[:, 0, :], start=False, stop=True)
    to = attention(8, 1, 192 ** -0.5, score2, vm, (pb0, pb1), ptb, [act_evacs(), t1], free=[all_used()])

    merged = place("merged", [P, TT, D], F32, offset=F0 + 8192)
    gat = place("gat", [P, TT, D], F32, offset=F0 + 16384)

    def sig_tm(dst, func):
        return lambda e, c, u, ch: e.activation(
            dst[:, :, bass.ds(c * 256, 256)], G[u][:, :].rearrange("p (t n) -> p t n", t=TT), func)
    gemm(4, cols(Win, first=C_G + D), tm_chunk(h_hi, h_lo), act_chunk=sig_tm(gat, ACT.Sigmoid), act_ready=[to], ready=[])
    t_gat = act_evacs()

    def gated(e, c, u, ch):
        cs = slice(c * 256, (c + 1) * 256)
        return e.tensor_tensor(merged[:, :, cs], G[u][:, :].rearrange("p (t n) -> p t n", t=TT),
                               gat[:, :, cs], ALU.mult)
    gemm(4, cols(A["w_o_mla_2"][0]), tm_chunk(a_hi, a_lo), dve_chunk=gated, ready=[to], dve_ready=[t_gat, to])
    t_mla = [all_used(), dve_evacs(), act_evacs()]

    NS = 8
    o_all = place("o_all", [P, TT, 8, P], F32, offset=F0 + 16384)
    kf = place("kf", [P, 4, SEQ], F32, offset=F0 + 24576)
    qf = place("qf", [P, 4, SEQ], F32, offset=F0 + 28672)
    vf = place("vf", [P, 4, SEQ], F32, offset=F0 + 32768)
    otmp = place("otmp", [P, 2, 4, P], F32, offset=F0 + 32768)
    kt_ = place("kt_", [P, TT, 4, P], F32, offset=F0 + 36864)
    vt_ = place("vt_", [P, TT, 4, P], F32, offset=XN)
    bsc = place("bsc", [P, TT, NS, CH], F32, offset=XN + 4096)
    sq2 = place("sq2", [P, 8, SEQ], F32, offset=XN)
    Tm = place("Tm", [P, TT, NS, CH], F32, offset=A0)
    TT_ = place("TT_", [P, TT, NS, CH], F32, offset=A0 + 4096)
    LT = place("LT", [P, TT, NS, CH], F32, offset=A0 + 8192)
    IT = place("IT", [P, TT, NS, CH], F32, offset=A0 + 12288)
    Ym = place("Ym", [P, TT, NS, CH], F32, offset=A0 + 16384)
    AT = place("AT", [P, TT, NS, CH], F32, offset=A0 + 20480)
    DR = place("DR", [P, TT, NS, CH], F32, offset=A0 + 24576)
    pad = place("pad", [P, 2, 2, SEQ + 4], F32, offset=A0 + 16384)
    cy = place("cy", [P, 2, 2, SEQ], F32, offset=A0 + 24576)
    Sst = place("Sst", [P, NS, P], F32, offset=A0 + 24576)
    rr = place("rr", [P, 2, 4, P], F32, offset=A0 + 16384)
    vn = place("vn", [P, 2, 4, P], F32, offset=A0 + 20480)
    ks = place("ks", [P, TT, NS, P], F32, offset=A0 + 28672)
    vb = place("vb", [P, TT, NS, P], F32, offset=A0 + 36864)
    blk = place("blk", [P, P], F32, offset=KEEP + 1056)
    tri = place("tri", [P, 2, P], F32, offset=sbuf_at["rope1"])
    hal = place("hal", [P, 2, P], F32, offset=F0 + 40960)
    id64 = place("id64", [P, CH], F32, offset=KEEP + 800)
    msk = place("msk", [P, 3, 2, CH], F32, offset=sbuf_at["rope1"] + 1024)
    lev = place("lev", [P, 6, CH], F32, offset=sbuf_at["rope1"] + 2560)
    gb = place("gb", [P, 8, TT, 16], F32, offset=F0 + 41984)
    glb = place("glb", [P, 2, 32], F32, offset=KEEP + 544)

    def half(buf, b):
        return buf[64 * b:64 * b + 64]
    t = pool.do(lambda e: e.memset(blk[:, :], 0.0), *t_mla)
    pool.do(lambda e: e.memset(tri[:, :, :], 0.0))
    pool.do(lambda e: e.memset(hal[:, :, :], 0.0))
    pool.do(lambda e: e.memset(id64[:, :], 0.0))
    pool.do(lambda e: e.memset(msk[:, :, :, :], 1.0))
    t = pool.do(lambda e: e.memset(lev[:, :, :], 1.0))
    for b in range(2):
        cs = slice(64 * b, 64 * b + 64)
        pool.do(lambda e, b=b, cs=cs: e.memset(blk[cs, cs], 1.0), t)
        pool.do(lambda e, b=b, cs=cs: e.memset(hal[cs, b, :], 1.0), t)
        t2 = pool.do(lambda e, b=b, cs=cs: e.memset(tri[cs, :, cs], 1.0), t)
        pool.do(lambda e, cs=cs: e.affine_select(out=id64[cs, :], in_=id64[cs, :], compare_op=ALU.not_equal,
                                                 fill=1.0, base=0, pattern=[[-1, CH]], channel_multiplier=1), t2)
        pool.do(lambda e, cs=cs: e.affine_select(out=tri[cs, 0, cs], in_=tri[cs, 0, cs], compare_op=ALU.is_ge,
                                                 fill=0.0, base=0, pattern=[[1, CH]], channel_multiplier=-1), t2)
        pool.do(lambda e, cs=cs: e.affine_select(out=tri[cs, 1, cs], in_=tri[cs, 1, cs], compare_op=ALU.is_ge,
                                                 fill=0.0, base=0, pattern=[[-1, CH]], channel_multiplier=1), t2)
        for m_, d_, sgn, op in ((0, 0, -1, ALU.is_gt), (0, 1, 1, ALU.is_gt), (1, 0, 1, ALU.is_ge),
                                (1, 1, -1, ALU.is_ge), (2, 0, 1, ALU.is_gt), (2, 1, -1, ALU.is_gt)):
            pool.do(lambda e, cs=cs, m_=m_, d_=d_, sgn=sgn, op=op: e.affine_select(
                out=msk[cs, m_, d_, :], in_=msk[cs, m_, d_, :], compare_op=op, fill=0.0, base=0,
                pattern=[[sgn, CH]], channel_multiplier=-sgn), t2)
        for l in range(6):
            sz = 2 ** (l + 1)
            v_ = lev[cs, l, :].rearrange("p (n s) -> p n s", s=sz)
            t3 = pool.do(lambda e, v_=v_, sz=sz: e.affine_select(
                out=v_, in_=v_, compare_op=ALU.is_ge, fill=0.0, base=0,
                pattern=[[-sz, CH // sz], [0, sz]], channel_multiplier=1), t2)
            t3 = pool.do(lambda e, v_=v_, sz=sz: e.affine_select(
                out=v_, in_=v_, compare_op=ALU.is_ge, fill=0.0, base=sz - 1,
                pattern=[[sz, CH // sz], [0, sz]], channel_multiplier=-1), t3)
    for l in range(5, -1, -1):
        lower = lev[:, l - 1, :] if l else id64[:, :]
        t3 = pool.do(lambda e, l=l, lower=lower: e.tensor_tensor(lev[:, l, :], lev[:, l, :], lower, ALU.subtract), t3)
    t_masks = t3

    beta, gg, gc, eg, be, ek, s1, s2 = (gb[:, j, :, :] for j in range(8))
    t = act.do(lambda e: e.activation(beta, ab[:, :, 0:16], ACT.Sigmoid), act_evacs(), t_lat)
    t_beta = t
    t = dve.do(lambda e: e.tensor_tensor(s1, ab[:, :, 16:32], dtb[:, 1:2, :].broadcast_to((P, TT, 16)), ALU.add), t_lat, (gfin_in, 48))
    t1 = dve.do(lambda e: e.tensor_scalar(s2, s1, -1.0, None, ALU.mult), t)
    t1 = dve.do(lambda e: e.tensor_tensor(s2, s2, s1, ALU.min), t1)
    t1 = act.do(lambda e: e.activation(s2, s2, ACT.Exp), t1)
    t2 = act.do(lambda e: e.activation(dtb[:, 0, :], dtb[:, 0, :], ACT.Exp), (gfin_in, 48))
    t1 = act.do(lambda e: e.activation(s2, s2, ACT.Ln, bias=1.0), t1)
    t1 = dve.do(lambda e: e.scalar_tensor_tensor(out=s1, in0=s1, scalar=0.0, in1=s2, op0=ALU.max, op1=ALU.add), t1, t)
    t1 = dve.do(lambda e: e.scalar_tensor_tensor(out=gg, in0=s1, scalar=-1.0, in1=dtb[:, 0:1, :].broadcast_to((P, TT, 16)),
                                                 op0=ALU.mult, op1=ALU.mult), t1, t2)
    for t_ in range(TT):
        for d_ in range(2):
            tp = pe.do(lambda e, t_=t_, d_=d_: e.matmul(X[0][:, t_ * 16 + d_ * 8:t_ * 16 + d_ * 8 + 8], tri[:, d_, :],
                                                        gg[:, t_, d_ * 8:d_ * 8 + 8], start=True, stop=True), t1, t_masks, xfree[0])
    ggf = gb[:, 1, :, :].rearrange("p t s -> p (t s)")
    pe.do(lambda e: e.matmul(X[0][:, 32:64], blk[:, :], ggf, start=True, stop=True))
    for b in range(2):
        tp = pe.do(lambda e, b=b: e.matmul(X[0][:, 64 + 32 * b:96 + 32 * b], hal[:, b, :], ggf, start=True, stop=True))
    v3 = lambda a_: a_.rearrange("p (t s) -> p t s", t=TT)
    t1 = dve.do(lambda e: e.tensor_copy(gc, v3(X[0][:, 0:32])), tp)
    t2 = dve.do(lambda e: e.tensor_tensor(s1, v3(X[0][:, 32:64]), gc, ALU.subtract), t1)
    t3 = act.do(lambda e: e.activation(glb[:, :, :], X[0][:, 64:128].rearrange("p (b s) -> p b s", b=2), ACT.Exp), tp, t2)
    xfree[0] = t3
    t1 = act.do(lambda e: e.activation(eg, gc, ACT.Exp), t1)
    t2 = act.do(lambda e: e.activation(ek, s1, ACT.Exp), t2)
    t_gates = dve.do(lambda e: e.tensor_tensor(be, beta, eg, ALU.mult), t1, t_beta, t2)

    def streams(v_, h0):
        return v_.rearrange("p t (d h) -> p t d h", d=2)[:, :, :, h0:h0 + 4]

    o_done = None
    group_free = t_mla
    for grp in range(2):
        h0 = grp * 4
        def conv_source(c, slot, h0=h0):
            v = Win.rearrange("(k p) n -> p k n", p=P)
            c0 = (c // 2) * D + h0 * P + (c % 2) * 256
            return [(slot[:, :].rearrange("p (k n) -> p k n", k=KT), v[:, :, c0:c0 + 256])]
        fin = (qf, kf, vf)
        ea0, ev0 = st.evac_a, st.evac_v

        def silu_of(e, c, fin=fin, ev0=ev0):
            e.wait_ge(S["dve_evac"], ev0 + c + 1)
            return e.activation(fin[c // 2][:, (c % 2) * 2:(c % 2) * 2 + 2, :], cy[:, c % 2, :, :], ACT.Silu)

        def act_pad(e, c, u, ch, silu_of=silu_of, ev0=ev0):
            if c >= 1:
                silu_of(e, c - 1)
            e.wait_ge(S["dve_evac"], ev0 + max(0, c - 1))
            return e.activation(pad[:, c % 2, :, 2:2 + SEQ], G[u][:, :].rearrange("p (k t) -> p k t", k=2), ACT.Copy)

        def dve_conv(e, c, u, ch, h0=h0, ea0=ea0):
            e.wait_ge(S["act_evac"], ea0 + c + 1)
            for f in range(2):
                k = (c // 2) * 8 + h0 + (c % 2) * 2 + f
                y = cy[:, c % 2, f, :]
                for w in range(CONV2):
                    src = pad[:, c % 2, f, w:w + SEQ]
                    ins = (e.tensor_scalar(y, src, w5col(w, k), None, ALU.mult) if w == 0 else
                           e.scalar_tensor_tensor(out=y, in0=src, scalar=w5col(w, k), in1=y, op0=ALU.mult, op1=ALU.add))
                    if (f, w) != (1, CONV2 - 1):
                        ch.link(ins)
            return ins
        tz = None
        for b in range(2):
            for o_ in (0, SEQ + 2):
                tz = dve.do(lambda e, b=b, o_=o_: e.memset(pad[:, b, :, o_:o_ + 2], 0.0), *group_free)
        gemm(6, conv_source, fm_chunk(h_hi, h_lo), act_chunk=act_pad, dve_chunk=dve_conv, dve_links=9,
             ready=group_free, act_ready=group_free + [tz], dve_ready=[tz])
        t_conv = act.do(lambda e, silu_of=silu_of: silu_of(e, 5))
        for j in range(4):
            src = (qf, kf)[j // 2][:, (j % 2) * 2:(j % 2) * 2 + 2, :]
            ts_ = act.do(lambda e, j=j, src=src: e.activation(sq2[:, 2 * j:2 * j + 2, :], src, ACT.Square), t_conv, *group_free)
            tp = pe.do(lambda e, j=j: e.matmul(X[j][:, :], ones[:, :], sq2[:, 2 * j:2 * j + 2, :].rearrange("p k t -> p (k t)"),
                                               start=True, stop=True), ts_, xfree[j])
            td = dve.do(lambda e, j=j: e.tensor_scalar(sq2[:, 2 * j:2 * j + 2, :].rearrange("p k t -> p (k t)"), X[j][:, :], EPS, None, ALU.add), tp)
            xfree[j] = td
            td = act.do(lambda e, j=j: e.activation(sq2[:, 2 * j:2 * j + 2, :], sq2[:, 2 * j:2 * j + 2, :], ACT.Sqrt), td)
            td = dve.do(lambda e, j=j: e.reciprocal(sq2[:, 2 * j:2 * j + 2, :], sq2[:, 2 * j:2 * j + 2, :]), td)
            td = dve.do(lambda e, j=j, src=src: e.scalar_tensor_tensor(
                out=src, in0=src, scalar=(128 ** -0.5 if j < 2 else 1.0), in1=sq2[:, 2 * j:2 * j + 2, :],
                op0=ALU.mult, op1=ALU.mult), td)
        t_unit = td
        for n_, (src, dst) in enumerate(((kf, kt_), (vf, vt_))):
            for t_ in range(TT):
                b = 2 * n_ + t_
                for h in range(4):
                    tp = pe.do(lambda e, b=b, h=h, t_=t_, src=src: e.transpose(
                        X[b][:, h * P:(h + 1) * P], src[:, h, t_ * P:(t_ + 1) * P], ident[:, :]), t_unit, t_conv, xfree[b])
                xfree[b] = act.do(lambda e, b=b, t_=t_, dst=dst: e.activation(
                    dst[:, t_, :, :], X[b][:, :].rearrange("p (h d) -> p h d", h=4), ACT.Copy), tp, t_unit, *group_free)
        t_tm = xfree[3]
        for t_ in range(TT):
            for d_ in range(2):
                for (dst, src, g_) in ((ks, kt_, ek), (vb, vt_, beta)):
                    gv = streams(g_, h0)[:, t_, d_, :].rearrange("p (h a) -> p h a", a=1).broadcast_to((P, 4, P))
                    tkv = pool.do(lambda e, dst=dst, src=src, t_=t_, d_=d_, gv=gv: e.tensor_tensor(
                        dst[:, t_, d_ * 4:d_ * 4 + 4, :], src[:, t_, :, :], gv, ALU.mult), t_tm, xfree[1], t_gates)
        t_ksvb = tkv
        R = {}
        for n_, g_ in enumerate((gc, beta)):
            for t_ in range(TT):
                gv = streams(g_, h0)[:, t_, :, :]
                for d_ in range(2):
                    tb_ = dve.do(lambda e, t_=t_, d_=d_, gv=gv: e.tensor_tensor(
                        bsc[:, t_, d_ * 4:d_ * 4 + 4, :], id64[:, :].rearrange("p (a j) -> p a j", a=1).broadcast_to((P, 4, CH)),
                        gv[:, d_, :].rearrange("p (h a) -> p h a", a=1).broadcast_to((P, 4, CH)), ALU.mult),
                        t_unit, t_gates, *( [R[(0, t_)]] if n_ else []))
                b = 2 * n_ + t_
                R[(n_, t_)] = pe.do(lambda e, b=b, t_=t_: e.matmul(X[b][:, :], blk[:, :], bsc[:, t_, :, :].rearrange("p s j -> p (s j)"),
                                                                   start=True, stop=True), tb_, xfree[b])
        tg0 = [act_evacs(), dve_evacs()]
        for n_, other in enumerate((kf, qf)):
            for t_ in range(TT):
                for b in range(2):
                    for h in range(4):
                        cs = slice(t_ * P + 64 * b, t_ * P + 64 * b + 64)
                        o_ = t_ * 256 + h * 64
                        tqk = pe.do(lambda e, n_=n_, b=b, h=h, cs=cs, o_=o_, other=other: e.matmul(
                            G[n_][64 * b:64 * b + 64, o_:o_ + 64], kf[:, h, cs], other[:, h, cs], start=True, stop=True), t_unit, *tg0)
        def f4(buf, t_):
            return buf[:, t_, :, :]
        def g4(t_, n_):
            return G[n_][:, t_ * 256:(t_ + 1) * 256].rearrange("p (a h j) -> p a h j", a=1, h=4).broadcast_to((P, 2, 4, CH))
        def as4(v_):
            return v_.rearrange("p (d h) j -> p d h j", d=2)
        def mk(m_):
            return msk[:, m_, :, :].rearrange("p d (a j) -> p d a j", a=1).broadcast_to((P, 2, 4, CH))
        for t_ in range(TT):
            gcv = streams(gc, h0)[:, t_, :, :]
            btv = streams(beta, h0)[:, t_, :, :]
            for d_ in range(2):
                x3 = X[t_][:, d_ * 256:(d_ + 1) * 256].rearrange("p (h j) -> p h j", h=4)
                ta = dve.do(lambda e, d_=d_, x3=x3, gcv=gcv, t_=t_: e.tensor_tensor(
                    DR[:, t_, d_ * 4:d_ * 4 + 4, :], x3, gcv[:, d_, :].rearrange("p (h a) -> p h a", a=1).broadcast_to((P, 4, CH)),
                    ALU.subtract), R[(0, t_)], t_conv)
            xfree[t_] = ta
            tb_ = dve.do(lambda e, t_=t_: e.tensor_scalar(f4(Tm, t_), f4(DR, t_), -1.0, 0.0, ALU.mult, ALU.min), ta, *group_free)
            tb_ = act.do(lambda e, t_=t_: e.activation(f4(Tm, t_), f4(Tm, t_), ACT.Exp), tb_)
            tc_ = dve.do(lambda e, t_=t_: e.tensor_scalar(f4(LT, t_), f4(DR, t_), 0.0, None, ALU.min), ta, *group_free)
            tc_ = act.do(lambda e, t_=t_: e.activation(f4(LT, t_), f4(LT, t_), ACT.Exp), tc_)
            tb_ = dve.do(lambda e, t_=t_: e.tensor_tensor(as4(f4(Tm, t_)), as4(f4(Tm, t_)), mk(0), ALU.mult), tb_, t_masks)
            tb_ = dve.do(lambda e, t_=t_: e.tensor_tensor(as4(f4(Tm, t_)), as4(f4(Tm, t_)), g4(t_, 0), ALU.mult), tb_, tqk)
            for d_ in range(2):
                td_ = dve.do(lambda e, t_=t_, d_=d_, btv=btv: e.tensor_tensor(
                    Tm[:, t_, d_ * 4:d_ * 4 + 4, :], Tm[:, t_, d_ * 4:d_ * 4 + 4, :],
                    btv[:, d_, :].rearrange("p (h a) -> p h a", a=1).broadcast_to((P, 4, CH)), ALU.mult), tb_)
            tc_ = dve.do(lambda e, t_=t_: e.tensor_tensor(as4(f4(LT, t_)), as4(f4(LT, t_)), mk(1), ALU.mult), tc_)
            te_ = dve.do(lambda e, t_=t_: e.tensor_tensor(as4(f4(IT, t_)), as4(f4(LT, t_)), g4(t_, 1), ALU.mult), tc_, *group_free)
            tc_ = dve.do(lambda e, t_=t_: e.tensor_tensor(as4(f4(LT, t_)), as4(f4(LT, t_)), mk(2), ALU.mult), te_)
            tc_ = dve.do(lambda e, t_=t_: e.tensor_tensor(as4(f4(LT, t_)), as4(f4(LT, t_)), g4(t_, 0), ALU.mult), tc_)
            tc_ = dve.do(lambda e, t_=t_: e.tensor_tensor(f4(LT, t_), f4(LT, t_), X[2 + t_][:, :].rearrange("p (s j) -> p s j", s=NS), ALU.mult), tc_, R[(1, t_)])
            xfree[2 + t_] = tc_
            lv = lev[:, 0:1, :].broadcast_to((P, NS, CH))
            idb = id64[:, :].rearrange("p (a j) -> p a j", a=1).broadcast_to((P, NS, CH))
            td_ = dve.do(lambda e, t_=t_, lv=lv: e.tensor_tensor(f4(Tm, t_), f4(Tm, t_), lv, ALU.mult), td_)
            td_ = dve.do(lambda e, t_=t_, idb=idb: e.tensor_tensor(f4(Tm, t_), idb, f4(Tm, t_), ALU.subtract), td_)
            tf_ = dve.do(lambda e, t_=t_, lv=lv: e.tensor_tensor(f4(TT_, t_), f4(LT, t_), lv, ALU.mult), tc_, *group_free)
            tf_ = dve.do(lambda e, t_=t_, idb=idb: e.tensor_tensor(f4(TT_, t_), idb, f4(TT_, t_), ALU.subtract), tf_)
        t_T = tf_
        t_y = None
        yfree = None
        for l in range(1, 6):
            lvl = {}
            for t_ in range(TT):
                lv = lev[:, l:l + 1, :].broadcast_to((P, NS, CH))
                lvl[t_] = pool.do(lambda e, t_=t_, lv=lv: e.tensor_tensor(f4(AT, t_), f4(LT, t_), lv, ALU.mult), t_T, t_conv,
                                  *([yfree] if yfree else []))
            def small_mm(out_bank, lhs, rhs, t_, *w):
                tok = None
                for b in range(2):
                    cs = slice(64 * b, 64 * b + 64)
                    for s_ in range(NS):
                        tok = pe.do(lambda e, cs=cs, s_=s_: e.matmul(out_bank[cs, s_ * 64:s_ * 64 + 64], lhs[cs, t_, s_, :],
                                                                     rhs[cs, t_, s_, :], start=True, stop=True), *w)
                        w = ()
                return tok
            ty = {}
            for t_ in range(TT):
                tp = small_mm(X[t_], AT, Tm, t_, lvl[t_], t_T, xfree[t_])
                ty[t_] = act.do(lambda e, t_=t_: e.activation(f4(Ym, t_), X[t_][:, :].rearrange("p (s j) -> p s j", s=NS), ACT.Copy),
                                tp, t_conv, *([yfree] if yfree else []))
                xfree[t_] = ty[t_]
            for t_ in range(TT):
                tp = small_mm(X[2 + t_], TT_, Ym, t_, ty[t_], xfree[2 + t_])
                tp2 = small_mm(X[t_], Ym, TT_, t_, xfree[t_])
                xfree[2 + t_] = dve.do(lambda e, t_=t_: e.tensor_tensor(f4(Tm, t_), f4(Tm, t_), X[2 + t_][:, :].rearrange("p (s j) -> p s j", s=NS), ALU.subtract), tp)
                t_T = dve.do(lambda e, t_=t_: e.tensor_tensor(f4(TT_, t_), f4(TT_, t_), X[t_][:, :].rearrange("p (s j) -> p s j", s=NS), ALU.subtract), tp2)
                xfree[t_] = t_T
            yfree = t_T
        t_s = {0: None, 1: None}
        gfree = t_T
        for step in range(4):
            for d_ in range(2):
                c = step if d_ == 0 else 3 - step
                t_, b = c // 2, c % 2
                cs = slice(64 * b, 64 * b + 64)
                tok_ = slice(c * 64, c * 64 + 64)
                hb = [X[d_], G[2 + d_], X[2 + d_], G[d_]]
                sl = slice(d_ * 4, d_ * 4 + 4)
                bc4 = lambda v_: v_.rearrange("p (h a) -> p h a", a=1).broadcast_to((64, 4, P))
                b4 = lambda v_, h0=h0, cs=cs, t_=t_, d_=d_: bc4(streams(v_, h0)[cs, t_, d_, :])
                w3 = lambda bk, cs=cs: bk[cs, :].rearrange("p (h d) -> p h d", h=4)
                rd, vd, od = rr[cs, d_, :, :], vn[cs, d_, :, :], otmp[cs, d_, :, :]
                if step:
                    for h in range(4):
                        tk = pe.do(lambda e, h=h, cs=cs, tok_=tok_, d_=d_: e.matmul(
                            X[d_][cs, h * P:(h + 1) * P], kf[:, h, tok_], Sst[:, d_ * 4 + h, :], start=True, stop=True), t_s[d_], xfree[d_])
                    for h in range(4):
                        tq = pe.do(lambda e, h=h, cs=cs, tok_=tok_, d_=d_: e.matmul(
                            G[2 + d_][cs, h * P:(h + 1) * P], qf[:, h, tok_], Sst[:, d_ * 4 + h, :], start=True, stop=True), t_gfree[d_])
                    t1 = dve.do(lambda e, rd=rd, w3=w3, d_=d_, b4=b4: e.tensor_tensor(rd, w3(X[d_]), b4(be), ALU.mult), tk, gfree)
                    xfree[d_] = t1
                    t1 = dve.do(lambda e, rd=rd, t_=t_, sl=sl, cs=cs: e.tensor_tensor(rd, vb[cs, t_, sl, :], rd, ALU.subtract), t1, t_ksvb)
                    rsrc, tr_ = rr[:, d_, :, :], t1
                    get_r = lambda h, cs=cs, d_=d_: rr[cs, d_, h, :]
                else:
                    tr_ = t_ksvb
                    get_r = lambda h, cs=cs, d_=d_, t_=t_: vb[cs, t_, d_ * 4 + h, :]
                for h in range(4):
                    tv = pe.do(lambda e, h=h, cs=cs, d_=d_, t_=t_, get_r=get_r: e.matmul(
                        X[2 + d_][cs, h * P:(h + 1) * P], TT_[cs, t_, d_ * 4 + h, :], get_r(h), start=True, stop=True), tr_, xfree[2 + d_], gfree)
                tvn = act.do(lambda e, vd=vd, w3=w3, d_=d_: e.activation(vd, w3(X[2 + d_]), ACT.Copy), tv, gfree,
                             *([t_s[d_]] if step else []))
                xfree[2 + d_] = tvn
                for h in range(4):
                    if step < 3:
                        tst = pe.do(lambda e, h=h, cs=cs, d_=d_, t_=t_: e.matmul(
                            X[d_][:, h * P:(h + 1) * P], ks[cs, t_, d_ * 4 + h, :], vn[cs, d_, h, :], start=True, stop=True), tvn, xfree[d_], gfree)
                for h in range(4):
                    tin = pe.do(lambda e, h=h, cs=cs, d_=d_, t_=t_: e.matmul(
                        G[d_][cs, h * P:(h + 1) * P], IT[cs, t_, d_ * 4 + h, :], vn[cs, d_, h, :], start=True, stop=True), tvn, gfree)
                first_dir = (d_ == 0 and step < 2) or (d_ == 1 and step < 2)
                oo = o_all[cs, t_, h0:h0 + 4, :]
                if step < 3:
                    if step:
                        t2 = dve.do(lambda e, sl=sl, d_=d_, b=b, t_=t_, h0=h0: e.tensor_tensor(
                            Sst[:, sl, :], Sst[:, sl, :],
                            glb[:, b, :].rearrange("p (t d h) -> p t d h", t=TT, d=2)[:, t_, d_, h0:h0 + 4]
                            .rearrange("p (h a) -> p h a", a=1).broadcast_to((P, 4, P)), ALU.mult), tk, tq)
                        t2 = dve.do(lambda e, sl=sl, d_=d_: e.tensor_tensor(
                            Sst[:, sl, :], Sst[:, sl, :], X[d_][:, :].rearrange("p (h d) -> p h d", h=4), ALU.add), t2, tst)
                    else:
                        t2 = dve.do(lambda e, sl=sl, d_=d_: e.tensor_copy(
                            Sst[:, sl, :], X[d_][:, :].rearrange("p (h d) -> p h d", h=4)), tst, gfree)
                    t_s[d_] = t2
                    xfree[d_] = t2
                if step:
                    t3 = dve.do(lambda e, od=od, w3=w3, d_=d_, b4=b4: e.tensor_tensor(od, w3(G[2 + d_]), b4(eg), ALU.mult), tq, t_tm)
                    t3 = dve.do(lambda e, od=od, w3=w3, d_=d_: e.tensor_tensor(od, od, w3(G[d_]), ALU.add), tin, t3)
                else:
                    t3 = dve.do(lambda e, od=od, w3=w3, d_=d_: e.tensor_copy(od, w3(G[d_])), tin, t_tm)
                if step < 2:
                    t3 = pool.do(lambda e, oo=oo, od=od: e.tensor_copy(oo, od), t3, *group_free)
                else:
                    t3 = pool.do(lambda e, oo=oo, od=od: e.tensor_tensor(oo, oo, od, ALU.add), t3, o_done)
                o_done = t3
                if step == 0 and d_ == 0:
                    t_gfree = {}
                t_gfree[d_] = t3
            gfree = t_gfree[1]
        group_free = [o_done, (S["pe_done"], pe.n), (S["dve_done"], dve.n), (S["act_done"], act.n)]
    t_o = group_free

    zs = place("zs", [P, TT, D], F32, offset=F0 + 24576)
    gemm(4, cols(Win, first=C_Z), tm_chunk(h_hi, h_lo), act_chunk=sig_tm(zs, ACT.Silu), ready=t_o, act_ready=t_o)
    of = o_all[:, :, :, :].rearrange("p t h d -> p (t h) d")
    osq = place("osq", [P, 16, P], F32, offset=XN)
    rh = gb[:, 6, :, :].rearrange("p t s -> p (t s)")[:, 0:16]
    rh2 = gb[:, 7, :, :].rearrange("p t s -> p (t s)")[:, 0:16]
    t = act.do(lambda e: e.activation(osq[:, :, :], of, ACT.Square), *t_o)
    t = dve.do(lambda e: e.tensor_reduce(rh, osq[:, :, :], AX_X, ALU.add), t)
    t = dve.do(lambda e: e.tensor_scalar(rh, rh, 1.0 / P, EPS, ALU.mult, ALU.add), t)
    t = act.do(lambda e: e.activation(rh, rh, ACT.Sqrt), t)
    t = dve.do(lambda e: e.reciprocal(rh2, rh), t)
    t = dve.do(lambda e: e.tensor_tensor(of, of, rh2.rearrange("p (s a) -> p s a", a=1).broadcast_to((P, 16, P)), ALU.mult), t)
    t = dve.do(lambda e: e.tensor_tensor(of, of, zs[:, :, :].rearrange("p t (h d) -> p (t h) d", h=8), ALU.mult), t, act_evacs())

    def to_features(src, ready, gain, free):
        for j in range(KT // 2):
            w = list(ready) + [xfree[j]]
            for kk in range(2):
                for t_ in range(TT):
                    k = 2 * j + kk
                    tp = pe.do(lambda e, j=j, kk=kk, k=k, t_=t_: e.transpose(
                        X[j][:, kk * SEQ + t_ * P:kk * SEQ + (t_ + 1) * P],
                        src[:, t_, k * P:(k + 1) * P], ident[:, :]), *w)
            x3 = X[j][:, :].rearrange("p (k t) -> p k t", k=2)
            dsl = slice(2 * j, 2 * j + 2)
            if gain is None:
                th = act.do(lambda e, x3=x3, dsl=dsl: e.activation(a_hi[:, dsl, :], x3, ACT.Copy), tp, *free)
                tl = dve.do(lambda e, x3=x3, dsl=dsl: e.tensor_tensor(a_lo[:, dsl, :], x3, a_hi[:, dsl, :].bitcast(F32), ALU.subtract), th, *free)
            else:
                th = act.do(lambda e, x3=x3, dsl=dsl: e.activation(a_hi[:, dsl, :], x3, ACT.Copy, scale=gain), tp, *free)
                tl = dve.do(lambda e, x3=x3, dsl=dsl: e.scalar_tensor_tensor(
                    out=a_lo[:, dsl, :], in0=x3, scalar=gain, in1=a_hi[:, dsl, :].bitcast(F32),
                    op0=ALU.mult, op1=ALU.subtract), th, *free)
            xfree[j] = tl
        return tl
    ov = o_all[:, :, :, :].rearrange("p t h d -> p t (h d)")
    tf = to_features(ov, [t], col("dn_o_gain_2"), t_o)
    t_zs_free = t
    gemm(4, cols(Win, first=C_G), tm_chunk(h_hi, h_lo), act_chunk=sig_tm(zs, ACT.Sigmoid), act_ready=[t_zs_free])
    t_gat = act_evacs()
    mt = place("mt", [P, 2, TT, 256], F32, offset=XN)
    ev_m = st.evac_v

    def merge(e, c, u, ch):
        e.wait_ge(S["dve_evac"], ev_m + c - 1)
        cs = slice(c * 256, (c + 1) * 256)
        ch.link(e.tensor_tensor(mt[:, c % 2, :, :], G[u][:, :].rearrange("p (t n) -> p t n", t=TT), zs[:, :, cs], ALU.mult))
        return e.tensor_tensor(merged[:, :, cs], merged[:, :, cs], mt[:, c % 2, :, :], ALU.add)
    gemm(4, cols(A["w_o_dn_2"][0]), tm_chunk(a_hi, a_lo), dve_chunk=merge, dve_links=1, ready=[tf], dve_ready=[t_gat, tf])
    tf = to_features(merged, [dve_evacs()], None, [all_used()])

    def residual(gate):
        ev0 = st.evac_v

        def chunk(e, c, u, ch):
            e.wait_ge(S["dve_evac"], ev0 + c - 1)
            cs = slice(c * 256, (c + 1) * 256)
            ch.link(e.tensor_tensor(mt[:, c % 2, :, :], G[u][:, :].rearrange("p (t n) -> p t n", t=TT),
                                    gt[:, gate:gate + 1, cs].broadcast_to((P, TT, 256)), ALU.mult))
            return e.tensor_tensor(x[:, :, cs], x[:, :, cs], mt[:, c % 2, :, :], ALU.add)
        return chunk
    gemm(4, cols(A["w_out_2"][0]), tm_chunk(a_hi, a_lo), dve_chunk=residual(0), dve_links=1, ready=[tf], dve_ready=[tf])
    t_x1 = dve_evacs()

    th = norm_to_features(x, [t_x1], lambda k: mcol[:, 3, k:k + 1], lambda k: mcol[:, 2, k:k + 1], [all_used()])
    E, C = N_EXP, CAP
    xeT = place("xeT", [P, KT, E * C], F32, offset=F0 + 8192)
    ye = place("ye", [P, E // 4, D], F32, offset=F0 + 24576)
    Sa = place("Sa", [P, TT, E * C], F32, offset=A0)
    SG = place("SG", [P, TT, E * C], F32, offset=A0 + 4096)
    GT = place("GT", [P, E // 4, SEQ], F32, offset=A0 + 8192)
    gus = place("gus", [64, 2, D], F32, offset=A0 + 12288)
    tmpd = place("tmpd", [C, D], F32, offset=A0 + 20480)
    sgl = place("sgl", [P, KT * C], F32, offset=A0 + 24576)
    prd = place("prd", [P, KT, C], F32, offset=A0 + 25600)
    xes = [place(f"xes{j}", [P, KT, 2 * C], F32R, offset=A0 + 26624 + 2048 * j) for j in range(2)]
    hid = [place(f"hid{j}", [P, KT, 2 * C], F32R, offset=A0 + 30720 + 2048 * j) for j in range(2)]
    lg = place("lg", [E, SEQ], F32, offset=A0 + 34816)
    cur = place("cur", [E, 2, SEQ], F32, offset=A0 + 35840)
    mk_ = place("mk_", [E, SEQ], F32, offset=A0 + 37888)
    ps = place("ps", [E, SEQ], F32, offset=A0 + 38912)
    m8 = place("m8", [E, 8], F32, offset=A0 + 39936)
    aff = place("aff", [P, 2, TT, E], F32, offset=A0 + 40000)
    sm = place("sm", [P, 4, TT], F32, offset=A0 + 40384)
    iot = place("iot", [P, C], F32, offset=A0 + 40448)
    comb = place("comb", [64, C], F32, offset=A0 + 40576)
    cap_free = [all_used(), t_x1]
    t_i = pool.do(lambda e: e.iota(iot[:, :], pattern=[[1, C]], base=1, channel_multiplier=0,
                                   allow_small_or_imprecise_dtypes=True), *cap_free)
    t = pool.do(lambda e: e.memset(comb[:, :], 0.0), *cap_free)
    for base_ in (0, -32):
        t = pool.do(lambda e, b_=base_: e.affine_select(out=comb[:, :], in_=comb[:, :], compare_op=ALU.not_equal, fill=1.0,
                                                        base=b_, pattern=[[-1, C]], channel_multiplier=1), t)
    t_comb = t
    Wr = A["w_router_2"][0].rearrange("(k p) n -> p k n", p=P)

    def r_source(c, slot):
        return [(slot[:, 0:KT * E].rearrange("p (k n) -> p k n", k=KT), Wr)]

    def r_chunk(e, c, u, slot):
        for k in range(KT):
            w0, w1 = whi[slot][:, k * E:(k + 1) * E], wlo[slot][:, k * E:(k + 1) * E]
            e.matmul(G[u][0:E, 0:SEQ], w0, h_hi[:, k, :], start=(k == 0), stop=False)
            e.matmul(G[u][0:E, 0:SEQ], w0, h_lo[:, k, :], start=False, stop=False)
            ins = e.matmul(G[u][0:E, 0:SEQ], w1, h_hi[:, k, :], start=False, stop=(k == KT - 1))
        return ins
    gemm(1, r_source, r_chunk, ready=[th], act_ready=cap_free,
         act_chunk=lambda e, c, u, ch: e.activation(lg[:, :], G[u][0:E, 0:SEQ], ACT.Copy))
    for t_ in range(TT):
        tp = pe.do(lambda e, t_=t_: e.transpose(X[0][:, t_ * E:(t_ + 1) * E], lg[:, t_ * P:(t_ + 1) * P], ident[0:E, 0:E]), act_evacs(), xfree[0])
    l3 = X[0][:, 0:TT * E].rearrange("p (t n) -> p t n", t=TT)
    col3 = lambda v_: v_.rearrange("p (t a) -> p t a", a=1).broadcast_to((P, TT, E))
    a0, a1 = aff[:, 0, :, :], aff[:, 1, :, :]
    t = dve.do(lambda e: e.tensor_reduce(sm[:, 0, :], l3, AX_X, ALU.max), tp, *cap_free)
    t = dve.do(lambda e: e.tensor_tensor(a0, l3, col3(sm[:, 0, :]), ALU.subtract), t)
    xfree[0] = t
    t = act.do(lambda e: e.activation(a0, a0, ACT.Exp), t)
    t = dve.do(lambda e: e.tensor_reduce(sm[:, 1, :], a0, AX_X, ALU.add), t)
    t = dve.do(lambda e: e.reciprocal(sm[:, 2, :], sm[:, 1, :]), t)
    t_aff = dve.do(lambda e: e.tensor_tensor(a0, a0, col3(sm[:, 2, :]), ALU.mult), t)
    for t_ in range(TT):
        tp = pe.do(lambda e, t_=t_: e.transpose(X[1][0:E, t_ * P:(t_ + 1) * P], a0[:, t_, :], ident[:, :]), t_aff, xfree[1])
    t = dve.do(lambda e: e.tensor_copy(cur[:, 0, :], X[1][0:E, 0:SEQ]), tp, *cap_free)
    xfree[1] = t
    for r_ in range(C // 8):
        a_, b_ = r_ % 2, (r_ + 1) % 2
        t = dve.do(lambda e, a_=a_: e.max(m8[:, :], cur[:, a_, :]), t)
        t = dve.do(lambda e, a_=a_, b_=b_: e.match_replace(cur[:, b_, :], m8[:, :], cur[:, a_, :], -1.0), t)
    t = dve.do(lambda e: e.tensor_scalar(mk_[:, :], cur[:, 0, :], 0.0, None, ALU.is_lt), t)
    t1 = dve.do(lambda e: e.memset(lg[:, :], 0.0), act_evacs(), tp)
    t = dve.do(lambda e: e.tensor_tensor_scan(ps[:, :], mk_[:, :], lg[:, :], 0.0, ALU.add, ALU.add), t, t1)
    t = dve.do(lambda e: e.tensor_tensor(ps[:, :], ps[:, :], mk_[:, :], ALU.mult), t)
    for t_ in range(TT):
        tp = pe.do(lambda e, t_=t_: e.transpose(X[0][:, t_ * E:(t_ + 1) * E], ps[:, t_ * P:(t_ + 1) * P], ident[0:E, 0:E]), t, xfree[0])
    t = dve.do(lambda e: e.tensor_copy(a1, l3), tp)
    xfree[0] = t
    e4 = lambda buf, t_: buf[:, t_, :].rearrange("p (e c) -> p e c", e=E)
    for t_ in range(TT):
        ta = dve.do(lambda e, t_=t_: e.tensor_tensor(
            e4(Sa, t_), iot[:, :].rearrange("p (a c) -> p a c", a=1).broadcast_to((P, E, C)),
            a1[:, t_, :].rearrange("p (e a) -> p e a", a=1).broadcast_to((P, E, C)), ALU.is_equal), t, t_i, *cap_free)
        tb_ = dve.do(lambda e, t_=t_: e.tensor_tensor(
            e4(SG, t_), e4(Sa, t_), a0[:, t_, :].rearrange("p (e a) -> p e a", a=1).broadcast_to((P, E, C)), ALU.mult), ta)
    for k in range(KT):
        b = k % 4
        for t_ in range(TT):
            tp = pe.do(lambda e, b=b, k=k, t_=t_: e.matmul(X[b][:, :], xn[:, t_, k * P:(k + 1) * P], Sa[:, t_, :],
                                                           start=(t_ == 0), stop=(t_ == 1)), ta, tb_, xfree[b])
        xfree[b] = act.do(lambda e, b=b, k=k: e.activation(xeT[:, k, :], X[b][:, :], ACT.Identity,
                                                           bias=mcol[:, 2, k:k + 1], scale=mcol[:, 3, k:k + 1]), tp, *cap_free)
    t_xe = xfree[3]
    for g_ in range(E // 4):
        for t_ in range(TT):
            tp = pe.do(lambda e, g_=g_, t_=t_: e.transpose(X[g_ % 4][:, t_ * P:(t_ + 1) * P], SG[:, t_, g_ * P:(g_ + 1) * P], ident[:, :]), tb_, xfree[g_ % 4])
        xfree[g_ % 4] = dve.do(lambda e, g_=g_: e.tensor_copy(GT[:, g_, :], X[g_ % 4][:, 0:SEQ]), tp, *cap_free)
    t_gt = xfree[3]

    base = st.n
    done_before = [(S["pe_done"], pe.n), (S["act_done"], act.n), (S["dve_done"], dve.n), act_evacs(), dve_evacs(), t_comb]
    sx, sgu, scb, shd, sdn, sye = (nc.alloc_semaphore(n_) for n_ in
                                   ("xe_split", "gate_up_out", "combined", "hidden_split", "down_out", "ye_added"))
    echain_a, echain_v = nc.alloc_semaphore("expert_act_chain"), nc.alloc_semaphore("expert_dve_chain")
    Wg = A["w_gate_2"][0].rearrange("e (k p) n -> p e k n", p=P)
    Wu = A["w_up_2"][0].rearrange("e (k p) n -> p e k n", p=P)
    Wd_ = A["w_down_2"][0].rearrange("e (k p) n -> p e k n", p=P)

    def experts(e, step, flush):
        step(0, 0, True)
        with e.Fori(0, 3) as i:
            for q in range(4):
                step(i * 4 + (q + 1), q + 1, False)
        for x_ in range(13, E):
            step(x_, x_, False)
        flush()

    def m_gu(x_):
        return base + (0 if isinstance(x_, int) and x_ == 0 else x_ * 12 - 4)

    def m_dn(x_):
        if isinstance(x_, int) and x_ == E - 1:
            return m_gu(E - 1) + 8 + 4
        return m_gu(x_ + 1) + 8

    def sp_experts(e):
        def load(W_, x_, m, j):
            slot = (base + j) % RING
            e.wait_ge(S["lo_ready"], m + j + 1)
            for dst, src in halves([(raw[slot][:, :].rearrange("p (k n) -> p k n", k=KT),
                                     W_[:, bass.ds(x_, 1), :, j * 256:(j + 1) * 256].rearrange("p a k n -> p (a k) n"))]):
                e.dma_start(dst, src).then_inc(raw_in[slot], 16)

        def step(x_, q, first):
            for j in range(4):
                load(Wg, x_, m_gu(x_), j)
            for j in range(4):
                load(Wu, x_, m_gu(x_) + 4, j)
            if not first:
                for j in range(4):
                    load(Wd_, x_ - 1, m_gu(x_) + 8, j)
        experts(e, step, lambda: [load(Wd_, E - 1, m_dn(E - 1), j) for j in range(4)])
    sp.raw(sp_experts)

    def pe_experts(e):
        for w in done_before:
            e.wait_ge(*w)

        def chunk(m, j, lhs, dst):
            slot = (base + j) % RING
            e.wait_ge(S["hi_ready"], m + j + 1)
            e.wait_ge(S["lo_ready"], RING + m + j + 1)
            for k in range(KT):
                e.matmul(dst, lhs[:, k, :], whi[slot][:, k * 256:(k + 1) * 256], start=(k == 0), stop=False)
                ins = e.matmul(dst, lhs[:, k, :], wlo[slot][:, k * 256:(k + 1) * 256], start=False, stop=(k == KT - 1))
            ins.then_inc(S["chunk_used"], 1)

        def down(x_, q, j):
            b, o_ = j // 2, (j % 2) * 256
            chunk(m_dn(x_), j, hid[q % 2], X[b][0:64, o_:o_ + 256])

        def step(x_, q, first):
            e.wait_ge(sx, x_ + 1)
            if not first:
                e.wait_ge(sgu, 2 * x_)
            for g_ in range(2):
                for j in range(4):
                    b, o_ = 2 * g_ + j // 2, (j % 2) * 256
                    chunk(m_gu(x_) + 4 * g_, j, xes[q % 2], G[b][0:64, o_:o_ + 256])
            if not first:
                e.wait_ge(shd, x_)
                e.wait_ge(sye, x_)
                down(x_ - 1, q - 1, 0)
                down(x_ - 1, q - 1, 1)
            combine(x_, first)
            if not first:
                down(x_ - 1, q - 1, 2)
                down(x_ - 1, q - 1, 3)

        def combine(x_, first):
            e.wait_ge(sgu, 2 * x_ + 2)
            e.wait_ge(shd, x_)
            for g_ in range(2):
                for f in range(KT):
                    ins = e.matmul(X[2][:, g_ * 256 + f * C:g_ * 256 + (f + 1) * C], gus[:, g_, f * P:(f + 1) * P],
                                   comb[:, :], start=True, stop=True)
            ins.then_inc(scb, 1)

        def flush():
            e.wait_ge(shd, E)
            e.wait_ge(sye, E)
            for j in range(4):
                down(E - 1, E - 1, j)
        experts(e, step, flush)
    pe.raw(pe_experts)

    def act_experts(e):
        for w in done_before:
            e.wait_ge(*w)
        stop_at = base + 12 * E

        def sp_(m, j, n_=1):
            if isinstance(m, int) and m + j + AHEAD >= stop_at:
                return
            hi_split(e, m + j + AHEAD, (base + j + AHEAD) % RING)

        def xe_hi(x_, q):
            e.wait_ge(S["chunk_used"], RING + m_gu(x_) + 0 - (4 if not (isinstance(x_, int) and x_ == 0) else 0))
            e.activation(xes[q % 2][:, :, 0:C], xeT[:, :, bass.ds(x_ * C, C)], ACT.Copy).then_inc(echain_a, 1)

        def step(x_, q, first):
            if first:
                xe_hi(0, 0)
            for j in range(4):
                sp_(m_gu(x_), j)
            e.wait_ge(S["chunk_used"], RING + m_gu(x_) + 4)
            e.wait_ge(scb, x_)
            e.activation(gus[:, 0, 0:BANK], G[0][0:64, :], ACT.Copy)
            e.activation(gus[:, 0, BANK:D], G[1][0:64, :], ACT.Copy).then_inc(sgu, 1)
            for j in range(4):
                sp_(m_gu(x_) + 4, j)
            if first:
                xe_next(x_, q)
                silu(x_)
            else:
                sp_(m_gu(x_) + 8, 0)
                sp_(m_gu(x_) + 8, 1)
                xe_next(x_, q)
                sp_(m_gu(x_) + 8, 2)
                silu(x_)
                sp_(m_gu(x_) + 8, 3)
                low(x_ - 1)

        def xe_next(x_, q):
            if isinstance(x_, int) and x_ == E - 1:
                return
            e.activation(xes[(q + 1) % 2][:, :, 0:C], xeT[:, :, bass.ds(x_ * C + C, C)], ACT.Copy).then_inc(echain_a, 1)

        def silu(x_):
            e.wait_ge(scb, x_ + 1)
            e.wait_ge(shd, x_)
            e.activation(sgl[:, :], X[2][:, 0:256], ACT.Silu).then_inc(echain_s, 1)

        def low(x_):
            e.wait_ge(S["chunk_used"], RING + m_dn(x_) + 4)
            e.wait_ge(sye, x_ + 1)
            e.activation(tmpd[:, 0:BANK], X[0][32:64, :], ACT.Copy)
            e.activation(tmpd[:, BANK:D], X[1][32:64, :], ACT.Copy).then_inc(sdn, 1)

        def flush():
            for j in range(4):
                sp_(m_dn(E - 1), j)
            low(E - 1)
        experts(e, step, flush)
    echain_s = nc.alloc_semaphore("silu_out")
    act.raw(act_experts)

    def dve_experts(e):
        for w in done_before:
            e.wait_ge(*w)
        stop_at = base + 12 * E

        def sp_(m, j):
            if isinstance(m, int) and m + j + AHEAD >= stop_at:
                return
            lo_split(e, m + j + AHEAD, (base + j + AHEAD) % RING)

        def xe_lo(x_, q):
            if isinstance(x_, int) and x_ == E:
                return
            e.wait_ge(echain_a, x_ + 1)
            e.tensor_tensor(xes[q % 2][:, :, C:2 * C], xeT[:, :, bass.ds(x_ * C, C)],
                            xes[q % 2][:, :, 0:C].bitcast(F32), ALU.subtract).then_inc(sx, 1)

        def step(x_, q, first):
            if first:
                xe_lo(0, 0)
            for g_ in range(2):
                for j in range(4):
                    sp_(m_gu(x_) + 4 * g_, j)
            e.wait_ge(S["chunk_used"], RING + m_gu(x_) + 8)
            e.wait_ge(scb, x_)
            e.tensor_copy(gus[:, 1, 0:BANK], G[2][0:64, :])
            e.tensor_copy(gus[:, 1, BANK:D], G[3][0:64, :]).then_inc(sgu, 1)
            if first:
                xe_lo(x_ + 1, q + 1)
                gate(x_, q)
            else:
                sp_(m_gu(x_) + 8, 0)
                sp_(m_gu(x_) + 8, 1)
                xe_lo(x_ + 1, q + 1)
                sp_(m_gu(x_) + 8, 2)
                gate(x_, q)
                sp_(m_gu(x_) + 8, 3)
                add(x_ - 1, q - 1)

        def gate(x_, q):
            e.wait_ge(echain_s, x_ + 1)
            ch = Chain(e, echain_v, x_ * 2)
            ch.link(e.tensor_tensor(prd[:, :, :], sgl[:, :].rearrange("p (f c) -> p f c", f=KT),
                                    X[2][:, 256:512].rearrange("p (f c) -> p f c", f=KT), ALU.mult))
            ch.link(e.tensor_copy(hid[q % 2][:, :, 0:C], prd[:, :, :]))
            e.tensor_tensor(hid[q % 2][:, :, C:2 * C], prd[:, :, :], hid[q % 2][:, :, 0:C].bitcast(F32),
                            ALU.subtract).then_inc(shd, 1)

        def add(x_, q):
            e.wait_ge(sdn, x_ + 1)
            qd = q % 4
            g_ = x_ // 4 if isinstance(x_, int) else (x_ - qd) // 4
            for b in range(2):
                ins = e.tensor_tensor(
                    ye[32 * qd:32 * qd + 32, bass.ds(g_, 1), b * BANK:(b + 1) * BANK].rearrange("p a n -> p (a n)"),
                    X[b][0:C, :], tmpd[:, b * BANK:(b + 1) * BANK], ALU.add)
            ins.then_inc(sye, 1)

        def flush():
            for j in range(4):
                sp_(m_dn(E - 1), j)
            add(E - 1, E - 1)
        experts(e, step, flush)
    dve.raw(lambda e: e.memset(small[:, 187:188], 0.0).then_inc(sye, 1))
    dve.raw(dve_experts)
    st.n += 12 * E

    for t_ in range(TT):
        for hf in range(2):
            for g_ in range(E // 4):
                tp = pe.do(lambda e, t_=t_, hf=hf, g_=g_: e.matmul(
                    G[2 * t_ + hf][:, :], GT[:, g_, t_ * P:(t_ + 1) * P], ye[:, g_, hf * BANK:(hf + 1) * BANK],
                    start=(g_ == 0), stop=(g_ == E // 4 - 1)), (sye, E + 1), (sgu, 2 * E), t_gt)
            cs = slice(hf * BANK, (hf + 1) * BANK)
            t = dve.do(lambda e, t_=t_, hf=hf, cs=cs: e.tensor_tensor(xn[:, t_, cs], G[2 * t_ + hf][:, :], gt[:, 1, cs], ALU.mult), tp)
            t = dve.do(lambda e, t_=t_, cs=cs: e.tensor_tensor(x[:, t_, cs], x[:, t_, cs], xn[:, t_, cs], ALU.add), t)
    gf2 = place("gf2b", [P, D], F32, offset=A0)
    g2_in = nc.alloc_semaphore("g_final_in")

    def load_g2(e):
        e.wait_ge(sye, E + 1)
        e.dma_start(gf2[:, :], A["g_final_2"].rearrange("(a d) -> a d", a=1).broadcast_to((P, D))).then_inc(g2_in, 16)
    act.raw(load_g2)
    rs, t = rstd_rows(x, [t], D, "")
    for t_ in range(TT):
        dve.do(lambda e, t_=t_, rs=rs: e.scalar_tensor_tensor(
            out=x[:, t_, :], in0=x[:, t_, :], scalar=rs[:, t_:t_ + 1], in1=gf2[:, :],
            op0=ALU.mult, op1=ALU.mult), t, (g2_in, 16))
    return finish()


def constants():
    inv = np.zeros((ROPE_2, 2), np.float32)
    f1 = np.float32(THETA_1) ** (-np.arange(0, ROT, 2, dtype=np.float32) / np.float32(ROT))
    f2 = np.float32(THETA_2) ** (-np.arange(ROPE_2 // 2, dtype=np.float32) / np.float32(ROPE_2 // 2))
    inv[:, 0] = np.tile(f1, 4)
    inv[:, 1] = np.tile(f2, 2)
    return {"inv_freq": inv}


def kernel(**inputs):
    import concourse.bacc as bacc
    from concourse.bass_utils import run_bass_kernel_spmd

    nc = bacc.Bacc("TRN2", target_bir_lowering=False, num_devices=1, dynamic_dma_scratch_size=1024)
    arrays, A = {}, {}
    for name, value in list(inputs.items()) + list(constants().items()):
        a = np.ascontiguousarray(value)
        arrays[f"in_{name}_dram"] = a
        A[name] = nc.dram_tensor(f"in_{name}_dram", a.shape, mybir.dt.from_np(a.dtype), kind="ExternalInput").ap()
    out = nc.dram_tensor("out_0_dram", [1, SEQ, D], F32, kind="ExternalOutput").ap()
    build(nc, A, out)
    r = run_bass_kernel_spmd(nc, [arrays], core_ids=[0])
    return r.results[0]["out_0_dram"]
```

```python
import math

import concourse.bass as bass
import numpy as np
from concourse import mybir

ALU = mybir.AluOpType
ACT = mybir.ActivationFunctionType
F32 = mybir.dt.float32
F32R = mybir.dt.float32r
I32 = mybir.dt.int32
AX_X = mybir.AxisListType.X

P = 128
EPS = 1e-6
RING = 4
LANDED = 2 * 16
AHEAD = 2
CHUNK_W = 2048
BANK = 512

SEQ = 256
D = 1024
KT = D // P
TT = SEQ // P
D_FF = 2816
FT = D_FF // P
ROT = 32
THETA_1 = 500000.0
CONV1 = 3
CONV2 = 5
DN_H = 8
CH = 64
ROPE_2 = 64
THETA_2 = 10000.0
N_EXP = 16
CAP = 2 * SEQ // N_EXP

TWO_PI = 2.0 * math.pi
TP1 = 6.28125
TP2 = float(np.float32(TWO_PI - TP1))
TP3 = float(np.float32(TWO_PI - TP1 - TP2))
ROUND = 1.5 * 2.0**23


class Queue:

    def __init__(self, sem, chain):
        self.sem, self.n, self.ops = sem, 0, []
        self.chain, self.links = chain, 0

    def do(self, fn, *after):
        self.n += 1

        def run(e):
            for sem, value in after:
                e.wait_ge(sem, value)
            fn(e).then_inc(self.sem, 1)

        self.ops.append(run)
        return (self.sem, self.n)

    def raw(self, fn):
        self.ops.append(fn)


class Chain:

    def __init__(self, e, sem, base):
        self.e, self.sem, self.base, self.k = e, sem, base, 0

    def link(self, ins):
        self.k += 1
        ins.then_inc(self.sem, 1)
        self.e.wait_ge(self.sem, self.base + self.k)

    def link_but_one(self, ins, last=False):
        self.k += 1
        ins.then_inc(self.sem, 1)
        if self.k > 1:
            self.e.wait_ge(self.sem, self.base + self.k - (0 if last else 1))


def build(nc, A, out):
    sbuf_at = {}
    top = [0]

    def place(name, shape, dt, offset=None):
        size = 4 * int(np.prod(shape[1:]))
        if offset is None:
            offset = top[0]
            top[0] += (size + 31) // 32 * 32
        sbuf_at[name] = offset
        return nc.alloc_sbuf_tensor_at(name, list(shape), dt, offset=BASE + offset)

    BASE = (nc.sbuf_base + 63) // 64 * 64

    S = {n: nc.alloc_semaphore(n) for n in (
        "pe_done", "act_done", "dve_done", "pool_done", "sp_done",
        "pe_chain", "act_chain", "dve_chain", "pool_chain",
        "hi_ready", "lo_ready", "chunk_used", "act_evac", "dve_evac")}
    raw_in = [nc.alloc_semaphore(f"raw_in{s}") for s in range(RING)]

    pe = Queue(S["pe_done"], S["pe_chain"])
    act = Queue(S["act_done"], S["act_chain"])
    dve = Queue(S["dve_done"], S["dve_chain"])
    pool = Queue(S["pool_done"], S["pool_chain"])
    sp = Queue(S["sp_done"], None)

    bank = [nc.alloc_psum_tensor(f"bank{b}", [P, BANK], F32) for b in range(8)]
    G = bank[:4]
    X = bank[4:]

    raw = [place(f"w_raw{s}", [P, CHUNK_W], F32) for s in range(RING)]
    whi = [place(f"w_hi{s}", [P, CHUNK_W], F32R) for s in range(RING)]
    wlo = [place(f"w_lo{s}", [P, CHUNK_W], F32R) for s in range(RING)]
    x = place("x", [P, TT, D], F32)
    h_hi = place("h_hi", [P, KT, SEQ], F32R)
    h_lo = place("h_lo", [P, KT, SEQ], F32R)
    xn = place("xn", [P, TT, D], F32)
    ident = place("ident", [P, P], F32)
    ones = place("ones", [P, P], F32)
    vcol = place("vcol", [P, 256], F32)
    small = place("small", [P, 192], F32)
    neg_half = place("neg_half", [P, 4], F32)
    eps = place("eps", [P, 4], F32)
    swap1 = place("swap1", [ROT, ROT], F32)
    swap2 = place("swap2", [ROPE_2, ROPE_2], F32)
    rope1 = place("rope1", [ROT, 2, SEQ], F32)
    rope2 = place("rope2", [ROPE_2, 2, SEQ], F32)
    a_hi = place("a_hi", [P, FT, SEQ], F32R)
    a_lo = place("a_lo", [P, FT, SEQ], F32R)
    invf = place("invf", [ROPE_2, 2], F32)
    F0 = top[0]

    class Stream:
        n = 0
        evac_a = 4
        evac_v = 4
        tiles = None
    st = Stream()

    def all_used():
        return (S["chunk_used"], RING + st.n)

    def act_evacs():
        return (S["act_evac"], st.evac_a)

    def dve_evacs():
        return (S["dve_evac"], st.evac_v)

    def finish():
        stored = nc.alloc_semaphore("stored")
        waits = [all_used(), dve_evacs(), act_evacs(), (S["dve_done"], dve.n), (S["pool_done"], pool.n)]

        def store(e):
            for w in waits:
                e.wait_ge(*w)
            e.dma_start(out[0].rearrange("(t p) d -> p t d", p=P), x[:, :, :]).then_inc(stored, 16)
            e.wait_ge(stored, 16)
        sp.raw(store)
        with nc.Block() as block:
            for engine, queue in ((block.tensor, pe), (block.scalar, act), (block.vector, dve),
                                  (block.gpsimd, pool), (block.sync, sp)):
                def run(e, queue=queue):
                    for op in queue.ops:
                        op(e)
                engine(run)

    def loop(e, n, body):
        full = n // RING
        if full >= 2:
            with e.Fori(0, full) as i:
                for u in range(RING):
                    body(i * RING + u, u)
        else:
            full = 0
        for c in range(full * RING, n):
            body(c, c % RING)

    def halves(parts):
        if len(parts) == 2:
            return parts
        (dst, src), = parts
        h = dst.shape[1] // 2
        return [(dst[:, 0:h, :], src[:, 0:h, :]), (dst[:, h:2 * h, :], src[:, h:2 * h, :])]

    def load_chunks(n, source, base):
        def run(e):
            def one(c, u):
                slot = (base + u) % RING
                m = base + c
                e.wait_ge(S["lo_ready"], m + 1)
                for dst, src in halves(source(c, raw[slot])):
                    e.dma_start(dst, src).then_inc(raw_in[slot], 16)
            loop(e, n, one)
        sp.raw(run)

    def hi_split(e, m, slot):
        e.wait_ge(raw_in[slot], (m - slot) * (LANDED // RING) + LANDED)
        e.wait_ge(S["chunk_used"], m + 1)
        e.activation(whi[slot][:, :], raw[slot][:, :], ACT.Copy).then_inc(S["hi_ready"], 1)

    def lo_split(e, m, slot):
        e.wait_ge(S["hi_ready"], m + 1)
        e.wait_ge(S["chunk_used"], m + 1)
        e.tensor_tensor(wlo[slot][:, :], raw[slot][:, :], whi[slot][:, :].bitcast(F32),
                        ALU.subtract).then_inc(S["lo_ready"], 1)

    def first_splits():
        for m in range(AHEAD):
            act.raw(lambda e, m=m: hi_split(e, m, m % RING))
            dve.raw(lambda e, m=m: lo_split(e, m, m % RING))

    def gemm(n, source, pe_chunk, act_chunk=None, dve_chunk=None, ready=(), act_ready=(),
             dve_ready=(), last=False, act_links=0, dve_links=0, banks_of=None):
        base = st.n
        ea, ev = st.evac_a, st.evac_v
        load_chunks(n, source, base)

        tiles = [tiles_of[r] for r in ready if r in tiles_of]

        def run_pe(e):
            for sem, value in ready:
                if (sem, value) not in tiles_of:
                    e.wait_ge(sem, value)
            e.wait_ge(S["act_evac"], ea)
            if banks_of != "act":
                e.wait_ge(S["dve_evac"], ev)

            def one(c, u):
                slot = (base + u) % RING
                st.tiles = tiles[0] if tiles and u == 0 else None
                e.wait_ge(S["hi_ready"], base + c + 1)
                e.wait_ge(S["lo_ready"], RING + base + c + 1)
                if dve_chunk is not None and banks_of != "act":
                    e.wait_ge(S["dve_evac"], ev + c - 3)
                else:
                    e.wait_ge(S["act_evac"], ea + c - 3)
                pe_chunk(e, c, u, slot).then_inc(S["chunk_used"], 1)
            loop(e, n, one)
        pe.raw(run_pe)

        def splits(e, c, u, split):
            m = base + c + AHEAD
            if last and isinstance(c, int) and c + AHEAD >= n:
                return
            split(e, m, (base + u + AHEAD) % RING)

        def runner(split, chunk, waits, sem, evbase, links, chain):
            def run(e):
                def one(c, u):
                    splits(e, c, u, split)
                    if chunk is not None:
                        if isinstance(c, int) and c == 0:
                            for s_, v_ in waits:
                                e.wait_ge(s_, v_)
                        e.wait_ge(S["chunk_used"], RING + base + c + 1)
                        ch = Chain(e, chain[0], chain[1] + c * links)
                        chunk(e, c, u, ch).then_inc(sem, 1)
                        assert ch.k == links, (ch.k, links)
                if chunk is not None:
                    for s_, v_ in waits:
                        e.wait_ge(s_, v_)
                loop(e, n, one)
            return run
        act.raw(runner(hi_split, act_chunk, act_ready, S["act_evac"], ea, act_links,
                       (S["act_chain"], act.links)))
        dve.raw(runner(lo_split, dve_chunk, dve_ready, S["dve_evac"], ev, dve_links,
                       (S["dve_chain"], dve.links)))
        act.links += act_links * n
        dve.links += dve_links * n
        if act_chunk is not None:
            st.evac_a += n
        if dve_chunk is not None:
            st.evac_v += n
        st.n += n

    tiles_of = {}

    def wait_tile(e, k):
        if st.tiles is not None and (k == 0 or st.tiles[k] != st.tiles[k - 1]):
            e.wait_ge(*st.tiles[k])

    def cols(W, width=256, first=0):
        K = W.shape[0]
        v = W.rearrange("(k p) n -> p k n", p=P)
        k = K // P

        def source(c, slot):
            return [(slot[:, 0:k * width].rearrange("p (k n) -> p k n", k=k),
                     v[:, :, bass.ds(c * width + first, width)])]
        return source

    def fm_chunk(bh, bl, width=256, kts=KT):
        def chunk(e, c, u, slot):
            for f in range(width // P):
                dst = G[u][:, f * SEQ:(f + 1) * SEQ]
                for k in range(kts):
                    if f == 0:
                        wait_tile(e, k)
                    lo, hi_ = k * width + f * P, k * width + (f + 1) * P
                    e.matmul(dst, whi[slot][:, lo:hi_], bh[:, k, :], start=(k == 0), stop=False)
                    e.matmul(dst, whi[slot][:, lo:hi_], bl[:, k, :], start=False, stop=False)
                    ins = e.matmul(dst, wlo[slot][:, lo:hi_], bh[:, k, :], start=False,
                                   stop=(k == kts - 1))
            return ins
        return chunk

    def tm_chunk(bh, bl, width=256, kts=KT):
        def chunk(e, c, u, slot):
            for t in range(TT):
                dst = G[u][:, t * width:(t + 1) * width]
                for k in range(kts):
                    if t == 0:
                        wait_tile(e, k)
                    xs = slice(t * P, (t + 1) * P)
                    w0, w1 = whi[slot][:, k * width:(k + 1) * width], wlo[slot][:, k * width:(k + 1) * width]
                    e.matmul(dst, bh[:, k, xs], w0, start=(k == 0), stop=False)
                    e.matmul(dst, bh[:, k, xs], w1, start=False, stop=False)
                    ins = e.matmul(dst, bl[:, k, xs], w0, start=False, stop=(k == kts - 1))
            return ins
        return chunk

    def copy_fm(dst):
        flat = dst.rearrange("p k t -> p (k t)")
        return lambda e, c, u, ch: e.activation(flat[:, bass.ds(c * BANK, BANK)], G[u][:, :], ACT.Copy)

    def copy_tm(dst, width=256):
        return lambda e, c, u, ch: e.activation(
            dst[:, :, bass.ds(c * width, width)],
            G[u][:, 0:TT * width].rearrange("p (t n) -> p t n", t=TT), ACT.Copy)

    def add_tm(dst, width=256):
        def chunk(e, c, u, ch):
            d = dst[:, :, bass.ds(c * width, width)]
            return e.tensor_tensor(d, d, G[u][:, :].rearrange("p (t n) -> p t n", t=TT), ALU.add)
        return chunk

    VROWS = [("norm_mix", 16), ("norm_mem", 16), ("norm_memkv", 16), ("norm_ffn", 16),
             ("kv_norm", 8), ("conv_w", 24), ("g_mix_2", 8), ("g_ffn_2", 8), ("q_gain_2", 4),
             ("kv_gain_2", 2), ("dn_o_gain_2", 1), ("c_2", 8)]
    vat, r = {}, 0
    for n_, k_ in VROWS:
        vat[n_] = r
        r += k_
    V1 = r
    vrow = place("vrow", [P, 2, P], F32, offset=F0)

    def col(name, k=0):
        return vcol[:, vat[name] + k:vat[name] + k + 1]

    misc = nc.alloc_semaphore("vectors_in")
    x_in = nc.alloc_semaphore("x_in")
    pos_in = nc.alloc_semaphore("positions_in")

    pos_i = place("pos_i", [ROPE_2, 2, SEQ], I32, offset=sbuf_at["a_hi"])
    pos_f = place("pos_f", [ROPE_2, 2, SEQ], F32, offset=sbuf_at["a_hi"] + 2048)
    ang = place("ang", [ROPE_2, 8, SEQ], F32, offset=sbuf_at["a_hi"] + 4096)

    def load_x(e):
        e.dma_start(x[:, :, :], A["x"][0].rearrange("(t p) d -> p t d", p=P)).then_inc(x_in, 16)
    act.raw(load_x)

    def load_vectors(e):
        for n_, k_ in VROWS:
            src = A[n_]
            flat = src.rearrange(" ".join("abc"[:len(src.shape)]) + " -> (" + " ".join("abc"[:len(src.shape)]) + ")")
            e.dma_start(vrow[vat[n_]:vat[n_] + k_, 0, :], flat.rearrange("(k p) -> k p", p=P)).then_inc(misc, 16)
        w5 = A["conv_w_2"][0].rearrange("w (k p) -> (w k) p", p=P)
        e.dma_start(vrow[0:CONV2 * 24, 1, :], w5).then_inc(misc, 16)
        e.dma_start(invf[:, :], A["inv_freq"]).then_inc(pos_in, 16)
        for j, nm in enumerate(("positions", "positions_2")):
            e.dma_start(pos_i[:, j, :], A[nm].broadcast_to((ROPE_2, SEQ))).then_inc(pos_in, 16)
    act.raw(load_vectors)
    MISC = (misc, 16 * (len(VROWS) + 1))

    t_ones = pool.do(lambda e: e.memset(ones[:, :], 1.0))
    t_nh = pool.do(lambda e: e.memset(neg_half[:, :], -0.5))
    t = pool.do(lambda e: e.memset(eps[:, :], EPS))
    t_eps = pool.do(lambda e: e.memset(eps[:, 0:1], 128 * EPS), t)
    pool.do(lambda e: e.memset(ident[:, :], 0.0))
    pool.do(lambda e: e.memset(swap1[:, :], 0.0))
    t = pool.do(lambda e: e.memset(swap2[:, :], 0.0))
    t_id = pool.do(lambda e: e.affine_select(out=ident[:, :], in_=ident[:, :], compare_op=ALU.not_equal,
                                             fill=1.0, base=0, pattern=[[-1, P]], channel_multiplier=1), t)
    for sw, n_ in ((swap1, ROT), (swap2, ROPE_2)):
        t = pool.do(lambda e, sw=sw, n_=n_: e.affine_select(
            out=sw[:, :], in_=sw[:, :], compare_op=ALU.not_equal, fill=-1.0, base=-(n_ // 2),
            pattern=[[-1, n_]], channel_multiplier=1), t)
        t = pool.do(lambda e, sw=sw, n_=n_: e.affine_select(
            out=sw[:, :], in_=sw[:, :], compare_op=ALU.not_equal, fill=1.0, base=n_ // 2,
            pattern=[[-1, n_]], channel_multiplier=1), t)
    t_swap = t

    act.raw(lambda e: e.wait_ge(*t_nh))
    for n_ in range(4):
        act.raw(lambda e, n_=n_: e.activation(small[:, 160 + n_:161 + n_], neg_half[:, 0:1], ACT.Copy).then_inc(S["act_evac"], 1))
        act.raw(lambda e, n_=n_: e.activation(small[:, 164 + n_:165 + n_], neg_half[:, 0:1], ACT.Copy).then_inc(S["chunk_used"], 1))
        dve.raw(lambda e, n_=n_: e.memset(small[:, 168 + n_:169 + n_], 0.0).then_inc(S["dve_evac"], 1))
        dve.raw(lambda e, n_=n_: e.memset(small[:, 172 + n_:173 + n_], 0.0).then_inc(S["lo_ready"], 1))
    xfree = {0: None, 1: None, 2: None, 3: None}

    def w5col(w, k):
        return vcol[:, 128 + w * 24 + k:129 + w * 24 + k]

    slot_of = {"n": 0}

    def rstd_rows(src, ready, width):
        s0 = (slot_of["n"] % 8) * 8
        slot_of["n"] += 1
        ss, rs = small[:, s0:s0 + 2], small[:, s0 + 2:s0 + 4]
        a_ = dve.do(lambda e: e.tensor_tensor_reduce(
            out=xn[:, 0, 0:width], in0=src[:, 0, :], in1=src[:, 0, :], scale=1.0, scalar=0.0,
            op0=ALU.mult, op1=ALU.add, accum_out=ss[:, 0:1]), *ready)
        b_ = act.do(lambda e: e.activation(xn[:, 1, 0:width], src[:, 1, :], ACT.Square,
                                           accum_out=ss[:, 1:2]), *ready)
        t = dve.do(lambda e: e.tensor_scalar(rs, ss, 1.0 / width, EPS, ALU.mult, ALU.add), a_, b_)
        t = pool.do(lambda e: e.tensor_tensor(ss, rs, neg_half[:, 0:2], ALU.pow), t, t_nh)
        return ss, t

    def norm_rows(src, ready):
        rs, t = rstd_rows(src, ready, D)
        t0 = dve.do(lambda e: e.tensor_scalar(xn[:, 0, :], src[:, 0, :], rs[:, 0:1], None, ALU.mult), t)
        t1 = act.do(lambda e: e.activation(xn[:, 1, :], src[:, 1, :], ACT.Copy, scale=rs[:, 1:2]), t)
        return [t0, t1]

    def turn_rows(src, ready):
        toks = []
        for j in range(KT // 2):
            w = list(ready) + [t_id] + ([xfree[j]] if xfree[j] else [])
            for kk in range(2):
                for t_ in range(TT):
                    k = 2 * j + kk
                    tp = pe.do(lambda e, j=j, kk=kk, k=k, t_=t_: e.transpose(
                        X[j][:, kk * SEQ + t_ * P:kk * SEQ + (t_ + 1) * P],
                        src[:, t_, k * P:(k + 1) * P], ident[:, :]), *w)
                    w = []
            toks.append(tp)
        return toks

    def split_features(toks, gain, bias, free, also=()):
        tls = []
        for j in range(KT // 2):
            tp = toks[j]
            if bias is None:
                pair = [(2 * j + kk, X[j][:, kk * SEQ:(kk + 1) * SEQ]) for kk in range(2)]
                for k, xj in pair:
                    th = act.do(lambda e, k=k, xj=xj: e.activation(h_hi[:, k, :], xj, ACT.Copy, scale=gain(k)),
                                tp, *free)
                for k, xj in pair:
                    tl = dve.do(lambda e, k=k, xj=xj: e.scalar_tensor_tensor(
                        out=h_lo[:, k, :], in0=xj, scalar=gain(k), in1=h_hi[:, k, :].bitcast(F32),
                        op0=ALU.mult, op1=ALU.subtract), th)
                xfree[j] = tl
                tls += [tl, tl]
                continue
            xt = ht_f[:, j % 2, :, :]
            war = [tls[2 * j - 4]] if j >= 2 else []
            for kk in range(2):
                k = 2 * j + kk
                te = dve.do(lambda e, j=j, kk=kk, k=k, xt=xt: e.tensor_scalar(
                    xt[:, kk, :], X[j][:, kk * SEQ:(kk + 1) * SEQ], gain(k), bias(k), ALU.mult, ALU.add), tp, *also, *war)
            xfree[j] = te
            th = act.do(lambda e, j=j, xt=xt: e.activation(h_hi[:, 2 * j:2 * j + 2, :], xt, ACT.Copy), te, *free)
            tl = dve.do(lambda e, j=j, xt=xt: e.tensor_tensor(
                h_lo[:, 2 * j:2 * j + 2, :], xt, h_hi[:, 2 * j:2 * j + 2, :].bitcast(F32), ALU.subtract), th)
            tls += [tl, tl]
        tiles_of[tls[-1]] = tls
        return tls[-1]

    def norm_to_features(src, ready, gain, bias, free):
        return split_features(turn_rows(xn, norm_rows(src, ready)), gain, bias, free)

    def attention(heads, kts, scale, score, v, pbuf, ptbuf, ready, causal=None, free=(), dh=None):
        t_soft, t_pt, t_pv = {}, {}, {}
        sc0 = 64

        def scores(h):
            b = h % 2
            w = list(ready) + ([xfree[b]] if xfree[b] else []) + ([t_soft[h - 2]] if h >= 2 else [])
            tok = None
            for t_ in range(TT):
                tok = pe.do(lambda e, h=h, t_=t_, b=b: score(e, h, t_, X[b][:, t_ * SEQ:(t_ + 1) * SEQ]), *w)
                w = []
            return tok

        def softmax(h, ts):
            b = h % 2
            o = sc0 + b * 16
            mx, nb, den, rd = (small[:, o + 2 * q:o + 2 * q + 2] for q in range(4))
            s3 = X[b][:, :].rearrange("p (t m) -> p t m", t=TT)
            p3 = pbuf[b]
            wfree = [t_pt[h - 2]] if h >= 2 else []
            if causal is not None:
                tm = dve.do(lambda e: e.tensor_tensor(p3[:, :, :], s3, causal[:, :, :], ALU.add), ts, *wfree, *ready)
                src = p3[:, :, :]
                soft_free = tm
            else:
                tm = ts
                src = s3
            t = dve.do(lambda e: e.tensor_reduce(mx, src, AX_X, ALU.max), tm)
            t = dve.do(lambda e: e.tensor_scalar(nb, mx, -scale, None, ALU.mult), t)
            for t_ in range(TT):
                te = act.do(lambda e, t_=t_: e.activation(
                    p3[:, t_, :], src[:, t_, :], ACT.Exp, bias=nb[:, t_:t_ + 1], scale=scale,
                    accum_out=den[:, t_:t_ + 1]), t, *wfree)
            t_soft[h] = te
            t = dve.do(lambda e: e.reciprocal(rd, den), te)
            for t_ in range(TT):
                t2 = dve.do(lambda e, t_=t_: e.tensor_scalar(p3[:, t_, :], p3[:, t_, :], rd[:, t_:t_ + 1],
                                                             None, ALU.mult), t)
            return t2

        def turn(h, tp):
            b = h % 2
            w = [tp] + ([xfree[2]] if xfree[2] else []) + [t_id]
            for m in range(2):
                for t_ in range(TT):
                    tok = pe.do(lambda e, m=m, t_=t_, b=b: e.transpose(
                        X[2][:, m * SEQ + t_ * P:m * SEQ + (t_ + 1) * P],
                        pbuf[b][:, t_, m * P:(m + 1) * P], ident[:, :]), *w)
                    w = []
            t_pt[h] = tok
            w = [t_pv[h - 1]] if h >= 1 else []
            tc = act.do(lambda e: e.activation(ptbuf[:, :, :], X[2][:, :].rearrange("p (m q) -> p m q", m=2),
                                               ACT.Copy), tok, *w)
            xfree[2] = tc
            return tc

        def values(h, tc):
            w = [tc] + ([xfree[3]] if xfree[3] else [])
            for d in range(kts):
                for m in range(2):
                    f0 = (h * kts + d) * P
                    tok = pe.do(lambda e, d=d, m=m, f0=f0: e.matmul(
                        X[3][:, d * SEQ:(d + 1) * SEQ], v[:, m, f0:f0 + P], ptbuf[:, m, :],
                        start=(m == 0), stop=(m == 1)), *w)
                    w = []
            t_pv[h] = tok
            o3 = X[3][:, 0:kts * SEQ].rearrange("p (d q) -> p d q", d=kts)
            th = act.do(lambda e: e.activation(a_hi[:, h * kts:(h + 1) * kts, :], o3, ACT.Copy), tok, *free)
            tl = dve.do(lambda e: e.tensor_tensor(a_lo[:, h * kts:(h + 1) * kts, :], o3,
                                                  a_hi[:, h * kts:(h + 1) * kts, :].bitcast(F32),
                                                  ALU.subtract), th, *free)
            xfree[3] = tl
            return tl

        tls = []
        ts = scores(0)
        tp = softmax(0, ts)
        for h in range(heads):
            if h + 1 < heads:
                ts = scores(h + 1)
            tc = turn(h, tp)
            if h + 1 < heads:
                tp = softmax(h + 1, ts)
            tl = values(h, tc)
            tls += [tl] * kts
        tiles_of[tl] = tls
        xfree[0] = xfree[1] = t_soft[heads - 1]
        return tl

    xn_rope = place("xn_rope", [P, KT, SEQ], F32, offset=sbuf_at["xn"])
    qT = place("qT", [P, KT, SEQ], F32, offset=F0)
    kT = place("kT", [P, KT, SEQ], F32, offset=F0 + 8192)
    vv = place("vv", [P, TT, D], F32, offset=F0 + 16384)
    mem = place("mem", [P, TT, D], F32, offset=F0 + 24640)
    pb0 = place("pb0", [P, TT, SEQ], F32, offset=F0 + 32832)
    pb1 = place("pb1", [P, TT, SEQ], F32, offset=F0 + 34880)
    ptb = place("ptb", [P, 2, SEQ], F32, offset=F0 + 38976)
    ht_f = place("ht_f", [P, 2, 2, SEQ], F32, offset=F0 + 38976)
    bc_flat = place("bc_flat", [P, 2 * KT * SEQ], F32, offset=F0)
    bT = bc_flat[:, 0:KT * SEQ].rearrange("p (k t) -> p k t", k=KT)
    cT = bc_flat[:, KT * SEQ:2 * KT * SEQ].rearrange("p (k t) -> p k t", k=KT)
    PADZ = SEQ + CONV1 - 1
    zT = place("zT", [P, KT, PADZ], F32, offset=F0 + 16384)
    causal = place("causal", [P, TT, SEQ], F32, offset=F0 + 36928)
    silu_g = place("silu_g", [P, 2, SEQ], F32, offset=F0)
    prod_g = place("prod_g", [P, 2, SEQ], F32, offset=F0 + 2048)

    mem_in = nc.alloc_semaphore("mem_in")

    def load_mem(e):
        e.dma_start(mem[:, :, :], A["mem"][0].rearrange("(t p) d -> p t d", p=P)).then_inc(mem_in, 16)
    act.raw(load_mem)

    t = pool.do(lambda e: e.memset(causal[:, :, :], 0.0))
    for t_ in range(TT):
        t = pool.do(lambda e, t_=t_: e.affine_select(
            out=causal[:, t_, :], in_=causal[:, t_, :], compare_op=ALU.is_ge, fill=-1e30,
            base=t_ * P, pattern=[[-1, SEQ]], channel_multiplier=1), t)
    t_causal = t

    turned = turn_rows(xn, norm_rows(x, [(x_in, 16)]))
    first_splits()

    pe.do(lambda e: e.transpose(G[3][:, 0:V1], vrow[0:V1, 0, :], ident[0:V1, 0:V1]), MISC, t_id)
    t = pe.do(lambda e: e.transpose(G[3][:, 128:128 + 120], vrow[0:120, 1, :], ident[0:120, 0:120]))
    dve.do(lambda e: e.tensor_copy(vcol[:, 0:V1], G[3][:, 0:V1]), t)
    t_vcol = dve.do(lambda e: e.tensor_copy(vcol[:, 128:248], G[3][:, 128:248]))
    th = split_features(turned, lambda k: col("norm_mix", k), None, [t_vcol])
    t = t_swap
    for j in range(2):
        tp_ = pool.do(lambda e, j=j: e.tensor_copy(pos_f[:, j, :], pos_i[:, j, :]), (pos_in, 48))
        t = pool.do(lambda e, j=j: e.tensor_scalar(ang[:, 0, :], pos_f[:, j, :], invf[:, j:j + 1], None, ALU.mult), tp_, t)
        for q, shift in ((0, 0.25), (1, 0.0)):
            t = pool.do(lambda e, s_=shift: e.tensor_scalar(ang[:, 1, :], ang[:, 0, :], 1.0 / TWO_PI, s_, ALU.mult, ALU.add), t)
            t = pool.do(lambda e: e.tensor_scalar(ang[:, 2, :], ang[:, 1, :], ROUND, None, ALU.add), t)
            t = pool.do(lambda e: e.tensor_scalar(ang[:, 1, :], ang[:, 2, :], -ROUND, None, ALU.add), t)
            for part, (a_, b_) in zip((TP1, TP2, TP3), ((0, 2), (2, 3), (3, 2))):
                t = pool.do(lambda e, p_=part, b_=b_: e.tensor_scalar(ang[:, b_, :], ang[:, 1, :], -p_, None, ALU.mult), t)
                t = pool.do(lambda e, a_=a_, b_=b_: e.tensor_tensor(ang[:, b_, :], ang[:, b_, :], ang[:, a_, :], ALU.add), t)
            t = pool.do(lambda e, s_=shift: e.tensor_scalar(ang[:, 3, :], ang[:, 2, :], s_ * TWO_PI, 3.1415925, ALU.add, ALU.min), t)
            t = pool.do(lambda e, j=j, q=q: e.tensor_scalar(ang[:, 4 + 2 * j + q, :], ang[:, 3, :], -3.1415925, None, ALU.max), t)
    t_ang = t

    t_z0 = pool.do(lambda e: e.memset(zT[:, :, 0:CONV1 - 1], 0.0))

    W = A["conv_w_in"][0]
    gemm(8, cols(W), fm_chunk(h_hi, h_lo), act_chunk=lambda e, c, u, ch: e.activation(
        bc_flat[:, bass.ds(c * BANK, BANK)], G[u][:, :], ACT.Copy), ready=[th])
    t_bc = act_evacs()
    for j, (tab, n_) in enumerate(((rope1, ROT), (rope2, ROPE_2))):
        for q in range(2):
            t_rope = act.do(lambda e, j=j, q=q, tab=tab, n_=n_: e.activation(tab[:, q, :], ang[0:n_, 4 + 2 * j + q, :], ACT.Sin), t_ang)
    mem_rows = norm_rows(mem, [(mem_in, 16), th])

    def conv_chunk(e, c, u, ch):
        k0 = 2 * c
        z2 = zT[:, k0:k0 + 2, CONV1 - 1:PADZ]
        ch.link(e.tensor_tensor(z2, G[u][:, :].rearrange("p (k t) -> p k t", k=2), cT[:, k0:k0 + 2, :], ALU.mult))
        for w in range(CONV1):
            for k in (k0, k0 + 1):
                y = cT[:, k, :]
                wc = vcol[:, vat["conv_w"] + w * KT + k:vat["conv_w"] + w * KT + k + 1]
                if w == 0:
                    ins = e.tensor_scalar(y, zT[:, k, 0:SEQ], wc, None, ALU.mult)
                else:
                    ins = e.scalar_tensor_tensor(out=y, in0=zT[:, k, w:w + SEQ], scalar=wc, in1=y,
                                                 op0=ALU.mult, op1=ALU.add)
                ch.link_but_one(ins, last=(w, k) == (CONV1 - 1, k0 + 1))
        y2 = cT[:, k0:k0 + 2, :]
        ch.link(e.tensor_tensor(y2, y2, bT[:, k0:k0 + 2, :], ALU.mult))
        ch.link(e.tensor_copy(a_hi[:, k0:k0 + 2, :], y2))
        return e.tensor_tensor(a_lo[:, k0:k0 + 2, :], y2, a_hi[:, k0:k0 + 2, :].bitcast(F32), ALU.subtract)

    ev0 = st.evac_v
    gemm(4, cols(W, first=2 * D), fm_chunk(h_hi, h_lo), dve_chunk=conv_chunk, dve_links=9,
         dve_ready=[t_bc, t_z0, t_rope])
    t_conv_out = dve_evacs()
    tiles_of[t_conv_out] = [(S["dve_evac"], ev0 + k // 2 + 1) for k in range(KT)]
    t_memkv = split_features(turn_rows(xn, mem_rows), lambda k: col("norm_memkv", k), None, [all_used()])
    gemm(4, cols(A["conv_w_out"][0]), tm_chunk(a_hi, a_lo), dve_chunk=add_tm(x), ready=[t_conv_out])

    def mem_attention(l, x_ready, tm_, last=False):
        W = A["mem_w_kv"][l]
        gemm(4, cols(W), fm_chunk(h_hi, h_lo), act_chunk=copy_fm(kT), ready=[tm_],
             act_ready=[x_ready])
        gemm(4, cols(W, first=D), tm_chunk(h_hi, h_lo), act_chunk=copy_tm(vv))
        tx = norm_to_features(x, [x_ready], lambda k: col("norm_mem", 8 * l + k), None, [all_used()])
        gemm(4, cols(A["mem_w_q"][l]), fm_chunk(h_hi, h_lo), act_chunk=copy_fm(qT), ready=[tx])

        def score(e, h, t_, dst):
            for k in (2 * h, 2 * h + 1):
                ins = e.matmul(dst, qT[:, k, t_ * P:(t_ + 1) * P], kT[:, k, :], start=(k == 2 * h), stop=(k == 2 * h + 1))
            return ins
        to = attention(4, 2, 256 ** -0.5, score, vv, (pb0, pb1), ptb, [act_evacs(), dve_evacs()], free=[all_used()])
        gemm(4, cols(A["mem_w_o"][l]), tm_chunk(a_hi, a_lo), dve_chunk=add_tm(x), ready=[to], last=last)

    def ffn(l, last=False, between=None):
        tx = norm_to_features(x, [dve_evacs()], lambda k: col("norm_ffn", 8 * l + k), None, [all_used()])
        W = A["ffn_w_gu"][l].rearrange("(k p) (h n) -> p k h n", p=P, h=2)

        def source(c, slot):
            dst = slot[:, :].rearrange("p (k h n) -> p k h n", k=KT, h=2)
            return [(dst[:, :, h, :], W[:, :, h, bass.ds(c * P, P)]) for h in range(2)]
        ta = act_evacs()

        def act_silu(e, c, u, ch):
            e.wait_ge(S["dve_evac"], ev0 + c - 1)
            return e.activation(silu_g[:, u % 2, :], G[u][:, 0:SEQ], ACT.Silu)
        ea0, ev0 = st.evac_a, st.evac_v

        def dve_gate(e, c, u, ch):
            e.wait_ge(S["act_evac"], ea0 + c + 1)
            pr = prod_g[:, u % 2, :]
            ch.link(e.tensor_tensor(pr, silu_g[:, u % 2, :], G[u][:, SEQ:2 * SEQ], ALU.mult))
            ch.link(e.tensor_copy(a_hi[:, bass.ds(c, 1), :], pr.rearrange("p (a t) -> p a t", a=1)))
            return e.tensor_tensor(a_lo[:, bass.ds(c, 1), :], pr.rearrange("p (a t) -> p a t", a=1),
                                   a_hi[:, bass.ds(c, 1), :].bitcast(F32), ALU.subtract)
        gemm(FT, source, fm_chunk(h_hi, h_lo), act_chunk=act_silu, dve_chunk=dve_gate, dve_links=2,
             ready=[tx], act_ready=[tx], dve_ready=[tx])
        Wd = A["ffn_w_down"][l].rearrange("(c k p) n -> p c k n", p=P, k=2)

        def down_source(c, slot):
            return [(slot[:, :].rearrange("p (k n) -> p k n", k=2), Wd[:, bass.ds(c, 1), :, :].rearrange("p a k n -> p (a k) n"))]

        n = FT // 2
        extra = between([tx, all_used()]) if between else None
        down(n, down_source, last)
        for t_ in range(TT):
            for hf in range(2):
                b = 2 * t_ + hf
                xs = x[:, t_, hf * BANK:(hf + 1) * BANK]
                tok = dve.do(lambda e, b=b, xs=xs: e.tensor_tensor(xs, xs, G[b][:, :], ALU.add), all_used())
        return (tok, extra) if between else tok

    def down(n, source, last):
        def chunk(e, c, u, slot):
            for kk in range(2):
                k = 2 * c + kk
                for t_ in range(TT):
                    for hf in range(2):
                        dst = G[2 * t_ + hf][:, :]
                        w0 = whi[slot][:, kk * D + hf * BANK:kk * D + (hf + 1) * BANK]
                        w1 = wlo[slot][:, kk * D + hf * BANK:kk * D + (hf + 1) * BANK]
                        xh, xl = a_hi[:, k, t_ * P:(t_ + 1) * P], a_lo[:, k, t_ * P:(t_ + 1) * P]
                        e.matmul(dst, xh, w0, start=(k == 0), stop=False)
                        e.matmul(dst, xh, w1, start=False, stop=False)
                        ins = e.matmul(dst, xl, w0, start=False, stop=(k == 2 * n - 1))
            return ins
        base = st.n
        gemm_straight(n, source, chunk, last=last)

    def gemm_straight(n, source, chunk, ready=(), last=False):
        base = st.n
        ea, ev = st.evac_a, st.evac_v
        load_chunks(n, source, base)

        def run_pe(e):
            for sem, value in ready:
                e.wait_ge(sem, value)
            e.wait_ge(S["act_evac"], ea)
            e.wait_ge(S["dve_evac"], ev)
            for c in range(n):
                e.wait_ge(S["hi_ready"], base + c + 1)
                e.wait_ge(S["lo_ready"], RING + base + c + 1)
                chunk(e, c, c % RING, (base + c) % RING).then_inc(S["chunk_used"], 1)
        pe.raw(run_pe)

        def ahead(split):
            def run(e):
                loop(e, n - AHEAD * last, lambda c, u: split(e, base + c + AHEAD, (base + u + AHEAD) % RING))
            return run
        act.raw(ahead(hi_split))
        dve.raw(ahead(lo_split))
        st.n += n

    def rope_fm(buf, tiles, tab, swap, rows, ready, tmp):
        n = (tiles + 1) // 2
        f = buf[0:rows, :, :].rearrange("p k t -> p (k t)")
        tf = tmp[0:rows, :, :].rearrange("p k t -> p (k t)")
        for j in range(n):
            kk = min(2, tiles - 2 * j)
            w = list(ready) + ([xfree[j % 4]] if xfree[j % 4] else [])
            cs = slice(j * BANK, j * BANK + kk * SEQ)
            tp = pe.do(lambda e, j=j, cs=cs, kk=kk: e.matmul(X[j % 4][0:rows, 0:kk * SEQ], swap[:, :], f[:, cs],
                                                             start=True, stop=True), *w, t_swap)
            td = dve.do(lambda e, j=j, cs=cs, kk=kk: e.tensor_tensor(
                tf[:, cs].rearrange("p (k t) -> p k t", k=kk),
                X[j % 4][0:rows, 0:kk * SEQ].rearrange("p (k t) -> p k t", k=kk),
                tab[:, 1:2, :].broadcast_to((rows, kk, SEQ)), ALU.mult), tp, t_rope, *ready)
            xfree[j % 4] = td
        b3 = buf[0:rows, 0:tiles, :]
        t = dve.do(lambda e: e.tensor_tensor(b3, b3, tab[:, 0:1, :].broadcast_to((rows, tiles, SEQ)), ALU.mult), td, tp)
        return dve.do(lambda e: e.tensor_tensor(b3, b3, tmp[0:rows, 0:tiles, :], ALU.add), t)

    mem_attention(0, dve_evacs(), t_memkv)
    tx = ffn(0)
    th = norm_to_features(x, [tx], lambda k: col("kv_norm", k), None, [all_used()])
    gemm(4, cols(A["w_kv"]), fm_chunk(h_hi, h_lo), act_chunk=copy_fm(kT), ready=[th])
    t1 = rope_fm(kT, KT, rope1, swap1, ROT, [act_evacs(), th], xn_rope)
    gemm(4, cols(A["w_kv"], first=D), tm_chunk(h_hi, h_lo), act_chunk=copy_tm(vv))
    th = norm_to_features(x, [tx, t1], lambda k: col("norm_mix", 8 + k), None, [all_used()])
    gemm(4, cols(A["moba_w_q"][0]), fm_chunk(h_hi, h_lo), act_chunk=copy_fm(qT), ready=[th])
    t1 = rope_fm(qT, KT, rope1, swap1, ROT, [act_evacs(), t1, th], xn_rope)

    t_memkv = norm_to_features(mem, [(mem_in, 16), t1], lambda k: col("norm_memkv", 8 + k), None, [all_used()])

    def score1(e, h, t_, dst):
        return e.matmul(dst, qT[:, h, t_ * P:(t_ + 1) * P], kT[:, h, :], start=True, stop=True)
    to = attention(8, 1, 128 ** -0.5, score1, vv, (pb0, pb1), ptb, [act_evacs(), t1, t_causal],
                   causal=causal, free=[all_used()])
    gemm(4, cols(A["moba_w_o"][0]), tm_chunk(a_hi, a_lo), dve_chunk=add_tm(x), ready=[to])
    mem_attention(1, dve_evacs(), t_memkv)
    A0 = sbuf_at["a_hi"]
    XN = sbuf_at["xn"]
    mem_done = [all_used(), dve_evacs(), act_evacs()]
    gt = place("gt", [P, 2, D], F32, offset=F0)
    mod = place("mod", [P, 6, D], F32, offset=F0 + 8192)
    gfin = place("gfin", [P, D], F32, offset=F0 + 36928)
    KEEP = F0 + 43072
    mcol = place("mcol", [P, 4, KT], F32, offset=KEEP)
    dtb = place("dtb", [P, 2, 16], F32, offset=KEEP + 128)

    mod_in, gfin_in = nc.alloc_semaphore("mod_in"), nc.alloc_semaphore("gfin_in")

    def load_late(e):
        for w in mem_done:
            e.wait_ge(*w)
        e.dma_start(mod[:, :, :].rearrange("p v d -> p (v d)"),
                    A["b_mod_2"].broadcast_to((P, 6 * D))).then_inc(mod_in, 16)
        e.dma_start(gfin[:, :], A["norm_final"].rearrange("(a d) -> a d", a=1).broadcast_to((P, D))).then_inc(gfin_in, 16)
        for j, nm in enumerate(("a_log_2", "dt_bias_2")):
            e.dma_start(dtb[:, j, :], A[nm].rearrange("a b c -> a (b c)").broadcast_to((P, 16))).then_inc(gfin_in, 16)
    act.raw(load_late)

    def modulation_operand(after):
        csil = place("csil", [P, KT], F32, offset=KEEP + 256)
        cb = place("cb", [P, KT, P], F32, offset=XN)
        t = act.do(lambda e: e.activation(csil[:, :], vcol[:, vat["c_2"]:vat["c_2"] + KT], ACT.Silu), t_vcol)
        for k in range(KT):
            t2 = dve.do(lambda e, k=k: e.tensor_scalar(cb[:, k, :], ones[:, :], csil[:, k:k + 1], None, ALU.mult), t, t_ones, *after)
        t3 = act.do(lambda e: e.activation(h_hi[:, :, 0:P], cb[:, :, :], ACT.Copy), t2, all_used())
        t4 = dve.do(lambda e: e.tensor_tensor(h_lo[:, :, 0:P], cb[:, :, :], h_hi[:, :, 0:P].bitcast(F32), ALU.subtract), t3)
        return t4

    tx, t4 = ffn(1, between=modulation_operand)

    C_Z, C_B, C_CQ, C_CKV, C_KR, C_G = 3072, 4096, 4128, 4640, 4896, 4960

    def mod_chunk(e, c, u, slot):
        for k in range(KT):
            w0, w1 = whi[slot][:, k * 256:(k + 1) * 256], wlo[slot][:, k * 256:(k + 1) * 256]
            e.matmul(G[u][:, 0:256], h_hi[:, k, 0:P], w0, start=(k == 0), stop=False)
            e.matmul(G[u][:, 0:256], h_hi[:, k, 0:P], w1, start=False, stop=False)
            ins = e.matmul(G[u][:, 0:256], h_lo[:, k, 0:P], w0, start=False, stop=(k == KT - 1))
        return ins
    mflat = mod[:, :, :].rearrange("p v d -> p (v d)")

    def modulation(n, first):
        gemm(n, cols(A["w_mod_2"][0], first=first * 256), mod_chunk, ready=[t4, tx], dve_ready=[(mod_in, 16)],
             dve_chunk=lambda e, c, u, ch: e.tensor_tensor(
                 mflat[:, bass.ds(c * 256 + first * 256, 256)], mflat[:, bass.ds(c * 256 + first * 256, 256)],
                 G[u][:, 0:256], ALU.add))

    modulation(3, 0)
    rs, t = rstd_rows(x, [tx, t4], D)
    for t_ in range(TT):
        t_x0 = dve.do(lambda e, t_=t_, rs=rs: e.scalar_tensor_tensor(
            out=x[:, t_, :], in0=x[:, t_, :], scalar=rs[:, t_:t_ + 1], in1=gfin[:, :],
            op0=ALU.mult, op1=ALU.mult), t, (gfin_in, 48))
    turned = turn_rows(xn, norm_rows(x, [t_x0, t4]))
    modulation(5, 3)
    t_mod = dve_evacs()
    dg = place("dg", [P, KT, P], F32, offset=XN + 4096)
    def columns(j, v_, gain, after):
        t = dve.do(lambda e: e.tensor_tensor(
            dg[:, :, :], mod[:, v_, :].rearrange("p (k q) -> p k q", k=KT),
            ident[:, :].rearrange("p (a q) -> p a q", a=1).broadcast_to((P, KT, P)), ALU.mult), t_mod, t_id, *after)
        t = dve.do(lambda e: e.tensor_reduce(mcol[:, j, :], dg[:, :, :], AX_X, ALU.add), t)
        if gain:
            t = dve.do(lambda e: e.scalar_tensor_tensor(
                out=mcol[:, j, :], in0=mcol[:, j, :], scalar=1.0, in1=vcol[:, vat[gain]:vat[gain] + KT],
                op0=ALU.add, op1=ALU.mult), t)
        return t
    tcol = columns(0, 0, None, turned)
    tcol = columns(1, 1, "g_mix_2", [tcol])
    modulation(16, 8)
    t_mod = dve_evacs()
    th = split_features(turned, lambda k: mcol[:, 1, k:k + 1], lambda k: mcol[:, 0, k:k + 1], [all_used()], also=[tcol])
    tcol = columns(2, 3, None, [tcol])
    tcol = columns(3, 4, "g_ffn_2", [tcol])
    tg = dve.do(lambda e: e.tensor_copy(gt[:, 0, :], mod[:, 2, :]), t_mod)
    tg = dve.do(lambda e: e.tensor_copy(gt[:, 1, :], mod[:, 5, :]), t_mod)

    Win = A["w_in_2"][0]
    qn = place("qn", [P, 8, SEQ], F32, offset=F0 + 8192)
    kn = place("kn", [P, 8, SEQ], F32, offset=F0 + 16384)
    vm = place("vm", [P, TT, D], F32, offset=F0 + 24576)
    AU = 14 * SEQ * 4
    lat = place("lat", [P, 6, SEQ], F32, offset=A0 + AU)
    krr = place("krr", [ROPE_2, 1, SEQ], F32, offset=A0 + AU + 6144)
    qr = place("qr", [ROPE_2, 8, SEQ], F32, offset=sbuf_at["a_lo"] + AU)
    ab = place("ab", [P, TT, 32], F32, offset=KEEP + 288)

    gemm(3, cols(Win, first=C_CQ), fm_chunk(h_hi, h_lo), act_chunk=copy_fm(lat[:, :, :]), ready=[th], act_ready=[th])

    def kr_source(c, slot):
        v = Win.rearrange("(k p) n -> p k n", p=P)
        dst = slot[:, 0:KT * 96].rearrange("p (k n) -> p k n", k=KT)
        return [(dst[:, :, 0:64], v[:, :, C_KR:C_KR + 64]), (dst[:, :, 64:96], v[:, :, C_B:C_B + 32])]

    def kr_chunk(e, c, u, slot):
        for k in range(KT):
            w0, w1 = whi[slot][:, k * 96:k * 96 + 64], wlo[slot][:, k * 96:k * 96 + 64]
            e.matmul(G[u][0:64, 0:SEQ], w0, h_hi[:, k, :], start=(k == 0), stop=False)
            e.matmul(G[u][0:64, 0:SEQ], w0, h_lo[:, k, :], start=False, stop=False)
            e.matmul(G[u][0:64, 0:SEQ], w1, h_hi[:, k, :], start=False, stop=(k == KT - 1))
        for t_ in range(TT):
            for k in range(KT):
                w0, w1 = whi[slot][:, k * 96 + 64:k * 96 + 96], wlo[slot][:, k * 96 + 64:k * 96 + 96]
                xs = slice(t_ * P, (t_ + 1) * P)
                d_ = G[u][:, SEQ + t_ * 32:SEQ + t_ * 32 + 32]
                e.matmul(d_, h_hi[:, k, xs], w0, start=(k == 0), stop=False)
                e.matmul(d_, h_hi[:, k, xs], w1, start=False, stop=False)
                ins = e.matmul(d_, h_lo[:, k, xs], w0, start=False, stop=(k == KT - 1))
        return ins

    def kr_evac(e, c, u, ch):
        e.activation(krr[:, 0, :], G[u][0:64, 0:SEQ], ACT.Copy)
        return e.activation(ab[:, :, :], G[u][:, SEQ:SEQ + 64].rearrange("p (t n) -> p t n", t=TT), ACT.Copy)
    gemm(1, kr_source, kr_chunk, act_chunk=kr_evac)
    t_lat = act_evacs()

    sq = place("sq", [P, 6, SEQ], F32, offset=XN)
    rl = place("rl", [P, 2, SEQ], F32, offset=XN + 6144)
    t = act.do(lambda e: e.activation(sq[:, :, :], lat[:, :, :], ACT.Square), t_lat, th)
    for j, (k0, k1) in enumerate(((0, 4), (4, 6))):
        for k in range(k0, k1):
            tp = pe.do(lambda e, j=j, k=k, k0=k0, k1=k1: e.matmul(X[j][:, 0:SEQ], ones[:, :], sq[:, k, :],
                                                                  start=(k == k0), stop=(k == k1 - 1)), t, xfree[j])
        t2 = dve.do(lambda e, j=j, n_=(k1 - k0) * P: e.tensor_scalar(rl[:, j, :], X[j][:, 0:SEQ], 1.0 / n_, EPS, ALU.mult, ALU.add), tp, th)
        xfree[j] = t2
        t3 = act.do(lambda e, j=j: e.activation(rl[:, j, :], rl[:, j, :], ACT.Sqrt), t2)
        t3 = dve.do(lambda e, j=j: e.reciprocal(rl[:, j, :], rl[:, j, :]), t3)
        for k in range(k0, k1):
            g_ = col("q_gain_2", k) if j == 0 else col("kv_gain_2", k - 4)
            t4 = dve.do(lambda e, j=j, k=k, g_=g_: e.scalar_tensor_tensor(
                out=lat[:, k, :], in0=lat[:, k, :], scalar=g_, in1=rl[:, j, :], op0=ALU.mult, op1=ALU.mult), t3)
    t5 = act.do(lambda e: e.activation(a_hi[:, 8:14, :], lat[:, :, :], ACT.Copy), t4)
    t_l = dve.do(lambda e: e.tensor_tensor(a_lo[:, 8:14, :], lat[:, :, :], a_hi[:, 8:14, :].bitcast(F32), ALU.subtract), t5)

    def uq_chunk(e, c, u, slot):
        if c == 0:
            for b in range(4):
                e.wait_ge(*xfree_at[b])
        if c >= 2:
            e.wait_ge(S["act_evac"], ea_uq + c - 1)
        for hh in range(2):
            for (m, o, dst) in ((P, 0, G[u][:, hh * SEQ:(hh + 1) * SEQ]),
                                (64, P, X[c % 2][0:64, hh * SEQ:(hh + 1) * SEQ])):
                for k in range(4):
                    a_ = k * 384 + hh * 192 + o
                    w0, w1 = whi[slot][:, a_:a_ + m], wlo[slot][:, a_:a_ + m]
                    e.matmul(dst, w0, a_hi[:, 8 + k, :], start=(k == 0), stop=False)
                    e.matmul(dst, w0, a_lo[:, 8 + k, :], start=False, stop=False)
                    ins = e.matmul(dst, w1, a_hi[:, 8 + k, :], start=False, stop=(k == 3))
        return ins

    def uq_evac(e, c, u, ch):
        e.activation(qn[:, 2 * c:2 * c + 2, :], G[u][:, :].rearrange("p (h t) -> p h t", h=2), ACT.Copy)
        return e.activation(qr[:, 2 * c:2 * c + 2, :], X[c % 2][0:64, :].rearrange("p (h t) -> p h t", h=2), ACT.Copy)
    xfree_at = dict(xfree)
    ea_uq = st.evac_a
    gemm(4, cols(A["w_uq_2"][0], width=384), uq_chunk, act_chunk=uq_evac, ready=[t_l], act_ready=[t_l])

    def ukv_chunk(e, c, u, slot):
        e.wait_ge(S["act_evac"], ea_kv + max(0, c - 3))
        for hh in range(2):
            dst = G[u][:, hh * SEQ:(hh + 1) * SEQ]
            for k in range(2):
                a_ = k * BANK + hh * 256
                w0, w1 = whi[slot][:, a_:a_ + P], wlo[slot][:, a_:a_ + P]
                e.matmul(dst, w0, a_hi[:, 12 + k, :], start=(k == 0), stop=False)
                e.matmul(dst, w0, a_lo[:, 12 + k, :], start=False, stop=False)
                e.matmul(dst, w1, a_hi[:, 12 + k, :], start=False, stop=(k == 1))
        for t_ in range(TT):
            for hh in range(2):
                dst = X[u][:, t_ * 256 + hh * P:t_ * 256 + (hh + 1) * P]
                for k in range(2):
                    a_ = k * BANK + hh * 256 + P
                    w0, w1 = whi[slot][:, a_:a_ + P], wlo[slot][:, a_:a_ + P]
                    xs = slice(t_ * P, (t_ + 1) * P)
                    e.matmul(dst, a_hi[:, 12 + k, xs], w0, start=(k == 0), stop=False)
                    e.matmul(dst, a_hi[:, 12 + k, xs], w1, start=False, stop=False)
                    ins = e.matmul(dst, a_lo[:, 12 + k, xs], w0, start=False, stop=(k == 1))
        return ins

    def ukv_evac(e, c, u, ch):
        e.activation(kn[:, 2 * c:2 * c + 2, :], G[u][:, :].rearrange("p (h t) -> p h t", h=2), ACT.Copy)
        return e.activation(vm[:, :, c * 256:(c + 1) * 256], X[u][:, :].rearrange("p (t n) -> p t n", t=TT), ACT.Copy)
    ea_kv = st.evac_a
    gemm(4, cols(A["w_ukv_2"][0], width=512), ukv_chunk, act_chunk=ukv_evac)
    for b in range(4):
        xfree[b] = act_evacs()
    t1 = rope_fm(qr, 8, rope2, swap2, ROPE_2, [act_evacs()], xn_rope)
    t1 = rope_fm(krr, 1, rope2, swap2, ROPE_2, [act_evacs(), t1], xn_rope)

    def score2(e, h, t_, dst):
        e.matmul(dst, qn[:, h, t_ * P:(t_ + 1) * P], kn[:, h, :], start=True, stop=False)
        return e.matmul(dst, qr[:, h, t_ * P:(t_ + 1) * P], krr[:, 0, :], start=False, stop=True)
    to = attention(8, 1, 192 ** -0.5, score2, vm, (pb0, pb1), ptb, [act_evacs(), t1], free=[all_used()])

    merged = place("merged", [P, TT, D], F32, offset=F0 + 8192)
    gat = place("gat", [P, TT, D], F32, offset=F0 + 16384)

    def sig_tm(dst, func):
        return lambda e, c, u, ch: e.activation(
            dst[:, :, bass.ds(c * 256, 256)], G[u][:, :].rearrange("p (t n) -> p t n", t=TT), func)
    gemm(4, cols(Win, first=C_G + D), tm_chunk(h_hi, h_lo), act_chunk=sig_tm(gat, ACT.Sigmoid), act_ready=[to], ready=[])
    t_gat = act_evacs()

    NS = 8
    o_all = place("o_all", [P, TT, 8, P], F32, offset=F0 + 16384)
    kf = place("kf", [P, 4, SEQ], F32, offset=F0 + 24576)
    qf = place("qf", [P, 4, SEQ], F32, offset=F0 + 28672)
    vf = place("vf", [P, 4, SEQ], F32, offset=F0 + 32768)
    otmp = place("otmp", [P, 2, 4, P], F32, offset=F0 + 32768)
    kt_ = place("kt_", [P, TT, 4, P], F32, offset=F0 + 36864)
    vt_ = place("vt_", [P, TT, 4, P], F32, offset=XN)
    bsc = place("bsc", [P, TT, NS, CH], F32, offset=XN + 4096)
    sq2 = place("sq2", [P, 8, SEQ], F32, offset=XN)
    bsc2 = place("bsc2", [P, TT, NS, CH], F32, offset=XN)
    Tm = place("Tm", [P, TT, NS, CH], F32, offset=A0)
    TT_ = place("TT_", [P, TT, NS, CH], F32, offset=A0 + 4096)
    LT = place("LT", [P, TT, NS, CH], F32, offset=A0 + 8192)
    IT = place("IT", [P, TT, NS, CH], F32, offset=A0 + 12288)
    Ym = place("Ym", [P, TT, NS, CH], F32, offset=A0 + 16384)
    AT = place("AT", [P, TT, NS, CH], F32, offset=A0 + 20576)
    DR = place("DR", [P, TT, NS, CH], F32, offset=A0 + 36864)
    pad = place("pad", [P, 2, 2, SEQ + 4], F32, offset=A0 + 16384)
    cy = place("cy", [P, 2, 2, SEQ], F32, offset=A0 + 24672)
    Sst = place("Sst", [P, NS, P], F32, offset=A0 + 24576)
    rr = place("rr", [P, 2, 4, P], F32, offset=A0 + 16384)
    vn = place("vn", [P, 2, 4, P], F32, offset=A0 + 20480)
    ks = place("ks", [P, TT, NS, P], F32, offset=A0 + 28672)
    vb = place("vb", [P, TT, NS, P], F32, offset=A0 + 36864)
    blk = place("blk", [P, P], F32, offset=KEEP + 1056)
    tri = place("tri", [P, 2, P], F32, offset=sbuf_at["rope1"])
    hal = place("hal", [P, 2, P], F32, offset=F0 + 40960)
    id64 = place("id64", [P, CH], F32, offset=KEEP + 800)
    msk = place("msk", [P, 3, 2, CH], F32, offset=sbuf_at["rope1"] + 1024)
    lev = place("lev", [P, 6, CH], F32, offset=sbuf_at["rope1"] + 2560)
    gb = place("gb", [P, 8, TT, 16], F32, offset=F0 + 41984)
    glb = place("glb", [P, 2, 32], F32, offset=KEEP + 544)

    t = pool.do(lambda e: e.memset(blk[:, :], 0.0), to)
    pool.do(lambda e: e.memset(tri[:, :, :], 0.0))
    pool.do(lambda e: e.memset(hal[:, :, :], 0.0))
    pool.do(lambda e: e.memset(id64[:, :], 0.0))
    pool.do(lambda e: e.memset(msk[:, :, :, :], 1.0))
    t = pool.do(lambda e: e.memset(lev[:, :, :], 1.0))
    for b in range(2):
        cs = slice(64 * b, 64 * b + 64)
        pool.do(lambda e, b=b, cs=cs: e.memset(blk[cs, cs], 1.0), t)
        pool.do(lambda e, b=b, cs=cs: e.memset(hal[cs, b, :], 1.0), t)
        t2 = pool.do(lambda e, b=b, cs=cs: e.memset(tri[cs, :, cs], 1.0), t)
        pool.do(lambda e, cs=cs: e.affine_select(out=id64[cs, :], in_=id64[cs, :], compare_op=ALU.not_equal,
                                                 fill=1.0, base=0, pattern=[[-1, CH]], channel_multiplier=1), t2)
        pool.do(lambda e, cs=cs: e.affine_select(out=tri[cs, 0, cs], in_=tri[cs, 0, cs], compare_op=ALU.is_ge,
                                                 fill=0.0, base=0, pattern=[[1, CH]], channel_multiplier=-1), t2)
        pool.do(lambda e, cs=cs: e.affine_select(out=tri[cs, 1, cs], in_=tri[cs, 1, cs], compare_op=ALU.is_ge,
                                                 fill=0.0, base=0, pattern=[[-1, CH]], channel_multiplier=1), t2)
        for m_, d_, sgn, op in ((0, 0, -1, ALU.is_gt), (0, 1, 1, ALU.is_gt), (1, 0, 1, ALU.is_ge),
                                (1, 1, -1, ALU.is_ge), (2, 0, 1, ALU.is_gt), (2, 1, -1, ALU.is_gt)):
            pool.do(lambda e, cs=cs, m_=m_, d_=d_, sgn=sgn, op=op: e.affine_select(
                out=msk[cs, m_, d_, :], in_=msk[cs, m_, d_, :], compare_op=op, fill=0.0, base=0,
                pattern=[[sgn, CH]], channel_multiplier=-sgn), t2)
        for l in range(6):
            sz = 2 ** (l + 1)
            v_ = lev[cs, l, :].rearrange("p (n s) -> p n s", s=sz)
            t3 = pool.do(lambda e, v_=v_, sz=sz: e.affine_select(
                out=v_, in_=v_, compare_op=ALU.is_ge, fill=0.0, base=0,
                pattern=[[-sz, CH // sz], [0, sz]], channel_multiplier=1), t2)
            t3 = pool.do(lambda e, v_=v_, sz=sz: e.affine_select(
                out=v_, in_=v_, compare_op=ALU.is_ge, fill=0.0, base=sz - 1,
                pattern=[[sz, CH // sz], [0, sz]], channel_multiplier=-1), t3)
    for l in range(5, -1, -1):
        lower = lev[:, l - 1, :] if l else id64[:, :]
        t3 = pool.do(lambda e, l=l, lower=lower: e.tensor_tensor(lev[:, l, :], lev[:, l, :], lower, ALU.subtract), t3)
    t3 = pool.do(lambda e: e.tensor_tensor(msk[:, 0, :, :], msk[:, 0, :, :], lev[:, 0:1, :].broadcast_to((P, 2, CH)), ALU.mult), t3)
    t_masks = t3

    beta, gg, gc, eg, be, ek, s1, s2 = (gb[:, j, :, :] for j in range(8))
    t = act.do(lambda e: e.activation(beta, ab[:, :, 0:16], ACT.Sigmoid), act_evacs(), t_lat)
    t_beta = t
    t = dve.do(lambda e: e.tensor_tensor(s1, ab[:, :, 16:32], dtb[:, 1:2, :].broadcast_to((P, TT, 16)), ALU.add), t_lat, (gfin_in, 48))
    t1 = dve.do(lambda e: e.tensor_scalar(s2, s1, -1.0, None, ALU.mult), t)
    t1 = dve.do(lambda e: e.tensor_tensor(s2, s2, s1, ALU.min), t1)
    t1 = act.do(lambda e: e.activation(s2, s2, ACT.Exp), t1)
    t2 = act.do(lambda e: e.activation(dtb[:, 0, :], dtb[:, 0, :], ACT.Exp), (gfin_in, 48))
    t1 = act.do(lambda e: e.activation(s2, s2, ACT.Ln, bias=1.0), t1)
    t1 = dve.do(lambda e: e.scalar_tensor_tensor(out=s1, in0=s1, scalar=0.0, in1=s2, op0=ALU.max, op1=ALU.add), t1, t)
    t1 = dve.do(lambda e: e.scalar_tensor_tensor(out=gg, in0=s1, scalar=-1.0, in1=dtb[:, 0:1, :].broadcast_to((P, TT, 16)),
                                                 op0=ALU.mult, op1=ALU.mult), t1, t2)
    for t_ in range(TT):
        for d_ in range(2):
            tp = pe.do(lambda e, t_=t_, d_=d_: e.matmul(X[0][:, t_ * 16 + d_ * 8:t_ * 16 + d_ * 8 + 8], tri[:, d_, :],
                                                        gg[:, t_, d_ * 8:d_ * 8 + 8], start=True, stop=True), t1, t_masks, xfree[0])
    ggf = gb[:, 1, :, :].rearrange("p t s -> p (t s)")
    pe.do(lambda e: e.matmul(X[0][:, 32:64], blk[:, :], ggf, start=True, stop=True))
    for b in range(2):
        tp = pe.do(lambda e, b=b: e.matmul(X[0][:, 64 + 32 * b:96 + 32 * b], hal[:, b, :], ggf, start=True, stop=True))
    v3 = lambda a_: a_.rearrange("p (t s) -> p t s", t=TT)
    t1 = dve.do(lambda e: e.tensor_copy(gc, v3(X[0][:, 0:32])), tp)
    t2 = dve.do(lambda e: e.tensor_tensor(s1, v3(X[0][:, 32:64]), gc, ALU.subtract), t1)
    t3 = act.do(lambda e: e.activation(glb[:, :, :], X[0][:, 64:128].rearrange("p (b s) -> p b s", b=2), ACT.Exp), tp, t2)
    xfree[0] = t3
    t1 = act.do(lambda e: e.activation(eg, gc, ACT.Exp), t1)
    t2 = act.do(lambda e: e.activation(ek, s1, ACT.Exp), t2)
    t_gates = dve.do(lambda e: e.tensor_tensor(be, beta, eg, ALU.mult), t1, t_beta, t2)

    def streams(v_, h0):
        return v_.rearrange("p t (d h) -> p t d h", d=2)[:, :, :, h0:h0 + 4]

    def gated(e, c, u, ch):
        cs = slice(c * 256, (c + 1) * 256)
        return e.tensor_tensor(merged[:, :, cs], G[u][:, :].rearrange("p (t n) -> p t n", t=TT),
                               gat[:, :, cs], ALU.mult)
    gemm(4, cols(A["w_o_mla_2"][0]), tm_chunk(a_hi, a_lo), dve_chunk=gated, ready=[to], dve_ready=[t_gat, to])
    t_mla = [all_used(), dve_evacs(), act_evacs()]

    o_done = None
    group_free = t_mla
    for grp in range(2):
        h0 = grp * 4
        def conv_source(c, slot, h0=h0):
            v = Win.rearrange("(k p) n -> p k n", p=P)
            c0 = (c // 2) * D + h0 * P + (c % 2) * 256
            return [(slot[:, :].rearrange("p (k n) -> p k n", k=KT), v[:, :, c0:c0 + 256])]
        fin = (qf, kf, vf)
        ea0, ev0 = st.evac_a, st.evac_v

        def silu_of(e, c, fin=fin, ev0=ev0):
            e.wait_ge(S["dve_evac"], ev0 + c + 1)
            return e.activation(fin[c // 2][:, (c % 2) * 2:(c % 2) * 2 + 2, :], cy[:, c % 2, :, :], ACT.Silu)

        def act_pad(e, c, u, ch, silu_of=silu_of, ev0=ev0):
            if c not in (0, 4, 5):
                silu_of(e, c - 1)
            e.wait_ge(S["dve_evac"], ev0 + max(0, c - 1))
            return e.activation(pad[:, c % 2, :, 2:2 + SEQ], G[u][:, :].rearrange("p (k t) -> p k t", k=2), ACT.Copy)

        def dve_conv(e, c, u, ch, h0=h0, ea0=ea0):
            e.wait_ge(S["act_evac"], ea0 + c + 1)
            for w in range(CONV2):
                for f in range(2):
                    k = (c // 2) * 8 + h0 + (c % 2) * 2 + f
                    y = cy[:, c % 2, f, :]
                    src = pad[:, c % 2, f, w:w + SEQ]
                    ins = (e.tensor_scalar(y, src, w5col(w, k), None, ALU.mult) if w == 0 else
                           e.scalar_tensor_tensor(out=y, in0=src, scalar=w5col(w, k), in1=y, op0=ALU.mult, op1=ALU.add))
                    if (w, f) != (CONV2 - 1, 1):
                        ch.link_but_one(ins, last=(w == CONV2 - 1))
            return ins
        tz = None
        for b in range(2):
            for o_ in (0, SEQ + 2):
                tz = dve.do(lambda e, b=b, o_=o_: e.memset(pad[:, b, :, o_:o_ + 2], 0.0), *group_free)
        def conv_chunks(n, first, *free, bank=0, conv_source=conv_source, act_pad=act_pad, dve_conv=dve_conv):
            products = fm_chunk(h_hi, h_lo)
            gemm(n, lambda c, slot: conv_source(first + c, slot),
                 lambda e, c, u, slot: products(e, c, u + bank, slot),
                 act_chunk=lambda e, c, u, ch: act_pad(e, first + c, u + bank, ch),
                 dve_chunk=lambda e, c, u, ch: dve_conv(e, first + c, u, ch), dve_links=9, banks_of="act",
                 ready=[*free], act_ready=[*free, tz], dve_ready=[tz])

        conv_chunks(4, 0, *group_free)
        t_qk = act.do(lambda e, silu_of=silu_of: silu_of(e, 3))
        squares, lengths = [], []
        for j in range(4):
            src = (qf, kf)[j // 2][:, (j % 2) * 2:(j % 2) * 2 + 2, :]
            ts_ = act.do(lambda e, j=j, src=src: e.activation(sq2[:, 2 * j:2 * j + 2, :], src, ACT.Square), t_qk, *group_free)
            squares.append(ts_)
        conv_chunks(1, 4)
        for j in range(4):
            src = (qf, kf)[j // 2][:, (j % 2) * 2:(j % 2) * 2 + 2, :]
            ts_ = squares[j]
            tp = pe.do(lambda e, j=j: e.matmul(X[j][:, :], ones[:, :], sq2[:, 2 * j:2 * j + 2, :].rearrange("p k t -> p (k t)"),
                                               start=True, stop=True), ts_, xfree[j])
            td = act.do(lambda e, j=j: e.activation(sq2[:, 2 * j:2 * j + 2, :].rearrange("p k t -> p (k t)"), X[j][:, :],
                                                    ACT.Ln, scale=(128.0 if j < 2 else 1.0),
                                                    bias=eps[:, 0:1] if j < 2 else eps[:, 1:2]), tp, t_eps)
            xfree[j] = td
            lengths.append(td)
        for j in range(4):
            src = (qf, kf)[j // 2][:, (j % 2) * 2:(j % 2) * 2 + 2, :]
            td = act.do(lambda e, j=j: e.activation(sq2[:, 2 * j:2 * j + 2, :], sq2[:, 2 * j:2 * j + 2, :], ACT.Exp, scale=-0.5), lengths[j])
            td = dve.do(lambda e, j=j, src=src: e.tensor_tensor(src, src, sq2[:, 2 * j:2 * j + 2, :], ALU.mult), td)
        t_unit = td
        diag = {}
        for n_, (g_, buf) in enumerate(((gc, bsc), (beta, bsc2))):
            for t_ in range(TT):
                gv = streams(g_, h0)[:, t_, :, :]
                for d_ in range(2):
                    diag[(n_, t_)] = dve.do(lambda e, t_=t_, d_=d_, gv=gv, buf=buf: e.tensor_tensor(
                        buf[:, t_, d_ * 4:d_ * 4 + 4, :], id64[:, :].rearrange("p (a j) -> p a j", a=1).broadcast_to((P, 4, CH)),
                        gv[:, d_, :].rearrange("p (h a) -> p h a", a=1).broadcast_to((P, 4, CH)), ALU.mult), t_unit, t_gates)
        R = {}
        for n_, buf in enumerate((bsc, bsc2)):
            for t_ in range(TT):
                b = 2 * n_ + t_
                R[(n_, t_)] = pe.do(lambda e, b=b, t_=t_, buf=buf: e.matmul(
                    X[b][:, :], blk[:, :], buf[:, t_, :, :].rearrange("p s j -> p (s j)"), start=True, stop=True),
                    diag[(n_, t_)], xfree[b])
        tg0 = [act_evacs()]
        for n_, other in enumerate((kf, qf)):
            for t_ in range(TT):
                for b in range(2):
                    for h in range(4):
                        cs = slice(t_ * P + 64 * b, t_ * P + 64 * b + 64)
                        o_ = t_ * 256 + h * 64
                        tqk = pe.do(lambda e, n_=n_, b=b, h=h, cs=cs, o_=o_, other=other: e.matmul(
                            G[n_][64 * b:64 * b + 64, o_:o_ + 64], kf[:, h, cs], other[:, h, cs], start=True, stop=True), t_unit, *tg0)
        def f4(buf, t_):
            return buf[:, t_, :, :]
        def g4(t_, n_):
            return G[n_][:, t_ * 256:(t_ + 1) * 256].rearrange("p (a h j) -> p a h j", a=1, h=4).broadcast_to((P, 2, 4, CH))
        def as4(v_):
            return v_.rearrange("p (d h) j -> p d h j", d=2)
        def mk(m_):
            return msk[:, m_, :, :].rearrange("p d (a j) -> p d a j", a=1).broadcast_to((P, 2, 4, CH))
        T_ready = {}
        for t_ in range(TT):
            gcv = streams(gc, h0)[:, t_, :, :]
            btv = streams(beta, h0)[:, t_, :, :]
            for d_ in range(2):
                x3 = X[t_][:, d_ * 256:(d_ + 1) * 256].rearrange("p (h j) -> p h j", h=4)
                ta = dve.do(lambda e, d_=d_, x3=x3, gcv=gcv, t_=t_: e.tensor_tensor(
                    DR[:, t_, d_ * 4:d_ * 4 + 4, :], x3, gcv[:, d_, :].rearrange("p (h a) -> p h a", a=1).broadcast_to((P, 4, CH)),
                    ALU.subtract), R[(0, t_)], *group_free)
            xfree[t_] = ta
            tb_ = dve.do(lambda e, t_=t_: e.tensor_scalar(f4(Tm, t_), f4(DR, t_), -1.0, 0.0, ALU.mult, ALU.min), ta, *group_free)
            tb_ = act.do(lambda e, t_=t_: e.activation(f4(Tm, t_), f4(Tm, t_), ACT.Exp), tb_)
            tc_ = dve.do(lambda e, t_=t_: e.tensor_scalar(f4(LT, t_), f4(DR, t_), 0.0, None, ALU.min), ta, *group_free)
            tc_ = act.do(lambda e, t_=t_: e.activation(f4(LT, t_), f4(LT, t_), ACT.Exp), tc_)
            tb_ = dve.do(lambda e, t_=t_: e.tensor_tensor(as4(f4(Tm, t_)), as4(f4(Tm, t_)), mk(0), ALU.mult), tb_, t_masks)
            tb_ = dve.do(lambda e, t_=t_: e.tensor_tensor(as4(f4(Tm, t_)), as4(f4(Tm, t_)), g4(t_, 0), ALU.mult), tb_, tqk)
            for d_ in range(2):
                td_ = dve.do(lambda e, t_=t_, d_=d_, btv=btv: e.tensor_tensor(
                    Tm[:, t_, d_ * 4:d_ * 4 + 4, :], Tm[:, t_, d_ * 4:d_ * 4 + 4, :],
                    btv[:, d_, :].rearrange("p (h a) -> p h a", a=1).broadcast_to((P, 4, CH)), ALU.mult), tb_)
            tc_ = dve.do(lambda e, t_=t_: e.tensor_tensor(as4(f4(LT, t_)), as4(f4(LT, t_)), mk(1), ALU.mult), tc_)
            te_ = dve.do(lambda e, t_=t_: e.tensor_tensor(as4(f4(IT, t_)), as4(f4(LT, t_)), g4(t_, 1), ALU.mult), tc_, *group_free)
            tc_ = dve.do(lambda e, t_=t_: e.tensor_tensor(as4(f4(LT, t_)), as4(f4(LT, t_)), mk(2), ALU.mult), te_)
            tc_ = dve.do(lambda e, t_=t_: e.tensor_tensor(as4(f4(LT, t_)), as4(f4(LT, t_)), g4(t_, 0), ALU.mult), tc_)
            tc_ = dve.do(lambda e, t_=t_: e.tensor_tensor(f4(LT, t_), f4(LT, t_), X[2 + t_][:, :].rearrange("p (s j) -> p s j", s=NS), ALU.mult), tc_, R[(1, t_)])
            xfree[2 + t_] = tc_
            lv = lev[:, 0:1, :].broadcast_to((P, NS, CH))
            idb = id64[:, :].rearrange("p (a j) -> p a j", a=1).broadcast_to((P, NS, CH))
            td_ = dve.do(lambda e, t_=t_, idb=idb: e.tensor_tensor(f4(Tm, t_), idb, f4(Tm, t_), ALU.subtract), td_)
            tf_ = dve.do(lambda e, t_=t_, lv=lv: e.tensor_tensor(f4(TT_, t_), f4(LT, t_), lv, ALU.mult), tc_, *group_free)
            tf_ = dve.do(lambda e, t_=t_, idb=idb: e.tensor_tensor(f4(TT_, t_), idb, f4(TT_, t_), ALU.subtract), tf_)
            T_ready[t_] = [td_, tf_]
        conv_chunks(1, 5, bank=2)
        t_c5 = dve_evacs()
        kv_free = {2: [act_evacs()], 3: tg0}

        def turn_heads(src, dst, *after):
            for t_ in range(TT):
                b = 2 + t_
                for h in range(4):
                    tp = pe.do(lambda e, b=b, h=h, t_=t_: e.transpose(
                        G[b][:, h * P:(h + 1) * P], src[:, h, t_ * P:(t_ + 1) * P], ident[:, :]), *after, *kv_free[b])
                tok = act.do(lambda e, b=b, t_=t_: e.activation(
                    dst[:, t_, :, :], G[b][:, :].rearrange("p (h d) -> p h d", h=4), ACT.Copy), tp, R[(1, 1)], *group_free)
                kv_free[b] = [tok]
            return tok

        def scaled(src, dst, g_, *after):
            for t_ in range(TT):
                for d_ in range(2):
                    gv = streams(g_, h0)[:, t_, d_, :].rearrange("p (h a) -> p h a", a=1).broadcast_to((P, 4, P))
                    tok = pool.do(lambda e, t_=t_, d_=d_, gv=gv: e.tensor_tensor(
                        dst[:, t_, d_ * 4:d_ * 4 + 4, :], src[:, t_, :, :], gv, ALU.mult), *after, t_gates)
            return tok
        t_masked = T_ready[0] + T_ready[1]
        def small_mm(out_bank, lhs, rhs, t_, *w):
            for b in range(2):
                cs = slice(64 * b, 64 * b + 64)
                for s_ in range(NS):
                    tok = pe.do(lambda e, cs=cs, s_=s_: e.matmul(out_bank[cs, s_ * 64:s_ * 64 + 64], lhs[cs, t_, s_, :],
                                                                 rhs[cs, t_, s_, :], start=True, stop=True), *w)
                    w = ()
            return tok

        def level_part(l, t_, *w):
            lv = lev[:, l:l + 1, :].broadcast_to((P, NS, CH))
            return pool.do(lambda e: e.tensor_tensor(f4(AT, t_), f4(LT, t_), lv, ALU.mult), *w)
        lvl = {t_: level_part(1, t_, *T_ready[t_]) for t_ in range(TT)}
        bank3 = lambda b: X[b][:, :].rearrange("p (s j) -> p s j", s=NS)
        ty = {}

        def y_part(l, t_):
            tp = small_mm(X[t_], AT, Tm, t_, lvl[t_], *T_ready[t_], xfree[t_])
            ty[t_] = act.do(lambda e: e.activation(f4(Ym, t_), bank3(t_), ACT.Copy), tp, *([t_c5] if t_ else []))
            xfree[t_] = ty[t_]
            if l < 5:
                lvl[t_] = level_part(l + 1, t_, tp)

        def t_part(l, t_):
            T_ready[t_] = []
            if l < 5:
                tp = small_mm(X[2 + t_], TT_, Ym, t_, ty[t_], xfree[2 + t_])
            tp2 = small_mm(X[t_], Ym, TT_, t_, ty[t_])
            if l < 5:
                xfree[2 + t_] = dve.do(lambda e: e.tensor_tensor(f4(Tm, t_), f4(Tm, t_), bank3(2 + t_), ALU.subtract), tp)
                T_ready[t_].append(xfree[2 + t_])
            xfree[t_] = dve.do(lambda e: e.tensor_tensor(f4(TT_, t_), f4(TT_, t_), bank3(t_), ALU.subtract), tp2)
            T_ready[t_].append(xfree[t_])
        y_part(1, 0)
        t_part(1, 0)
        for l in range(1, 6):
            y_part(l, 1)
            if l < 5:
                y_part(l + 1, 0)
            t_part(l, 1)
            if l < 5:
                t_part(l + 1, 0)
            if l == 1:
                act.do(lambda e, silu_of=silu_of: silu_of(e, 4))
                t_v = act.do(lambda e, silu_of=silu_of: silu_of(e, 5))
                t_k = turn_heads(kf, kt_, t_unit)
            if l == 2:
                t_tm = turn_heads(vf, vt_, t_v)
                scaled(kt_, ks, ek, t_k, t_v)
            if l == 3:
                t_ksvb = scaled(vt_, vb, beta, t_tm, *t_masked)
        t_T = xfree[1]
        t_s = {0: None, 1: None}
        gfree = t_T
        t_gfree, t_added = {}, {0: None, 1: None}
        for step in range(4):
            for d_ in range(2):
                c = step if d_ == 0 else 3 - step
                t_, b = c // 2, c % 2
                cs = slice(64 * b, 64 * b + 64)
                tok_ = slice(c * 64, c * 64 + 64)
                sl = slice(d_ * 4, d_ * 4 + 4)
                bc4 = lambda v_: v_.rearrange("p (h a) -> p h a", a=1).broadcast_to((64, 4, P))
                b4 = lambda v_, h0=h0, cs=cs, t_=t_, d_=d_: bc4(streams(v_, h0)[cs, t_, d_, :])
                w3 = lambda bk, cs=cs: bk[cs, :].rearrange("p (h d) -> p h d", h=4)
                rd, vd, od = rr[cs, d_, :, :], vn[cs, d_, :, :], otmp[cs, d_, :, :]
                if step:
                    for h in range(4):
                        tk = pe.do(lambda e, h=h, cs=cs, tok_=tok_, d_=d_: e.matmul(
                            X[d_][cs, h * P:(h + 1) * P], kf[:, h, tok_], Sst[:, d_ * 4 + h, :], start=True, stop=True), t_s[d_], xfree[d_])
                    for h in range(4):
                        tq = pe.do(lambda e, h=h, cs=cs, tok_=tok_, d_=d_: e.matmul(
                            G[2 + d_][cs, h * P:(h + 1) * P], qf[:, h, tok_], Sst[:, d_ * 4 + h, :], start=True, stop=True), t_gfree[d_])
                    t1 = dve.do(lambda e, rd=rd, w3=w3, d_=d_, b4=b4: e.tensor_tensor(rd, w3(X[d_]), b4(be), ALU.mult), tk, gfree)
                    xfree[d_] = t1
                    t1 = dve.do(lambda e, rd=rd, t_=t_, sl=sl, cs=cs: e.tensor_tensor(rd, vb[cs, t_, sl, :], rd, ALU.subtract), t1, t_ksvb)
                    tr_ = t1
                    get_r = lambda h, cs=cs, d_=d_: rr[cs, d_, h, :]
                else:
                    tr_ = t_ksvb
                    get_r = lambda h, cs=cs, d_=d_, t_=t_: vb[cs, t_, d_ * 4 + h, :]
                for h in range(4):
                    tv = pe.do(lambda e, h=h, cs=cs, d_=d_, t_=t_, get_r=get_r: e.matmul(
                        X[2 + d_][cs, h * P:(h + 1) * P], TT_[cs, t_, d_ * 4 + h, :], get_r(h), start=True, stop=True), tr_, xfree[2 + d_], gfree)
                tvn = act.do(lambda e, vd=vd, w3=w3, d_=d_: e.activation(vd, w3(X[2 + d_]), ACT.Copy), tv, gfree,
                             *([t_s[d_]] if step else []))
                xfree[2 + d_] = tvn
                for h in range(4):
                    if step < 3:
                        tst = pe.do(lambda e, h=h, cs=cs, d_=d_, t_=t_: e.matmul(
                            X[d_][:, h * P:(h + 1) * P], ks[cs, t_, d_ * 4 + h, :], vn[cs, d_, h, :], start=True, stop=True), tvn, xfree[d_], gfree)
                for h in range(4):
                    tin = pe.do(lambda e, h=h, cs=cs, d_=d_, t_=t_: e.matmul(
                        G[d_][cs, h * P:(h + 1) * P], IT[cs, t_, d_ * 4 + h, :], vn[cs, d_, h, :], start=True, stop=True), tvn, gfree)
                oo = o_all[cs, t_, h0:h0 + 4, :]
                if step < 3:
                    if step:
                        t2 = dve.do(lambda e, sl=sl, d_=d_, b=b, t_=t_, h0=h0: e.tensor_tensor(
                            Sst[:, sl, :], Sst[:, sl, :],
                            glb[:, b, :].rearrange("p (t d h) -> p t d h", t=TT, d=2)[:, t_, d_, h0:h0 + 4]
                            .rearrange("p (h a) -> p h a", a=1).broadcast_to((P, 4, P)), ALU.mult), tk, tq)
                        t2 = dve.do(lambda e, sl=sl, d_=d_: e.tensor_tensor(
                            Sst[:, sl, :], Sst[:, sl, :], X[d_][:, :].rearrange("p (h d) -> p h d", h=4), ALU.add), t2, tst)
                    else:
                        t2 = dve.do(lambda e, sl=sl, d_=d_: e.tensor_copy(
                            Sst[:, sl, :], X[d_][:, :].rearrange("p (h d) -> p h d", h=4)), tst, gfree)
                    t_s[d_] = t2
                    xfree[d_] = t2
                if step:
                    t3 = dve.do(lambda e, od=od, w3=w3, d_=d_, b4=b4: e.tensor_tensor(od, w3(G[2 + d_]), b4(eg), ALU.mult),
                                tq, t_tm, *([t_added[d_]] if t_added[d_] else []))
                dst = oo if step < 2 else od
                after = list(group_free) if step < 2 else []
                if step:
                    t3 = dve.do(lambda e, od=od, dst=dst, w3=w3, d_=d_: e.tensor_tensor(dst, od, w3(G[d_]), ALU.add), tin, t3, *after)
                else:
                    t3 = dve.do(lambda e, dst=dst, w3=w3, d_=d_: e.tensor_copy(dst, w3(G[d_])), tin, t_tm, *after)
                t_gfree[d_] = t3
                o_done = t3
                if step >= 2:
                    o_done = pool.do(lambda e, oo=oo, od=od: e.tensor_tensor(oo, oo, od, ALU.add), t3)
                    t_added[d_] = o_done
            gfree = t_gfree[1]
        group_free = [o_done, (S["pe_done"], pe.n), (S["dve_done"], dve.n), (S["act_done"], act.n)]
    t_o = group_free

    zs = place("zs", [P, TT, D], F32, offset=F0 + 24576)
    of = o_all[:, :, :, :].rearrange("p t h d -> p (t h) d")
    osq = place("osq", [P, 16, P], F32, offset=XN)
    rh = gb[:, 6, :, :].rearrange("p t s -> p (t s)")[:, 0:16]
    rh2 = gb[:, 7, :, :].rearrange("p t s -> p (t s)")[:, 0:16]
    t = act.do(lambda e: e.activation(osq[:, :, :], of, ACT.Square), *t_o)
    t = dve.do(lambda e: e.tensor_reduce(rh, osq[:, :, :], AX_X, ALU.add), t)
    t = dve.do(lambda e: e.tensor_scalar(rh, rh, 1.0 / P, EPS, ALU.mult, ALU.add), t)
    t = act.do(lambda e: e.activation(rh, rh, ACT.Sqrt), t)
    t = dve.do(lambda e: e.reciprocal(rh2, rh), t)
    t = dve.do(lambda e: e.tensor_tensor(of, of, rh2.rearrange("p (s a) -> p s a", a=1).broadcast_to((P, 16, P)), ALU.mult), t)
    ea_z = st.evac_a
    gemm(4, cols(Win, first=C_Z), tm_chunk(h_hi, h_lo), act_chunk=sig_tm(zs, ACT.Silu), ready=t_o, act_ready=t_o)
    ov = o_all[:, :, :, :].rearrange("p t h d -> p t (h d)")
    for c in range(4):
        cs = slice(c * 256, (c + 1) * 256)
        t = dve.do(lambda e, cs=cs: e.tensor_tensor(ov[:, :, cs], ov[:, :, cs], zs[:, :, cs], ALU.mult), t, (S["act_evac"], ea_z + c + 1))
    gemm(4, cols(Win, first=C_G), tm_chunk(h_hi, h_lo), act_chunk=sig_tm(zs, ACT.Sigmoid), act_ready=[t])
    t_gat = act_evacs()

    def to_features(src, ready, gain, free):
        tls = []
        for j in range(KT // 2):
            w = list(ready) + [xfree[j]]
            for kk in range(2):
                for t_ in range(TT):
                    k = 2 * j + kk
                    tp = pe.do(lambda e, j=j, kk=kk, k=k, t_=t_: e.transpose(
                        X[j][:, kk * SEQ + t_ * P:kk * SEQ + (t_ + 1) * P],
                        src[:, t_, k * P:(k + 1) * P], ident[:, :]), *w)
            x3 = X[j][:, :].rearrange("p (k t) -> p k t", k=2)
            dsl = slice(2 * j, 2 * j + 2)
            if gain is None:
                th = act.do(lambda e, x3=x3, dsl=dsl: e.activation(a_hi[:, dsl, :], x3, ACT.Copy), tp, *free)
                tl = dve.do(lambda e, x3=x3, dsl=dsl: e.tensor_tensor(a_lo[:, dsl, :], x3, a_hi[:, dsl, :].bitcast(F32), ALU.subtract), th, *free)
            else:
                th = act.do(lambda e, x3=x3, dsl=dsl: e.activation(a_hi[:, dsl, :], x3, ACT.Copy, scale=gain), tp, *free)
                tl = dve.do(lambda e, x3=x3, dsl=dsl: e.scalar_tensor_tensor(
                    out=a_lo[:, dsl, :], in0=x3, scalar=gain, in1=a_hi[:, dsl, :].bitcast(F32),
                    op0=ALU.mult, op1=ALU.subtract), th, *free)
            xfree[j] = tl
            tls += [tl, tl]
        tiles_of[tl] = tls
        return tl
    tf = to_features(ov, [t], col("dn_o_gain_2"), t_o)
    mt = place("mt", [P, 2, TT, 256], F32, offset=XN)
    ev_m = st.evac_v

    def merge(e, c, u, ch):
        e.wait_ge(S["dve_evac"], ev_m + c - 1)
        cs = slice(c * 256, (c + 1) * 256)
        ch.link(e.tensor_tensor(mt[:, c % 2, :, :], G[u][:, :].rearrange("p (t n) -> p t n", t=TT), zs[:, :, cs], ALU.mult))
        return e.tensor_tensor(merged[:, :, cs], merged[:, :, cs], mt[:, c % 2, :, :], ALU.add)
    gemm(4, cols(A["w_o_dn_2"][0]), tm_chunk(a_hi, a_lo), dve_chunk=merge, dve_links=1, ready=[tf], dve_ready=[t_gat, tf])
    tf = to_features(merged, [dve_evacs()], None, [all_used()])

    def residual(gate):
        ev0 = st.evac_v

        def chunk(e, c, u, ch):
            e.wait_ge(S["dve_evac"], ev0 + c - 1)
            cs = slice(c * 256, (c + 1) * 256)
            ch.link(e.tensor_tensor(mt[:, c % 2, :, :], G[u][:, :].rearrange("p (t n) -> p t n", t=TT),
                                    gt[:, gate:gate + 1, cs].broadcast_to((P, TT, 256)), ALU.mult))
            return e.tensor_tensor(x[:, :, cs], x[:, :, cs], mt[:, c % 2, :, :], ALU.add)
        return chunk
    gemm(4, cols(A["w_out_2"][0]), tm_chunk(a_hi, a_lo), dve_chunk=residual(0), dve_links=1, ready=[tf], dve_ready=[tf])
    t_x1 = dve_evacs()

    th = norm_to_features(x, [t_x1], lambda k: mcol[:, 3, k:k + 1], lambda k: mcol[:, 2, k:k + 1], [all_used()])
    E, C = N_EXP, CAP
    xeT = place("xeT", [P, KT, E * C], F32, offset=F0 + 8192)
    ye = place("ye", [P, E // 4, D], F32, offset=F0 + 24576)
    Sa = place("Sa", [P, TT, E * C], F32R, offset=A0)
    SG = place("SG", [P, TT, E * C], F32, offset=A0 + 4096)
    GT = place("GT", [P, E // 4, SEQ], F32, offset=A0 + 8192)
    gus = place("gus", [64, 2, D], F32, offset=A0 + 12288)
    tmpd = place("tmpd", [C, D], F32, offset=A0 + 20480)
    sgl = place("sgl", [P, KT * C], F32, offset=A0 + 24576)
    prd = place("prd", [P, KT, C], F32, offset=A0 + 25600)
    xes = [place(f"xes{j}", [P, KT, 2 * C], F32R, offset=A0 + 26624 + 2048 * j) for j in range(2)]
    hid = [place(f"hid{j}", [P, KT, 2 * C], F32R, offset=A0 + 30720 + 2048 * j) for j in range(2)]
    lg = place("lg", [E, SEQ], F32, offset=A0 + 34816)
    cur = place("cur", [E, 2, SEQ], F32, offset=A0 + 35840)
    mk_ = place("mk_", [E, SEQ], F32, offset=A0 + 37888)
    ps = place("ps", [E, SEQ], F32, offset=A0 + 38912)
    m8 = place("m8", [E, 8], F32, offset=A0 + 39936)
    aff = place("aff", [P, 2, TT, E], F32, offset=A0 + 40000)
    sm = place("sm", [P, 4, TT], F32, offset=A0 + 40384)
    iot = place("iot", [P, C], F32, offset=A0 + 40448)
    comb = place("comb", [64, C], F32, offset=A0 + 40576)
    cap_free = [all_used(), t_x1]
    t_i = pool.do(lambda e: e.iota(iot[:, :], pattern=[[1, C]], base=1, channel_multiplier=0,
                                   allow_small_or_imprecise_dtypes=True), *cap_free)
    t = pool.do(lambda e: e.memset(comb[:, :], 0.0), *cap_free)
    for base_ in (0, -32):
        t = pool.do(lambda e, b_=base_: e.affine_select(out=comb[:, :], in_=comb[:, :], compare_op=ALU.not_equal, fill=1.0,
                                                        base=b_, pattern=[[-1, C]], channel_multiplier=1), t)
    t_comb = t
    Wr = A["w_router_2"][0].rearrange("(k p) n -> p k n", p=P)

    def r_source(c, slot):
        return [(slot[:, 0:KT * E].rearrange("p (k n) -> p k n", k=KT), Wr)]

    def r_chunk(e, c, u, slot):
        for k in range(KT):
            wait_tile(e, k)
            w0, w1 = whi[slot][:, k * E:(k + 1) * E], wlo[slot][:, k * E:(k + 1) * E]
            e.matmul(G[u][0:E, 0:SEQ], w0, h_hi[:, k, :], start=(k == 0), stop=False)
            e.matmul(G[u][0:E, 0:SEQ], w0, h_lo[:, k, :], start=False, stop=False)
            ins = e.matmul(G[u][0:E, 0:SEQ], w1, h_hi[:, k, :], start=False, stop=(k == KT - 1))
        return ins
    gemm(1, r_source, r_chunk, ready=[th], act_ready=cap_free,
         act_chunk=lambda e, c, u, ch: e.activation(lg[:, :], G[u][0:E, 0:SEQ], ACT.Copy))
    x_hi, x_lo = (buf[:, :, :].rearrange("p k t -> p (k t)") for buf in (h_hi, h_lo))
    xn2 = xn[:, :, :].rearrange("p t d -> p (t d)")
    t_xhi = act.do(lambda e: e.activation(x_hi, xn2, ACT.Copy), all_used())
    t_xlo = pool.do(lambda e: e.tensor_tensor(x_lo, xn2, x_hi.bitcast(F32), ALU.subtract), t_xhi)
    for t_ in range(TT):
        tp = pe.do(lambda e, t_=t_: e.transpose(X[0][:, t_ * E:(t_ + 1) * E], lg[:, t_ * P:(t_ + 1) * P], ident[0:E, 0:E]), act_evacs(), xfree[0])
    l3 = X[0][:, 0:TT * E].rearrange("p (t n) -> p t n", t=TT)
    col3 = lambda v_: v_.rearrange("p (t a) -> p t a", a=1).broadcast_to((P, TT, E))
    a0, a1 = aff[:, 0, :, :], aff[:, 1, :, :]
    t = dve.do(lambda e: e.tensor_reduce(sm[:, 0, :], l3, AX_X, ALU.max), tp, *cap_free)
    t = dve.do(lambda e: e.tensor_tensor(a0, l3, col3(sm[:, 0, :]), ALU.subtract), t)
    xfree[0] = t
    t = act.do(lambda e: e.activation(a0, a0, ACT.Exp), t)
    t = dve.do(lambda e: e.tensor_reduce(sm[:, 1, :], a0, AX_X, ALU.add), t)
    t = dve.do(lambda e: e.reciprocal(sm[:, 2, :], sm[:, 1, :]), t)
    t_aff = dve.do(lambda e: e.tensor_tensor(a0, a0, col3(sm[:, 2, :]), ALU.mult), t)
    for t_ in range(TT):
        tp = pe.do(lambda e, t_=t_: e.transpose(X[1][0:E, t_ * P:(t_ + 1) * P], a0[:, t_, :], ident[:, :]), t_aff, xfree[1])
    t = dve.do(lambda e: e.tensor_copy(cur[:, 0, :], X[1][0:E, 0:SEQ]), tp, *cap_free)
    xfree[1] = t
    for r_ in range(C // 8):
        a_, b_ = r_ % 2, (r_ + 1) % 2
        t = dve.do(lambda e, a_=a_: e.max(m8[:, :], cur[:, a_, :]), t)
        t = dve.do(lambda e, a_=a_, b_=b_: e.match_replace(cur[:, b_, :], m8[:, :], cur[:, a_, :], -1.0), t)
    t = dve.do(lambda e: e.tensor_scalar(mk_[:, :], cur[:, 0, :], 0.0, None, ALU.is_lt), t)
    t1 = dve.do(lambda e: e.memset(lg[:, :], 0.0), act_evacs(), tp)
    t = dve.do(lambda e: e.tensor_tensor_scan(ps[:, :], mk_[:, :], lg[:, :], 0.0, ALU.add, ALU.add), t, t1)
    t = dve.do(lambda e: e.tensor_tensor(ps[:, :], ps[:, :], mk_[:, :], ALU.mult), t)
    for t_ in range(TT):
        tp = pe.do(lambda e, t_=t_: e.transpose(X[0][:, t_ * E:(t_ + 1) * E], ps[:, t_ * P:(t_ + 1) * P], ident[0:E, 0:E]), t, xfree[0])
    t = dve.do(lambda e: e.tensor_copy(a1, l3), tp)
    xfree[0] = t
    e4 = lambda buf, t_: buf[:, t_, :].rearrange("p (e c) -> p e c", e=E)
    for t_ in range(TT):
        ta = dve.do(lambda e, t_=t_: e.tensor_tensor(
            e4(Sa, t_), iot[:, :].rearrange("p (a c) -> p a c", a=1).broadcast_to((P, E, C)),
            a1[:, t_, :].rearrange("p (e a) -> p e a", a=1).broadcast_to((P, E, C)), ALU.is_equal), t, t_i, *cap_free)
        tb_ = dve.do(lambda e, t_=t_: e.tensor_tensor(
            e4(SG, t_), e4(Sa, t_).bitcast(F32), a0[:, t_, :].rearrange("p (e a) -> p e a", a=1).broadcast_to((P, E, C)), ALU.mult), ta)
    for k in range(KT):
        b = k % 4
        for n_, (part, t_) in enumerate((part, t_) for part in (x_hi, x_lo) for t_ in range(TT)):
            tp = pe.do(lambda e, b=b, k=k, t_=t_, part=part, n_=n_: e.matmul(
                X[b][:, :], part[:, t_ * D + k * P:t_ * D + (k + 1) * P], Sa[:, t_, :],
                start=(n_ == 0), stop=(n_ == 3)), ta, t_xlo, xfree[b])
        xfree[b] = act.do(lambda e, b=b, k=k: e.activation(xeT[:, k, :], X[b][:, :], ACT.Identity,
                                                           bias=mcol[:, 2, k:k + 1], scale=mcol[:, 3, k:k + 1]), tp, *cap_free)

    base = st.n
    done_before = [(S["pe_done"], pe.n), (S["act_done"], act.n), (S["dve_done"], dve.n), act_evacs(), dve_evacs(), t_comb]
    sx, sgu, scb, shd, sdn, sye = (nc.alloc_semaphore(n_) for n_ in
                                   ("xe_split", "gate_up_out", "combined", "hidden_split", "down_out", "ye_added"))
    s_gates = nc.alloc_semaphore("gates_turned")
    echain_a, echain_v = nc.alloc_semaphore("expert_act_chain"), nc.alloc_semaphore("expert_dve_chain")
    Wg = A["w_gate_2"][0].rearrange("e (k p) n -> p e k n", p=P)
    Wu = A["w_up_2"][0].rearrange("e (k p) n -> p e k n", p=P)
    Wd_ = A["w_down_2"][0].rearrange("e (k p) n -> p e k n", p=P)

    def experts(e, step, flush):
        step(0, 0, True)
        with e.Fori(0, 3) as i:
            for q in range(4):
                step(i * 4 + (q + 1), q + 1, False)
        for x_ in range(13, E):
            step(x_, x_, False)
        flush()

    def m_gu(x_):
        return base + (0 if isinstance(x_, int) and x_ == 0 else x_ * 12 - 4)

    def m_dn(x_):
        if isinstance(x_, int) and x_ == E - 1:
            return m_gu(E - 1) + 8 + 4
        return m_gu(x_ + 1) + 8

    def sp_experts(e):
        def load(W_, x_, m, j):
            slot = (base + j) % RING
            e.wait_ge(S["lo_ready"], m + j + 1)
            for dst, src in halves([(raw[slot][:, :].rearrange("p (k n) -> p k n", k=KT),
                                     W_[:, bass.ds(x_, 1), :, j * 256:(j + 1) * 256].rearrange("p a k n -> p (a k) n"))]):
                e.dma_start(dst, src).then_inc(raw_in[slot], 16)

        def step(x_, q, first):
            for j in range(4):
                load(Wg, x_, m_gu(x_), j)
            for j in range(4):
                load(Wu, x_, m_gu(x_) + 4, j)
            if not first:
                for j in range(4):
                    load(Wd_, x_ - 1, m_gu(x_) + 8, j)
        experts(e, step, lambda: [load(Wd_, E - 1, m_dn(E - 1), j) for j in range(4)])
    sp.raw(sp_experts)

    def pe_experts(e):
        for w in done_before:
            e.wait_ge(*w)

        def chunk(m, j, lhs, dst):
            slot = (base + j) % RING
            e.wait_ge(S["hi_ready"], m + j + 1)
            e.wait_ge(S["lo_ready"], RING + m + j + 1)
            for k in range(KT):
                e.matmul(dst, lhs[:, k, :], whi[slot][:, k * 256:(k + 1) * 256], start=(k == 0), stop=False)
                ins = e.matmul(dst, lhs[:, k, :], wlo[slot][:, k * 256:(k + 1) * 256], start=False, stop=(k == KT - 1))
            ins.then_inc(S["chunk_used"], 1)

        def down(x_, q, j):
            b, o_ = j // 2, (j % 2) * 256
            chunk(m_dn(x_), j, hid[q % 2], X[b][0:64, o_:o_ + 256])

        def step(x_, q, first):
            e.wait_ge(sx, x_ + 1)
            if not first:
                e.wait_ge(sgu, 2 * x_)
            for g_ in range(2):
                for j in range(4):
                    b, o_ = 2 * g_ + j // 2, (j % 2) * 256
                    chunk(m_gu(x_) + 4 * g_, j, xes[q % 2], G[b][0:64, o_:o_ + 256])
            if not first:
                if not isinstance(x_, int) and q == 1:
                    e.wait_ge(s_gates, 2)
                e.wait_ge(shd, x_)
                e.wait_ge(sye, x_)
                down(x_ - 1, q - 1, 0)
                down(x_ - 1, q - 1, 1)
            combine(x_, first)
            if not first:
                down(x_ - 1, q - 1, 2)
                down(x_ - 1, q - 1, 3)

        def turn_gates():
            for g_ in range(E // 4):
                for t_ in range(TT):
                    o_ = (g_ % 2) * SEQ + t_ * P
                    ins = e.transpose(X[g_ // 2][:, o_:o_ + P], SG[:, t_, g_ * P:(g_ + 1) * P], ident[:, :])
            ins.then_inc(s_gates, 1)

        def combine(x_, first):
            e.wait_ge(sgu, 2 * x_ + 2)
            e.wait_ge(shd, x_)
            if first:
                turn_gates()
            for g_ in range(2):
                for f in range(KT):
                    ins = e.matmul(X[2][:, g_ * 256 + f * C:g_ * 256 + (f + 1) * C], gus[:, g_, f * P:(f + 1) * P],
                                   comb[:, :], start=True, stop=True)
            ins.then_inc(scb, 1)

        def flush():
            e.wait_ge(shd, E)
            e.wait_ge(sye, E)
            for j in range(4):
                down(E - 1, E - 1, j)
        experts(e, step, flush)
    pe.raw(pe_experts)

    def act_experts(e):
        for w in done_before:
            e.wait_ge(*w)
        stop_at = base + 12 * E

        def sp_(m, j):
            if isinstance(m, int) and m + j + AHEAD >= stop_at:
                return
            hi_split(e, m + j + AHEAD, (base + j + AHEAD) % RING)

        def xe_hi(x_, q):
            e.activation(xes[q % 2][:, :, 0:C], xeT[:, :, bass.ds(x_ * C, C)], ACT.Copy).then_inc(echain_a, 1)

        def step(x_, q, first):
            if first:
                xe_hi(0, 0)
            for j in range(4):
                sp_(m_gu(x_), j)
            e.wait_ge(S["chunk_used"], RING + m_gu(x_) + 4)
            e.wait_ge(scb, x_)
            e.activation(gus[:, 0, 0:BANK], G[0][0:64, :], ACT.Copy)
            e.activation(gus[:, 0, BANK:D], G[1][0:64, :], ACT.Copy).then_inc(sgu, 1)
            for j in range(4):
                sp_(m_gu(x_) + 4, j)
            if first:
                e.wait_ge(s_gates, 1)
                for b in range(2):
                    ins = e.activation(GT[:, 2 * b:2 * b + 2, :], X[b][:, :].rearrange("p (g t) -> p g t", g=2), ACT.Copy)
                ins.then_inc(s_gates, 1)
                xe_next(x_, q)
                silu(x_)
            else:
                sp_(m_gu(x_) + 8, 0)
                sp_(m_gu(x_) + 8, 1)
                xe_next(x_, q)
                sp_(m_gu(x_) + 8, 2)
                silu(x_)
                sp_(m_gu(x_) + 8, 3)
                low(x_ - 1)

        def xe_next(x_, q):
            if isinstance(x_, int) and x_ == E - 1:
                return
            e.activation(xes[(q + 1) % 2][:, :, 0:C], xeT[:, :, bass.ds(x_ * C + C, C)], ACT.Copy).then_inc(echain_a, 1)

        def silu(x_):
            e.wait_ge(scb, x_ + 1)
            e.wait_ge(shd, x_)
            e.activation(sgl[:, :], X[2][:, 0:256], ACT.Silu).then_inc(echain_s, 1)

        def low(x_):
            e.wait_ge(S["chunk_used"], RING + m_dn(x_) + 4)
            e.wait_ge(sye, x_ + 1)
            e.activation(tmpd[:, 0:BANK], X[0][32:64, :], ACT.Copy)
            e.activation(tmpd[:, BANK:D], X[1][32:64, :], ACT.Copy).then_inc(sdn, 1)

        def flush():
            for j in range(4):
                sp_(m_dn(E - 1), j)
            low(E - 1)
        experts(e, step, flush)
    echain_s = nc.alloc_semaphore("silu_out")
    act.raw(act_experts)

    def dve_experts(e):
        for w in done_before:
            e.wait_ge(*w)
        stop_at = base + 12 * E

        def sp_(m, j):
            if isinstance(m, int) and m + j + AHEAD >= stop_at:
                return
            lo_split(e, m + j + AHEAD, (base + j + AHEAD) % RING)

        def xe_lo(x_, q):
            if isinstance(x_, int) and x_ == E:
                return
            e.wait_ge(echain_a, x_ + 1)
            e.tensor_tensor(xes[q % 2][:, :, C:2 * C], xeT[:, :, bass.ds(x_ * C, C)],
                            xes[q % 2][:, :, 0:C].bitcast(F32), ALU.subtract).then_inc(sx, 1)

        def step(x_, q, first):
            if first:
                xe_lo(0, 0)
            for g_ in range(2):
                for j in range(4):
                    sp_(m_gu(x_) + 4 * g_, j)
            e.wait_ge(S["chunk_used"], RING + m_gu(x_) + 8)
            e.wait_ge(scb, x_)
            e.tensor_copy(gus[:, 1, 0:BANK], G[2][0:64, :])
            e.tensor_copy(gus[:, 1, BANK:D], G[3][0:64, :]).then_inc(sgu, 1)
            if first:
                xe_lo(x_ + 1, q + 1)
                gate(x_, q)
            else:
                sp_(m_gu(x_) + 8, 0)
                sp_(m_gu(x_) + 8, 1)
                xe_lo(x_ + 1, q + 1)
                sp_(m_gu(x_) + 8, 2)
                gate(x_, q)
                sp_(m_gu(x_) + 8, 3)
                add(x_ - 1, q - 1)

        def gate(x_, q):
            e.wait_ge(echain_s, x_ + 1)
            ch = Chain(e, echain_v, x_ * 2)
            ch.link(e.tensor_tensor(prd[:, :, :], sgl[:, :].rearrange("p (f c) -> p f c", f=KT),
                                    X[2][:, 256:512].rearrange("p (f c) -> p f c", f=KT), ALU.mult))
            ch.link(e.tensor_copy(hid[q % 2][:, :, 0:C], prd[:, :, :]))
            e.tensor_tensor(hid[q % 2][:, :, C:2 * C], prd[:, :, :], hid[q % 2][:, :, 0:C].bitcast(F32),
                            ALU.subtract).then_inc(shd, 1)

        def add(x_, q):
            e.wait_ge(sdn, x_ + 1)
            qd = q % 4
            g_ = x_ // 4 if isinstance(x_, int) else (x_ - qd) // 4
            for b in range(2):
                ins = e.tensor_tensor(
                    ye[32 * qd:32 * qd + 32, bass.ds(g_, 1), b * BANK:(b + 1) * BANK].rearrange("p a n -> p (a n)"),
                    X[b][0:C, :], tmpd[:, b * BANK:(b + 1) * BANK], ALU.add)
            ins.then_inc(sye, 1)

        def flush():
            for j in range(4):
                sp_(m_dn(E - 1), j)
            add(E - 1, E - 1)
        experts(e, step, flush)
    dve.raw(lambda e: e.memset(small[:, 187:188], 0.0).then_inc(sye, 1))
    dve.raw(dve_experts)
    st.n += 12 * E

    for t_ in range(TT):
        for hf in range(2):
            for g_ in range(E // 4):
                tp = pe.do(lambda e, t_=t_, hf=hf, g_=g_: e.matmul(
                    G[2 * t_ + hf][:, :], GT[:, g_, t_ * P:(t_ + 1) * P], ye[:, g_, hf * BANK:(hf + 1) * BANK],
                    start=(g_ == 0), stop=(g_ == E // 4 - 1)), (sye, E + 1), (sgu, 2 * E), (s_gates, 2))
            cs = slice(hf * BANK, (hf + 1) * BANK)
            t = dve.do(lambda e, t_=t_, hf=hf, cs=cs: e.tensor_tensor(xn[:, t_, cs], G[2 * t_ + hf][:, :], gt[:, 1, cs], ALU.mult), tp)
            t = dve.do(lambda e, t_=t_, cs=cs: e.tensor_tensor(x[:, t_, cs], x[:, t_, cs], xn[:, t_, cs], ALU.add), t)
    gf2 = place("gf2b", [P, D], F32, offset=A0)
    g2_in = nc.alloc_semaphore("g_final_in")

    def load_g2(e):
        e.wait_ge(sye, E + 1)
        e.dma_start(gf2[:, :], A["g_final_2"].rearrange("(a d) -> a d", a=1).broadcast_to((P, D))).then_inc(g2_in, 16)
    act.raw(load_g2)
    rs, t = rstd_rows(x, [t], D)
    for t_ in range(TT):
        dve.do(lambda e, t_=t_, rs=rs: e.scalar_tensor_tensor(
            out=x[:, t_, :], in0=x[:, t_, :], scalar=rs[:, t_:t_ + 1], in1=gf2[:, :],
            op0=ALU.mult, op1=ALU.mult), t, (g2_in, 16))
    return finish()


def constants():
    inv = np.zeros((ROPE_2, 2), np.float32)
    f1 = np.float32(THETA_1) ** (-np.arange(0, ROT, 2, dtype=np.float32) / np.float32(ROT))
    f2 = np.float32(THETA_2) ** (-np.arange(ROPE_2 // 2, dtype=np.float32) / np.float32(ROPE_2 // 2))
    inv[:, 0] = np.tile(f1, 4)
    inv[:, 1] = np.tile(f2, 2)
    return {"inv_freq": inv}


def kernel(**inputs):
    import concourse.bacc as bacc
    from concourse.bass_utils import run_bass_kernel_spmd

    nc = bacc.Bacc("TRN2", target_bir_lowering=False, num_devices=1, dynamic_dma_scratch_size=1024)
    arrays, A = {}, {}
    for name, value in list(inputs.items()) + list(constants().items()):
        a = np.ascontiguousarray(value)
        arrays[f"in_{name}_dram"] = a
        A[name] = nc.dram_tensor(f"in_{name}_dram", a.shape, mybir.dt.from_np(a.dtype), kind="ExternalInput").ap()
    out = nc.dram_tensor("out_0_dram", [1, SEQ, D], F32, kind="ExternalOutput").ap()
    build(nc, A, out)
    r = run_bass_kernel_spmd(nc, [arrays], core_ids=[0])
    return r.results[0]["out_0_dram"]
```
